# Optimizing a Trainium2 kernel written in Bass

```python
import jax, jax.numpy as jnp
from jax import lax
import numpy as np

D_MODEL = 1024
BATCH = 1
SEQ = 512
DEPTH = 1

HGRN_HEADS = 4
HGRN_DK = 128
HGRN_DV = 128
HGRN_WIDTH = HGRN_HEADS * HGRN_DK
CHUNK = 64
CONV_WIDTH = 512
CONV_K = 3
N_EXPERTS = 32
TOP_K = 4
D_FF = 1024
SWIGLU_LIMIT = 7.0
SWIGLU_ALPHA = 1.702
MOE_BLOCK = 128
EPS = 1e-6
IN_SIZES = (HGRN_WIDTH, HGRN_WIDTH, HGRN_WIDTH, HGRN_WIDTH, CONV_WIDTH, CONV_WIDTH, CONV_WIDTH, D_MODEL, D_MODEL)
IN_COLS = 4 * HGRN_WIDTH + 3 * CONV_WIDTH + 2 * D_MODEL

kernel_name = "hgrn2_shortconv_gated_moe_adaln"

def rms_norm(x, w):
    xf = x.astype(jnp.float32)
    y = xf * lax.rsqrt(jnp.mean(xf * xf, axis=-1, keepdims=True) + EPS)
    return (y * w.astype(jnp.float32)).astype(x.dtype)

def split_points():
    return [int(v) for v in np.cumsum(IN_SIZES)[:-1]]

def hgrn2_lower_bound(lb_table, layer):
    p = jax.nn.softmax(lb_table.astype(jnp.float32), axis=0)
    return jnp.cumsum(p, axis=0)[layer]

def hgrn2_mixer(q, f_pre, v, g_out, lb, norm_w):
    dt = q.dtype
    bsz, s_len, _ = q.shape
    n_chunks = s_len // CHUNK
    log_f = jnp.logaddexp(jnp.log(lb), jnp.log1p(-lb) + jax.nn.log_sigmoid(f_pre.astype(jnp.float32)))
    k = -jnp.expm1(log_f)

    def to_chunks(t, d):
        return t.astype(jnp.float32).reshape(bsz, n_chunks, CHUNK, HGRN_HEADS, d).transpose(1, 0, 3, 2, 4)

    qc, kc, gc = to_chunks(q, HGRN_DK), to_chunks(k, HGRN_DK), to_chunks(log_f, HGRN_DK)
    vc = to_chunks(v, HGRN_DV)
    causal = jnp.tril(jnp.ones((CHUNK, CHUNK), dtype=bool))[None, None, :, :, None]

    def step(state, inp):
        q_c, k_c, v_c, g_c = inp
        b = jnp.cumsum(g_c, axis=2)
        o_inter = jnp.einsum('bhtk,bhkv->bhtv', q_c * jnp.exp(b), state)
        diff = b[:, :, :, None, :] - b[:, :, None, :, :]
        decay = jnp.exp(jnp.where(causal, diff, -jnp.inf))
        scores = jnp.einsum('bhtsk,bhsk->bhts', q_c[:, :, :, None, :] * decay, k_c)
        o = o_inter + jnp.einsum('bhts,bhsv->bhtv', scores, v_c)
        b_last = b[:, :, -1:, :]
        state = jnp.exp(b_last[:, :, 0, :])[..., None] * state + jnp.einsum('bhsk,bhsv->bhkv', k_c * jnp.exp(b_last - b), v_c)
        return state, o

    state0 = jnp.zeros((bsz, HGRN_HEADS, HGRN_DK, HGRN_DV), jnp.float32)
    _, o = lax.scan(step, state0, (qc, kc, vc, gc))
    o = o.transpose(1, 0, 3, 2, 4).reshape(bsz, s_len, HGRN_HEADS, HGRN_DV)
    o = o * lax.rsqrt(jnp.mean(o * o, axis=-1, keepdims=True) + EPS) * norm_w.astype(jnp.float32)
    g = g_out.astype(jnp.float32).reshape(bsz, s_len, HGRN_HEADS, HGRN_DV)
    o = o * jax.nn.silu(g)
    return o.reshape(bsz, s_len, HGRN_WIDTH).astype(dt)

def short_conv_mixer(b_gate, c_gate, h, conv_w):
    u = c_gate * h
    rhs = conv_w.astype(u.dtype)[:, None, :]
    y = lax.conv_general_dilated(u, rhs, window_strides=(1,), padding=((CONV_K - 1, 0),),
                                 dimension_numbers=('NWC', 'WIO', 'NWC'), feature_group_count=CONV_WIDTH)
    return b_gate * y

def moe_ffn(u, w_router, b_router, w1, b1, w2, b2):
    bsz, s_len, d = u.shape
    n_tok = bsz * s_len
    n_assign = n_tok * TOP_K
    n_blocks = n_assign // MOE_BLOCK + N_EXPERTS
    n_rows = n_blocks * MOE_BLOCK
    xt = u.reshape(n_tok, d)
    logits = (xt @ w_router + b_router).astype(jnp.float32)
    top_vals, top_idx = lax.top_k(logits, TOP_K)
    probs = jax.nn.softmax(top_vals, axis=-1)
    flat_e = top_idx.reshape(n_assign).astype(jnp.int32)
    order = jnp.argsort(flat_e)
    e_sorted = flat_e[order]
    tok_sorted = (order // TOP_K).astype(jnp.int32)
    w_sorted = probs.reshape(n_assign)[order]
    sizes = jnp.bincount(flat_e, length=N_EXPERTS).astype(jnp.int32)
    padded = (sizes + MOE_BLOCK - 1) // MOE_BLOCK * MOE_BLOCK
    start = jnp.cumsum(sizes) - sizes
    pad_end = jnp.cumsum(padded)
    pad_start = pad_end - padded
    dest = pad_start[e_sorted] + jnp.arange(n_assign, dtype=jnp.int32) - start[e_sorted]
    row_tok = jnp.full((n_rows,), n_tok, jnp.int32).at[dest].set(tok_sorted)
    row_w = jnp.zeros((n_rows,), jnp.float32).at[dest].set(w_sorted)
    block_start = jnp.arange(n_blocks, dtype=jnp.int32) * MOE_BLOCK
    block_e = jnp.minimum(jnp.searchsorted(pad_end, block_start, side='right'), N_EXPERTS - 1).astype(jnp.int32)
    x_pad = jnp.concatenate([xt, jnp.zeros((1, d), xt.dtype)], axis=0)

    def expert_block(args):
        toks, e = args
        hs = x_pad[toks]
        hid = hs @ w1[e] + b1[e]
        glu, lin = jnp.split(hid, 2, axis=-1)
        glu = jnp.minimum(glu, SWIGLU_LIMIT)
        lin = jnp.clip(lin, -SWIGLU_LIMIT, SWIGLU_LIMIT)
        act = glu * jax.nn.sigmoid(SWIGLU_ALPHA * glu) * (lin + 1.0)
        return act @ w2[e] + b2[e]

    out = lax.map(expert_block, (row_tok.reshape(n_blocks, MOE_BLOCK), block_e))
    out = out.reshape(n_rows, d) * row_w[:, None].astype(out.dtype)
    y = jnp.zeros((n_tok + 1, d), out.dtype).at[row_tok].add(out)[:n_tok]
    return y.reshape(bsz, s_len, d)

def setup_inputs(seed: int = 0) -> dict:
    key = jax.random.key(seed)
    ks = jax.random.split(key, 20)
    nrm = jax.random.normal
    f32 = jnp.float32
    D = D_MODEL
    return {
        "x": nrm(ks[0], (BATCH, SEQ, D), f32),
        "c": nrm(ks[1], (BATCH, D), f32),
        "w_ada": nrm(ks[2], (DEPTH, D, 6 * D), f32) * D ** -0.5,
        "b_ada": nrm(ks[3], (DEPTH, 6 * D), f32) * 0.02,
        "norm_mix_w": 1.0 + 0.02 * nrm(ks[4], (DEPTH, D), f32),
        "w_in": nrm(ks[5], (DEPTH, D, IN_COLS), f32) * D ** -0.5,
        "hgrn_lower_bounds": nrm(ks[6], (DEPTH + 1, HGRN_WIDTH), f32) * 0.5,
        "hgrn_norm_w": 1.0 + 0.02 * nrm(ks[7], (DEPTH, HGRN_DV), f32),
        "conv_w": nrm(ks[8], (DEPTH, CONV_K, CONV_WIDTH), f32) * CONV_K ** -0.5,
        "w_hgrn_out": nrm(ks[9], (DEPTH, HGRN_WIDTH, D), f32) * HGRN_WIDTH ** -0.5,
        "w_conv_out": nrm(ks[10], (DEPTH, CONV_WIDTH, D), f32) * CONV_WIDTH ** -0.5,
        "w_mix_out": nrm(ks[11], (DEPTH, D, D), f32) * D ** -0.5,
        "norm_ffn_w": 1.0 + 0.02 * nrm(ks[12], (DEPTH, D), f32),
        "w_router": nrm(ks[13], (DEPTH, D, N_EXPERTS), f32) * D ** -0.5,
        "b_router": nrm(ks[14], (DEPTH, N_EXPERTS), f32) * 0.01,
        "w1": nrm(ks[15], (DEPTH, N_EXPERTS, D, 2 * D_FF), f32) * D ** -0.5,
        "b1": nrm(ks[16], (DEPTH, N_EXPERTS, 2 * D_FF), f32) * 0.01,
        "w2": nrm(ks[17], (DEPTH, N_EXPERTS, D_FF, D), f32) * D_FF ** -0.5,
        "b2": nrm(ks[18], (DEPTH, N_EXPERTS, D), f32) * 0.01,
        "norm_final_w": 1.0 + 0.02 * nrm(ks[19], (D,), f32),
    }

def reference(x, c, w_ada, b_ada, norm_mix_w, w_in, hgrn_lower_bounds, hgrn_norm_w, conv_w,
              w_hgrn_out, w_conv_out, w_mix_out, norm_ffn_w, w_router, b_router, w1, b1, w2, b2,
              norm_final_w):
    bsz, s_len, d = x.shape
    silu_c = jax.nn.silu(c)
    cuts = split_points()
    h = x
    for layer in range(DEPTH):
        mod = (silu_c @ w_ada[layer] + b_ada[layer]).reshape(bsz, 6, 1, d)
        shift_m, scale_m, gate_m = mod[:, 0], mod[:, 1], mod[:, 2]
        shift_f, scale_f, gate_f = mod[:, 3], mod[:, 4], mod[:, 5]

        u = rms_norm(h, norm_mix_w[layer]) * (1.0 + scale_m) + shift_m
        proj = u @ w_in[layer]
        q, f_pre, i_v, g_o, cb, cc, ch, ga, gb = jnp.split(proj, cuts, axis=-1)
        lb = hgrn2_lower_bound(hgrn_lower_bounds, layer)
        y_a = hgrn2_mixer(q, f_pre, i_v, g_o, lb, hgrn_norm_w[layer]) @ w_hgrn_out[layer]
        y_b = short_conv_mixer(cb, cc, ch, conv_w[layer]) @ w_conv_out[layer]
        merged = jax.nn.sigmoid(ga) * y_a + jax.nn.sigmoid(gb) * y_b
        h = h + gate_m * (merged @ w_mix_out[layer])

        u = rms_norm(h, norm_ffn_w[layer]) * (1.0 + scale_f) + shift_f
        h = h + gate_f * moe_ffn(u, w_router[layer], b_router[layer], w1[layer], b1[layer], w2[layer], b2[layer])
    return rms_norm(h, norm_final_w)


_drawn_inputs = setup_inputs


def setup_inputs(seed=0):
    import zlib

    import numpy as np

    out = dict(_drawn_inputs(seed))
    spreads = {}
    factors = {'hgrn_norm_w': 9.199,
     'b_router': 11.733,
     'b1': 33.684,
     'b2': 27.061,
     'norm_final_w': 21.558,
     'norm_ffn_w': 4.592}
    for name, (base, spread) in spreads.items():
        noise = np.random.default_rng([zlib.crc32(name.encode()), seed]).standard_normal(out[name].shape)
        drawn = base * np.exp(spread * noise) if base else spread * noise
        out[name] = __import__('jax').numpy.asarray(drawn.astype(out[name].dtype))
    for name, factor in factors.items():
        out[name] = (out[name] * factor).astype(out[name].dtype)
    return out
```

```python
from contextlib import ExitStack

import numpy as np

import concourse.bass as bass
from concourse import mybir

F32 = mybir.dt.float32
F32R = mybir.dt.float32r
U32 = mybir.dt.uint32
I32 = mybir.dt.int32
U8 = mybir.dt.uint8
ALU = mybir.AluOpType
ACT = mybir.ActivationFunctionType
AX = mybir.AxisListType

P = 128
D = 1024
KD = D // P
TOKENS = 512
TT = TOKENS // P
HEADS = 4
HW = HEADS * P
LEVELS = 7
CONV_K = 3
E = 32
TOP = 4
FF = 1024
LIMIT = 7.0
ALPHA = 1.702
EPS = 1e-6
TINY = 1e-18
CH = 2048
SPLITS = 4
RAWS = 12
MAX_EXTRA = 16
MAX_BLOCKS = E + MAX_EXTRA
UNFILLED = 4096.0
KB = 1024

C_ID, C_ONE, C_TRI, C_IOTA, C_EYE2, C_TOK, C_PART, C_RESET = 0, 128, 256, 384, 512, 544, 576, 608
C_END = C_RESET + TOKENS


def shape_constants():
    c = np.zeros((P, C_END), np.float32)
    p = np.arange(P)
    c[:, C_ID:C_ID + P] = np.eye(P)
    c[:, C_ONE:C_ONE + P] = 1
    c[:, C_TRI:C_TRI + P] = p[:, None] < p[None, :]
    c[:, C_IOTA:C_IOTA + P] = p[None, :]
    c[:64, C_EYE2:C_EYE2 + E] = (p[:64, None] % E) == np.arange(E)[None, :]
    tok = np.arange(TT)[None, :, None] * P + p[:, None, None] + 0 * np.arange(TOP)[None, None, :]
    c[:, C_TOK:C_TOK + 16] = tok.reshape(P, 16) - UNFILLED
    c[:, C_TOK + 16:C_TOK + 32] = (tok * TOP + np.arange(TOP)).reshape(P, 16) - UNFILLED
    c[:, C_PART] = p
    c[:, C_PART + 1] = TOP * p
    c[:, C_RESET:C_RESET + TOKENS] = (np.arange(TOKENS) % P != 0)[None, :]
    return c


def level_masks():
    s, t = np.arange(P)[:, None], np.arange(P)[None, :]
    m = np.zeros((P, LEVELS, P), np.float32)
    for level in range(LEVELS):
        m[:, level] = ((s ^ t) >> level == 1) & (t > s)
    return m.reshape(P, LEVELS * P)


class Chain:

    def __init__(self, eng, sem):
        self.eng, self.sem, self.count = eng, sem, 0

    def __call__(self, ins):
        ins.then_inc(self.sem, 1)
        self.count += 1
        self.eng.wait_ge(self.sem, self.count)


def layer_kernel(nc, consts, masks, x, c, w_ada, b_ada, norm_mix_w, w_in, lower_bounds, hgrn_norm_w, conv_w,
                 w_hgrn_out, w_conv_out, w_mix_out, norm_ffn_w, w_router, b_router, w1, b1, w2, b2,
                 norm_final_w, out):
    x2 = x[0]
    out2 = out[0]
    u2_d = nc.dram_tensor("ffn_input", [TOKENS, D], F32, kind="Internal").ap()
    h2_d = nc.dram_tensor("residual", [TOKENS, D], F32, kind="Internal").ap()
    y_d = nc.dram_tensor("expert_rows", [TOKENS * TOP, D], F32, kind="Internal").ap()

    with ExitStack() as ctx:
        base = (nc.sbuf_base + 63) // 64 * 64

        def at(name, kb, shape, dt=F32):
            return nc.alloc_sbuf_tensor_at(name, shape, dt, offset=base + int(kb * KB))

        def sem(name):
            return ctx.enter_context(nc.semaphore(name))

        w_hi = at("w_hi", 0, [P, SPLITS, CH], F32R)
        w_lo = at("w_lo", 32, [P, SPLITS, CH], F32R)
        RAW = 64
        raw = at("raw", RAW, [P, RAWS, CH])
        stage = at("stage", RAW, [P, 2, CH])
        uT_hi = at("uT_hi", RAW + 16, [P, KD, TOKENS], F32R)
        uT_lo = at("uT_lo", RAW + 32, [P, KD, TOKENS], F32R)
        M = RAW + 48
        merged_hi = at("merged_hi", M, [P, KD, TOKENS], F32R)
        merged_lo = at("merged_lo", M + 16, [P, KD, TOKENS], F32R)
        ada0 = at("ada0", M, [P, CH])
        wdiff = at("wdiff", M, [P, 2, HEADS, P])
        q_dec = at("q_dec", M + 4, [P, 2, HEADS, P])
        k_dec = at("k_dec", M + 8, [P, 2, HEADS, P])
        scores = at("scores", M + 12, [P, HEADS, P])
        state = at("state", M + 14, [P, HEADS, P])
        k_tok = at("k_tok", M + 16, [P, HEADS, P])
        o_norm = at("o_norm", M + 18, [P, HEADS, P])
        gates = at("gates", M + 20, [P, TT, HW])
        mask_f = at("mask_f", M + 20, [P, LEVELS * P])
        g_sig = at("g_sig", M + 28, [P, HW])
        y_tmp = at("y_tmp", M + 30, [P, TOKENS])
        yc_hi = at("yc_hi", RAW + 80, [P, HEADS, TOKENS], F32R)
        yc_lo = at("yc_lo", RAW + 88, [P, HEADS, TOKENS], F32R)
        cu = at("cu", RAW + 88, [P, HEADS, TOKENS])
        N = RAW + 96
        const = at("const", N, [P, C_RESET])
        ident = const[:, C_ID:C_ID + P]
        ones = const[:, C_ONE:C_ONE + P]
        tri = const[:, C_TRI:C_TRI + P]
        iota = const[:, C_IOTA:C_IOTA + P]
        S0 = N + 2.375
        small = at("small", S0, [P, 352])
        vecT = small[:, 0:28]
        modT = small[:, 28:44]
        lb = small[:, 44:48]
        om_lb = small[:, 48:52]
        cs = small[:, 52:60]
        rstd = small[:, 60:64]
        ms = small[:, 64:68]
        hms = small[:, 68:72]
        hrs = small[:, 72:76]
        elast = small[:, 76:80]
        lbt = small[:, 80:96]
        csig = small[:, 96:104]
        eps = small[:, 104:105]
        R0 = N + 3.75
        qT = at("qT", R0, [P, HEADS, TOKENS])
        kT = at("kT", R0 + 8, [P, HEADS, TOKENS])
        bT = at("bT", R0 + 16, [P, HEADS, TOKENS])
        v_tok = at("v_tok", R0 + 24, [P, TT, HW])
        x_in = at("x_in", R0, [P, TT, D])
        x_n = at("x_n", R0 + 16, [P, TT, D])
        oT_hi = at("oT_hi", R0 + 32, [P, HEADS, TOKENS], F32R)
        oT_lo = at("oT_lo", R0 + 40, [P, HEADS, TOKENS], F32R)
        u_full = at("u_full", R0 + 32, [P, 2, TOKENS])
        vec_rows = at("vec_rows", R0 + 36, [28, P])
        reset = at("reset", R0 + 40, [P, TOKENS])
        mask_sb = at("mask_sb", R0 + 48, [P, LEVELS, P], U8)
        nw_row = at("nw_row", R0 + 49, [P, P])
        ada12 = at("ada12", R0, [P, 2, CH])
        sg_a = at("sg_a", R0 + 16, [P, 4, TOKENS])
        sg_b = at("sg_b", R0 + 24, [P, 4, TOKENS])
        rows = at("rows", R0 + 16, [P, 3, D])
        gate_f = at("gate_f", R0 + 28, [P, D])
        x_t = at("x_t", R0, [P, 2, D])
        h2 = at("h2", R0 + 8, [P, 2, D])
        u2 = at("u2", R0 + 32, [P, 2, D])
        u2T = at("u2T", R0 + 40, [P, D])
        tmp_j = at("tmp_j", R0 + 44, [P, D])
        wr = at("wr", R0 + 49.5, [P, KD, E])
        br = at("br", R0 + 50.5, [1, E])
        wf_row = at("wf_row", M - 48, [P, D])
        lg = at("lg", R0, [P, TT, E])
        val8 = at("val8", R0 + 0.5, [P, TT, 8])
        idx8 = at("idx8", R0 + 0.75, [P, TT, 8], U32)
        idxf = at("idxf", R0 + 1, [P, TT, 8])
        prob = at("prob", R0 + 1.25, [P, TT, TOP])
        psm = at("psm", R0 + 1.375, [P, TT])
        prc = at("prc", R0 + 1.4375, [P, TT])
        pos = at("pos", R0 + 1.5, [P, 16])
        blk = at("blk", R0 + 1.625, [P, 16])
        ge = at("ge", R0 + 1.75, [P, 3, 16])
        qcol = at("qcol", R0 + 1.9375, [P, 16])
        onehot = at("onehot", R0 + 2, [P, TT, TOP, E])
        chosen = at("chosen", R0 + 4, [P, TT, E])
        ohpos = at("ohpos", R0 + 4.5, [P, TT, TOP, E])
        slot_row = at("slot_row", R0 + 6.5, [P, 2, P])
        slot_col = at("slot_col", R0 + 7.5, [P, 2, 3, P])
        vv = at("vv", R0 + 10.5, [P, 3, 16])
        cnt = at("cnt", R0 + 10.75, [E, 8])
        mex = at("mex", R0 + 10.875, [E, 2, MAX_EXTRA])
        mtmp = at("mtmp", R0 + 11, [E, 2, MAX_EXTRA])
        btf = at("btf", R0 + 11.25, [1, 2 * MAX_BLOCKS + 16])
        b1_raw = at("b1_raw", R0 + 32, [P, 2 * FF])
        b2_raw = at("b2_raw", R0 + 40, [P, D])
        bias1 = at("bias1", R0 + 16, [P, 2 * FF], F32R)
        bias2 = at("bias2", R0 + 24, [P, D], F32R)
        tabI = at("tabI", R0 + 12, [P, 2, P], U32)
        tabW = at("tabW", R0 + 13, [P, P])
        bt = at("bt", R0 + 13.5, [1, 2 * MAX_BLOCKS + 16], I32)
        sel1 = at("sel1", R0 + 14, [P, P], F32R)
        sel2 = at("sel2", R0 + 14.5, [P, P], F32R)
        cur_tok = at("cur_tok", R0 + 15, [P, 1], U32)
        cur_row = at("cur_row", R0 + 15.0625, [P, 1], U32)
        cur_w = at("cur_w", R0 + 15.125, [P, 1])
        hs = at("hs", R0 + 48, [P, D])
        hsT_hi = at("hsT_hi", R0, [P, KD, P], F32R)
        hsT_lo = at("hsT_lo", R0 + 4, [P, KD, P], F32R)
        glu = at("glu", R0 + 8, [P, FF])
        sig = at("sig", R0 + 32, [P, FF])
        lin = at("lin", R0 + 36, [P, FF])
        aT_hi = at("aT_hi", R0 + 40, [P, KD, P], F32R)
        aT_lo = at("aT_lo", R0 + 44, [P, KD, P], F32R)
        y_out = at("y_out", R0 + 52, [P, D])
        y_in = at("y_in", RAW, [P, 2, TOP, D])
        h_in = at("h_in", RAW + 32, [P, 2, D])
        y_01 = at("y_01", RAW + 40, [P, 2, D])
        y_23 = at("y_23", RAW + 48, [P, 2, D])
        h_out = at("h_out", RAW + 56, [P, 2, D])
        wfin = at("wfin", RAW + 64, [P, D])
        sq = at("sq", RAW + 68, [P, D])

        ps = ctx.enter_context(nc.psum_tensor("ps", [P, 8, 512], F32))

        consts_in = sem("consts_in")
        vec_in = sem("vec_in")
        c_in = sem("c_in")
        x_inn = [sem(f"x_in{t}") for t in range(TT)]
        ada_bias_in = sem("ada_bias_in")
        ada0_zero = sem("ada0_zero")
        ada_in = [sem(f"ada_in{s}") for s in range(2)]
        ada0_used = sem("ada0_used")
        csig_ready = sem("csig_ready")
        vec_turned = sem("vec_turned")
        square_x = sem("square_x")
        sqrt_x = sem("sqrt_x")
        eps_set = sem("eps_set")
        xn_ready = sem("xn_ready")
        x_turned = sem("x_turned")
        mod_sum = sem("mod_sum")
        lb_exp_in = sem("lb_exp_in")
        lb_exp = sem("lb_exp")
        u_ready = sem("u_ready")
        u_hi_ready = sem("u_hi_ready")
        u_lo_ready = sem("u_lo_ready")
        dve1 = sem("dve1")
        act1 = sem("act1")
        masks_in = sem("masks_in")
        mask_f_in = sem("mask_f_in")
        mask_set = sem("mask_set")
        stage_in = [sem(f"stage_in{s}") for s in range(2)]

        def w_in_chunk(col, half):
            return w_in[0, half * 512:half * 512 + 512, col:col + 512].rearrange("(k p) n -> p k n", p=P)

        def out_chunk(w, row, col):
            return w[0, row:row + 512, col:col + 512].rearrange("(k p) n -> p k n", p=P)

        COL = {"q": 0, "f": 512, "v": 1024, "g": 1536, "cb": 2048, "cc": 2560, "ch": 3072,
               "ga0": 3584, "ga1": 4096, "gb0": 4608, "gb1": 5120}
        weight_chunks = []
        group_chunks = {}
        for name in ("f", "q", "v", "g", "cc", "ch", "cb", "ga0", "ya0", "gb0", "yb0", "ga1", "ya1", "gb1", "yb1",
                     "mix0", "mix1"):
            first = len(weight_chunks)
            if name in COL:
                weight_chunks += [w_in_chunk(COL[name], 0), w_in_chunk(COL[name], 1)]
            elif name[:2] == "ya":
                weight_chunks.append(out_chunk(w_hgrn_out, 0, 512 * int(name[2])))
            elif name[:2] == "yb":
                weight_chunks.append(out_chunk(w_conv_out, 0, 512 * int(name[2])))
            else:
                weight_chunks += [out_chunk(w_mix_out, 0, 512 * int(name[3])), out_chunk(w_mix_out, 512, 512 * int(name[3]))]
            group_chunks[name] = list(range(first, len(weight_chunks)))
        NW = len(weight_chunks)
        ADA_FROM = group_chunks["ga0"][1]
        stream = []
        n_ada = 0
        for n in range(NW):
            stream.append(("w", n))
            if n > ADA_FROM and n_ada < 16:
                for _ in range(1 if n < NW - 6 else 2):
                    if n_ada < 16:
                        stream.append(("ada", n_ada))
                        n_ada += 1
        while n_ada < 16:
            stream.append(("ada", n_ada))
            n_ada += 1
        where = {item: n for n, item in enumerate(stream)}

        ada_v = w_ada[0].rearrange("(p k) n -> p k n", k=KD)

        lo_done = sem("lo_done")
        ada_done = sem("ada_done")

        def stream_load(eng, n):
            if n >= 2:
                kind, m = stream[n - 2]
                eng.wait_ge(lo_done if kind == "w" else ada_done, m + 1)
            kind, m = stream[n]
            if kind == "w":
                dst = stage[:, n % 2, :].rearrange("p (k n) -> p k n", k=4)
                eng.dma_start(dst, weight_chunks[m]).then_inc(stage_in[n % 2], 16)
            else:
                eng.dma_start(stage[:, n % 2, :], ada_v[:, m % KD, CH * (1 + m // KD):CH * (2 + m // KD)]).then_inc(
                    stage_in[n % 2], 16)

        def wait_stage(eng, item):
            n = where[item]
            eng.wait_ge(stage_in[n % 2], 16 * (n // 2 + 1))

        with nc.Block() as block:
            @block.sync
            def _(sp):
                sp.dma_start(cs, c[0].rearrange("(p k) -> p k", k=KD)).then_inc(c_in, 16)
                for t in range(TT):
                    sp.dma_start(x_in[:, t, :], x2[t * P:(t + 1) * P, :]).then_inc(x_inn[t], 16)
                for k in range(KD):
                    if k >= 2:
                        sp.wait_ge(ada0_used, k - 1)
                    sp.dma_start(stage[:, k % 2, :], ada_v[:, k, 0:CH]).then_inc(ada_in[k % 2], 16)
                sp.wait_ge(ada0_used, KD)
                stream_load(sp, 0)
                stream_load(sp, 1)

            @block.gpsimd
            def _(pool):
                pool.memset(ada0[:], 0.0).then_inc(ada0_zero, 1)
                pool.memset(eps, EPS).then_inc(eps_set, 1)
                pool.wait_ge(mask_f_in, 16)
                pool.tensor_copy(mask_sb[:].rearrange("p l t -> p (l t)"), mask_f[:]).then_inc(mask_set, 1)

            @block.scalar
            def _(act):
                chain = Chain(act, act1)
                act.dma_start(const[:], consts[:, 0:C_RESET]).then_inc(consts_in, 16)
                act.dma_start(vec_rows[0:8, :], norm_mix_w[0].rearrange("(j p) -> j p", p=P)).then_inc(vec_in, 16)
                act.dma_start(vec_rows[8:16, :], lower_bounds.rearrange("r (h p) -> (r h) p", p=P)).then_inc(vec_in, 16)
                act.dma_start(vec_rows[16:28, :], conv_w[0].rearrange("r (h p) -> (r h) p", p=P)).then_inc(vec_in, 16)
                act.wait_ge(ada0_zero, 1)
                act.dma_start(ada0[0:1, :], b_ada[:, 0:CH]).then_inc(ada_bias_in, 16)
                act.dma_start(reset[:], consts[:, C_RESET:C_END]).then_inc(masks_in, 16)
                act.dma_start(nw_row[:], hgrn_norm_w[0:1, :].to_broadcast([P, P])).then_inc(masks_in, 16)
                act.dma_start(mask_f[:], masks).then_inc(mask_f_in, 16)
                act.wait_ge(c_in, 16)
                act.activation(csig, cs, ACT.Sigmoid).then_inc(csig_ready, 1)
                for t in range(TT):
                    act.wait_ge(x_inn[t], 16)
                    act.activation(x_n[:, t, :], x_in[:, t, :], ACT.Square, scale=D ** -0.5,
                                   accum_out=ms[:, t:t + 1]).then_inc(square_x, 1)
                act.wait_ge(square_x, TT)
                act.wait_ge(eps_set, 1)
                act.activation(rstd, ms, ACT.Sqrt, bias=eps).then_inc(sqrt_x, 1)
                act.wait_ge(lb_exp_in, 1)
                act.activation(lbt[:, 0:8], lbt[:, 0:8], ACT.Exp).then_inc(lb_exp, 1)
                for j in range(KD):
                    act.wait_ge(u_ready, j + 1)
                    act.activation(uT_hi[:, j, :], u_full[:, j % 2, :], ACT.Copy).then_inc(u_hi_ready, 1)

            @block.vector
            def _(dve):
                chain = Chain(dve, dve1)
                dve.wait_ge(csig_ready, 1)
                chain(dve.tensor_tensor(cs, cs, csig, ALU.mult))
                dve.wait_ge(sqrt_x, 1)
                chain(dve.reciprocal(rstd, rstd))
                for t in range(TT):
                    dve.tensor_scalar(x_n[:, t, :], x_in[:, t, :], rstd[:, t:t + 1], None, ALU.mult).then_inc(xn_ready, 1)
                dve.wait_ge(vec_turned, 1)
                chain(dve.tensor_copy(vecT, ps[:, 7, 0:28]))
                chain(dve.tensor_tensor(lbt[:, 8:12], vecT[:, 8:12], vecT[:, 12:16], ALU.max))
                chain(dve.tensor_tensor(lbt[:, 0:4], vecT[:, 8:12], lbt[:, 8:12], ALU.subtract))
                dve.tensor_tensor(lbt[:, 4:8], vecT[:, 12:16], lbt[:, 8:12], ALU.subtract).then_inc(lb_exp_in, 1)
                dve.wait_ge(lb_exp, 1)
                chain(dve.tensor_tensor(lbt[:, 8:12], lbt[:, 0:4], lbt[:, 4:8], ALU.add))
                chain(dve.reciprocal(lbt[:, 12:16], lbt[:, 8:12]))
                chain(dve.tensor_tensor(lb, lbt[:, 0:4], lbt[:, 12:16], ALU.mult))
                chain(dve.tensor_tensor(om_lb, lbt[:, 4:8], lbt[:, 12:16], ALU.mult))
                chain(dve.tensor_scalar(lb, lb, TINY, None, ALU.max))
                dve.wait_ge(ada_bias_in, 16)
                for k in range(KD):
                    dve.wait_ge(ada_in[k % 2], 16 * (k // 2 + 1))
                    dve.scalar_tensor_tensor(ada0[:], stage[:, k % 2, :], cs[:, k:k + 1], ada0[:], ALU.mult,
                                             ALU.add).then_inc(ada0_used, 1)
                    dve.wait_ge(ada0_used, k + 1)
                dve.wait_ge(mod_sum, 1)
                chain(dve.scalar_tensor_tensor(modT[:, 0:8], ps[:, 7, 40:48], 1.0, vecT[:, 0:8], ALU.add, ALU.mult))
                chain(dve.tensor_copy(modT[:, 8:16], ps[:, 7, 32:40]))
                for j in range(KD):
                    dve.wait_ge(x_turned, j + 1)
                    if j >= 2:
                        dve.wait_ge(u_hi_ready, j - 1)
                    dve.tensor_scalar(u_full[:, j % 2, :], ps[:, j % 6, :], modT[:, j:j + 1], modT[:, 8 + j:9 + j],
                                      ALU.mult, ALU.add).then_inc(u_ready, 1)
                    dve.wait_ge(u_hi_ready, j + 1)
                    dve.wait_ge(u_ready, j + 1)
                    dve.tensor_tensor(uT_lo[:, j, :], u_full[:, j % 2, :], uT_hi[:, j, :].bitcast(F32),
                                      ALU.subtract).then_inc(u_lo_ready, 1)
                    dve.wait_ge(u_lo_ready, j + 1)

            @block.tensor
            def _(pe):
                pe.wait_ge(consts_in, 16)
                pe.wait_ge(vec_in, 48)
                pe.transpose(ps[:, 7, 0:28], vec_rows[:], ident[0:28, 0:28]).then_inc(vec_turned, 1)
                pe.wait_ge(xn_ready, TT)
                for j in range(KD):
                    if j == 6:
                        pe.wait_ge(ada0_used, KD)
                        pe.wait_ge(dve1, 3)
                        for m in range(16):
                            mm = pe.matmul(ps[:, 7, 32 + m:33 + m], ada0[:, m * P:(m + 1) * P], ones[:, 0:1],
                                           start=True, stop=True)
                        mm.then_inc(mod_sum, 1)
                    if j >= 6:
                        pe.wait_ge(u_ready, j - 5)
                    for t in range(TT):
                        mm = pe.transpose(ps[:, j % 6, t * P:(t + 1) * P], x_n[:, t, j * P:(j + 1) * P], ident)
                    mm.then_inc(x_turned, 1)

        hi_done = sem("hi_done")
        unit_done = sem("unit_done")
        act_read = sem("act_read")
        dve_read = sem("dve_read")
        act2 = sem("act2")
        dve2 = sem("dve2")
        pool2 = sem("pool2")
        sig_f = sem("sig_f")
        k_ready = sem("k_ready")
        logf_ready = sem("logf_ready")
        b_ready = sem("b_ready")
        gsig_ready = sem("gsig_ready")
        g_ready = sem("g_ready")
        elast_ready = sem("elast_ready")
        w_ready = sem("w_ready")
        e_ready = sem("e_ready")
        qd_ready = sem("qd_ready")
        kd_ready = sem("kd_ready")
        dec_used = sem("dec_used")
        diag_done = sem("diag_done")
        sc_read = sem("sc_read")
        ktok_ready = sem("ktok_ready")
        state_sum = sem("state_sum")
        state_ready = sem("state_ready")
        o_sq = sem("o_sq")
        o_ms = sem("o_ms")
        o_rms = sem("o_rms")
        o_ready = sem("o_ready")
        o_read = sem("o_read")
        o_turned = sem("o_turned")
        oT_hi_ready = sem("oT_hi_ready")
        oT_lo_ready = sem("oT_lo_ready")
        dec_zero = sem("dec_zero")
        yc_ready = sem("yc_ready")
        merged_ready = sem("merged_ready")
        ada12_in = sem("ada12_in")
        ada12_zero = sem("ada12_zero")

        units = []
        for name, owner in (("f", "act"), ("q", "act"), ("v", "act"), ("g", "dve"), ("cc", "act"), ("ch", "dve"),
                            ("cb", "dve"), ("ga0", "act"), ("ya0", "dve"), ("gb0", "act"), ("yb0", "dve"),
                            ("ga1", "act"), ("ya1", "dve"), ("gb1", "act"), ("yb1", "dve")):
            units += [(name, m, owner) for m in range(4)]
        unit_no = {(name, m): n for n, (name, m, _) in enumerate(units)}

        def bank(name, m):
            return ps[:, unit_no[name, m] % 3, :]

        def reads_upto(n):
            owner = units[n][2]
            return owner, sum(o == owner for _, _, o in units[:n + 1])

        def refills(name):
            return [n + SPLITS for n in group_chunks[name] if n + SPLITS < NW]

        def group_end(n):
            return next(unit_no[name, 3] + 1 for name, chunks in group_chunks.items() if n in chunks)

        def split_view(buf, n):
            return buf[:, n % SPLITS, :].rearrange("p (k n) -> p k n", k=4)

        def exact3(pe, dst, pairs):
            n = len(pairs)
            for i, (sh, sl, mh, ml) in enumerate(pairs):
                pe.matmul(dst, sh, mh, start=(i == 0), stop=False)
                pe.matmul(dst, sh, ml, start=False, stop=False)
                mm = pe.matmul(dst, sl, mh, start=False, stop=(i == n - 1))
            return mm

        def half(ap, level, which):
            m = 1 << level
            v = ap.rearrange("p h (s two m) -> p h s two m", two=2, m=m)
            return v[:, :, :, which, :]

        def edge(ap, level):
            m = 1 << level
            v = ap.rearrange("p h (s two m) -> p h s two m", two=2, m=m)
            return v[:, :, :, 0, m - 1:m].to_broadcast([P, HEADS, P // (2 * m), m])

        with nc.Block() as block:
            @block.sync
            def _(sp):
                for n in range(2, len(stream)):
                    stream_load(sp, n)

            @block.gpsimd
            def _(pool):
                chain = Chain(pool, pool2)
                pool.memset(q_dec[:], 0.0).then_inc(dec_zero, 1)
                pool.memset(k_dec[:], 0.0).then_inc(dec_zero, 1)
                pool.wait_ge(k_ready, HEADS)
                pool.wait_ge(masks_in, 32)
                for t in range(TT):
                    for level in range(LEVELS + 1):
                        n = 9 * t + level
                        pool.wait_ge(e_ready, n + 1)
                        if n >= 2:
                            pool.wait_ge(dec_used, n - 1)
                        kk = kT[:, :, t * P:(t + 1) * P]
                        if n < 2:
                            pool.wait_ge(dec_zero, 2)
                        if level < LEVELS:
                            pool.tensor_tensor(half(k_dec[:, n % 2], level, 0), half(kk, level, 0),
                                               half(wdiff[:, n % 2], level, 0), ALU.mult).then_inc(kd_ready, 1)
                        else:
                            pool.tensor_tensor(k_dec[:, n % 2], kk, wdiff[:, n % 2], ALU.mult).then_inc(kd_ready, 1)
                    if t == 0:
                        for m in range(TT):
                            pool.wait_ge(dve_read, m + 1)
                            v = gates[:, m, :].rearrange("p (h d) -> p h d", h=HEADS)
                            pool.tensor_tensor(v, v, nw_row[:, None, :].to_broadcast([P, HEADS, P]),
                                               ALU.mult).then_inc(g_ready, 1)
                pool.wait_ge(oT_lo_ready, TT)
                pool.memset(ada12[:], 0.0).then_inc(ada12_zero, 1)
                pool.wait_ge(ada12_zero, 1)
                pool.dma_start(ada12[0:1, :, :].rearrange("p a n -> p (a n)"), b_ada[:, CH:3 * CH]).then_inc(ada12_in, 16)

            @block.scalar
            def _(act):
                chain = Chain(act, act2)

                def split_hi(n):
                    wait_stage(act, ("w", n))
                    if n >= SPLITS:
                        act.wait_ge(unit_done, group_end(n - SPLITS))
                    act.activation(w_hi[:, n % SPLITS, :], stage[:, where["w", n] % 2, :], ACT.Copy).then_inc(hi_done, 1)

                def unit(name, m):
                    act.wait_ge(unit_done, unit_no[name, m] + 1)

                def decay(n):
                    t, level = n // 9, n % 9
                    if level == 8:
                        act.wait_ge(kd_ready, 8 * t + 7)
                        act.wait_ge(qd_ready, 8 * t + 7)
                        act.activation(wdiff[:, n % 2], bT[:, :, t * P:(t + 1) * P], ACT.Exp).then_inc(e_ready, 1)
                    else:
                        act.wait_ge(w_ready, 8 * t + level + 1)
                        act.activation(wdiff[:, n % 2], wdiff[:, n % 2], ACT.Exp).then_inc(e_ready, 1)

                for n in range(SPLITS):
                    split_hi(n)
                for m in range(HEADS):
                    unit("f", m)
                    act.activation(bT[:, m, :], bank("f", m), ACT.Sigmoid).then_inc(sig_f, 1)
                    act.activation(kT[:, m, :], bank("f", m), ACT.Sigmoid, scale=-1.0).then_inc(act_read, 1)
                for n in refills("f"):
                    split_hi(n)
                for m in range(HEADS):
                    act.wait_ge(sig_f, m + 1)
                    act.activation(bT[:, m, :], bT[:, m, :], ACT.Ln, bias=lb[:, m:m + 1],
                                   scale=om_lb[:, m:m + 1]).then_inc(logf_ready, 1)
                for m in range(HEADS):
                    unit("q", m)
                    act.activation(qT[:, m, :], bank("q", m), ACT.Copy).then_inc(act_read, 1)
                for n in refills("q"):
                    split_hi(n)
                for m in range(TT):
                    unit("v", m)
                    act.activation(v_tok[:, m, :], bank("v", m), ACT.Copy).then_inc(act_read, 1)
                for n in refills("v"):
                    split_hi(n)
                act.wait_ge(b_ready, HEADS)
                for t, name in enumerate(("g", "cc", "ch", "cb")):
                    def filler(m):
                        if name == "g":
                            unit("g", m)
                            if m >= 1:
                                act.wait_ge(dve_read, m)
                            act.activation(g_sig[:], bank("g", m), ACT.Sigmoid).then_inc(gsig_ready, 1)
                        if name == "cc":
                            unit("cc", m)
                            act.activation(cu[:, m, :], bank("cc", m), ACT.Copy).then_inc(act_read, 1)
                    if t >= 1:
                        act.wait_ge(state_ready, t)
                    act.activation(elast, bT[:, :, t * P + P - 1:t * P + P].rearrange("p h o -> p (h o)"),
                                   ACT.Exp).then_inc(elast_ready, 1)
                    for n in (0, 1, 2):
                        decay(9 * t + n)
                    filler(0)
                    for n in (3, 4, 5):
                        decay(9 * t + n)
                    filler(1)
                    for n in (6, 7, 8):
                        decay(9 * t + n)
                    filler(2)
                    act.wait_ge(dec_used, 9 * t + 8)
                    if t >= 1:
                        act.wait_ge(state_sum, t)
                    act.activation(k_tok[:].rearrange("p h d -> p (h d)"), ps[:, 5, :], ACT.Copy).then_inc(ktok_ready, 1)
                    filler(3)
                    act.wait_ge(dec_used, 9 * t + 9)
                    if t >= 1:
                        act.wait_ge(o_turned, t)
                    act.activation(o_norm[:].rearrange("p h d -> p (h d)"), ps[:, 6, :], ACT.Square,
                                   scale=P ** -0.5).then_inc(o_sq, 1)
                    act.wait_ge(o_ms, t + 1)
                    act.activation(hrs, hms, ACT.Sqrt, bias=eps).then_inc(o_rms, 1)
                    act.wait_ge(o_turned, t + 1)
                    act.activation(oT_hi[:, :, t * P:(t + 1) * P], ps[:, 5, :].rearrange("p (h t) -> p h t", h=HEADS),
                                   ACT.Copy).then_inc(oT_hi_ready, 1)
                    for n in refills(name):
                        split_hi(n)
                for h in range(2):
                    for m in range(4):
                        unit(f"ga{h}", m)
                        if h == 1:
                            act.wait_ge(merged_ready, m + 1)
                        if h == 0 and m == 0:
                            act.wait_ge(oT_lo_ready, TT)
                        act.activation(sg_a[:, m, :], bank(f"ga{h}", m), ACT.Sigmoid).then_inc(act_read, 1)
                    for n in refills(f"ga{h}"):
                        split_hi(n)
                    for n in refills(f"ya{h}"):
                        split_hi(n)
                    for m in range(4):
                        unit(f"gb{h}", m)
                        if h == 1:
                            act.wait_ge(merged_ready, m + 1)
                        act.activation(sg_b[:, m, :], bank(f"gb{h}", m), ACT.Sigmoid).then_inc(act_read, 1)
                    for n in refills(f"gb{h}"):
                        split_hi(n)
                    for n in refills(f"yb{h}"):
                        split_hi(n)

            @block.vector
            def _(dve):
                chain = Chain(dve, dve2)

                ahead = [0]

                def add_ada(m):
                    dve.wait_ge(ada12_in, 16)
                    wait_stage(dve, ("ada", m))
                    dve.scalar_tensor_tensor(ada12[:, m // KD, :], stage[:, where["ada", m] % 2, :],
                                             cs[:, m % KD:m % KD + 1], ada12[:, m // KD, :], ALU.mult,
                                             ALU.add).then_inc(ada_done, 1)
                    dve.wait_ge(ada_done, m + 1)

                def split_lo(n):
                    while stream[ahead[0]] != ("w", n):
                        if stream[ahead[0]][0] == "ada":
                            add_ada(stream[ahead[0]][1])
                        ahead[0] += 1
                    dve.wait_ge(hi_done, n + 1)
                    dve.tensor_tensor(w_lo[:, n % SPLITS, :], stage[:, where["w", n] % 2, :],
                                      w_hi[:, n % SPLITS, :].bitcast(F32), ALU.subtract).then_inc(lo_done, 1)

                def unit(name, m):
                    dve.wait_ge(unit_done, unit_no[name, m] + 1)

                for n in range(SPLITS):
                    split_lo(n)
                dve.wait_ge(masks_in, 32)
                dve.wait_ge(mask_set, 1)
                for m in range(HEADS):
                    dve.wait_ge(act_read, m + 1)
                    dve.tensor_scalar(kT[:, m, :], kT[:, m, :], om_lb[:, m:m + 1], None, ALU.mult).then_inc(k_ready, 1)
                for n in refills("f"):
                    split_lo(n)
                for m in range(HEADS):
                    dve.wait_ge(logf_ready, m + 1)
                    dve.tensor_tensor_scan(bT[:, m, :], reset[:], bT[:, m, :], 0.0, ALU.mult, ALU.add).then_inc(b_ready, 1)
                for n in refills("q"):
                    split_lo(n)
                for n in refills("v"):
                    split_lo(n)
                dve.wait_ge(b_ready, HEADS)
                dve.wait_ge(act_read, 3 * HEADS)
                dve.wait_ge(dec_zero, 2)

                def diff(t, level):
                    n = 9 * t + level
                    if n >= 2:
                        p = 9 * t + level - 2
                        dve.wait_ge(qd_ready, sum(x % 9 != 7 for x in range(p + 1)))
                        dve.wait_ge(kd_ready, sum(x % 9 != 8 for x in range(p + 1)))
                    b = bT[:, :, t * P:(t + 1) * P]
                    w = wdiff[:, n % 2]
                    if level < LEVELS:
                        chain(dve.tensor_tensor(half(w, level, 1), half(b, level, 1), edge(b, level), ALU.subtract))
                        dve.tensor_tensor(half(w, level, 0), edge(b, level), half(b, level, 0),
                                          ALU.subtract).then_inc(w_ready, 1)
                    else:
                        dve.tensor_tensor(w, b[:, :, P - 1:P].to_broadcast([P, HEADS, P]), b,
                                          ALU.subtract).then_inc(w_ready, 1)

                def q_decay(t, level):
                    n = 9 * t + level
                    dve.wait_ge(e_ready, n + 1)
                    if n >= 2:
                        dve.wait_ge(dec_used, n - 1)
                    qq = qT[:, :, t * P:(t + 1) * P]
                    if level < LEVELS:
                        dve.tensor_tensor(half(q_dec[:, n % 2], level, 1), half(qq, level, 1),
                                          half(wdiff[:, n % 2], level, 1), ALU.mult).then_inc(qd_ready, 1)
                    else:
                        dve.tensor_tensor(q_dec[:, n % 2], qq, wdiff[:, n % 2], ALU.mult).then_inc(qd_ready, 1)

                def take_scores(t, level):
                    dve.wait_ge(dec_used, 9 * t + level + 1)
                    dve.wait_ge(sc_read, 8 * t + level + 1)
                    b = 3 + (8 * t + level + 1) % 2
                    dve.copy_predicated(scores[:], mask_sb[:, level, None, :].to_broadcast([P, HEADS, P]),
                                        ps[:, b, :].rearrange("p (h t) -> p h t", h=HEADS)).then_inc(sc_read, 1)

                for t, name in enumerate(("g", "cc", "ch", "cb")):
                    def filler(m):
                        if name == "g":
                            unit("g", m)
                            dve.wait_ge(gsig_ready, m + 1)
                            dve.tensor_tensor(gates[:, m, :], bank("g", m), g_sig[:], ALU.mult).then_inc(dve_read, 1)
                        if name == "ch":
                            unit("ch", m)
                            dve.tensor_tensor(cu[:, m, :], bank("ch", m), cu[:, m, :], ALU.mult).then_inc(dve_read, 1)
                        if name == "cb":
                            tap = lambda k: vecT[:, 16 + 4 * k + m:17 + 4 * k + m]
                            dve.wait_ge(dve_read, 8 + m)
                            chain(dve.tensor_scalar(y_tmp[:], cu[:, m, :], tap(2), None, ALU.mult))
                            chain(dve.scalar_tensor_tensor(y_tmp[:, 1:], cu[:, m, 0:TOKENS - 1], tap(1), y_tmp[:, 1:],
                                                           ALU.mult, ALU.add))
                            chain(dve.scalar_tensor_tensor(y_tmp[:, 2:], cu[:, m, 0:TOKENS - 2], tap(0), y_tmp[:, 2:],
                                                           ALU.mult, ALU.add))
                            unit("cb", m)
                            dve.tensor_tensor(y_tmp[:], y_tmp[:], bank("cb", m), ALU.mult).then_inc(dve_read, 1)
                            dve.wait_ge(dve_read, 9 + m)
                            chain(dve.tensor_copy(yc_hi[:, m, :], y_tmp[:]))
                            dve.tensor_tensor(yc_lo[:, m, :], y_tmp[:], yc_hi[:, m, :].bitcast(F32),
                                              ALU.subtract).then_inc(yc_ready, 1)
                            dve.wait_ge(yc_ready, m + 1)
                    diff(t, 0)
                    diff(t, 1)
                    dve.wait_ge(diag_done, t + 1)
                    if t >= 1:
                        dve.wait_ge(dec_used, 9 * t)
                    dve.tensor_tensor(scores[:], ps[:, 3 + (8 * t) % 2, :].rearrange("p (h t) -> p h t", h=HEADS),
                                      ident[:, None, :].to_broadcast([P, HEADS, P]), ALU.mult).then_inc(sc_read, 1)
                    q_decay(t, 0)
                    for level in range(2, 8):
                        diff(t, level)
                        q_decay(t, level - 1)
                        take_scores(t, level - 2)
                        if level in (3, 5, 7):
                            filler(level // 2 - 1)
                    q_decay(t, 8)
                    take_scores(t, 6)
                    if t < TT - 1:
                        dve.wait_ge(state_sum, t + 1)
                        dve.wait_ge(elast_ready, t + 1)
                        for h in range(HEADS):
                            src = ps[:, 7, h * P:(h + 1) * P]
                            if t == 0:
                                ins = dve.tensor_copy(state[:, h, :], src)
                            else:
                                ins = dve.scalar_tensor_tensor(state[:, h, :], state[:, h, :], elast[:, h:h + 1], src,
                                                               ALU.mult, ALU.add)
                        ins.then_inc(state_ready, 1)
                    filler(3)
                    dve.wait_ge(o_sq, t + 1)
                    dve.tensor_reduce(hms, o_norm[:], AX.X, ALU.add).then_inc(o_ms, 1)
                    dve.wait_ge(o_rms, t + 1)
                    chain(dve.reciprocal(hrs, hrs))
                    if t == 0:
                        dve.wait_ge(g_ready, TT)
                    dve.tensor_tensor(o_norm[:].rearrange("p h d -> p (h d)"), ps[:, 6, :], gates[:, t, :],
                                      ALU.mult).then_inc(o_read, 1)
                    dve.wait_ge(o_read, t + 1)
                    dve.tensor_tensor(o_norm[:], o_norm[:], hrs[:, :, None].to_broadcast([P, HEADS, P]),
                                      ALU.mult).then_inc(o_ready, 1)
                    dve.wait_ge(oT_hi_ready, t + 1)
                    dve.tensor_tensor(oT_lo[:, :, t * P:(t + 1) * P], ps[:, 5, :].rearrange("p (h t) -> p h t", h=HEADS),
                                      oT_hi[:, :, t * P:(t + 1) * P].bitcast(F32), ALU.subtract).then_inc(oT_lo_ready, 1)
                    for n in refills(name):
                        split_lo(n)
                for h in range(2):
                    for m in range(4):
                        unit(f"ya{h}", m)
                        dve.tensor_tensor(sg_a[:, m, :], bank(f"ya{h}", m), sg_a[:, m, :], ALU.mult).then_inc(dve_read, 1)
                        if m == 0:
                            for n in refills(f"ga{h}"):
                                split_lo(n)
                    for n in refills(f"ya{h}"):
                        split_lo(n)
                    for m in range(4):
                        if m == 1:
                            for n in refills(f"gb{h}"):
                                split_lo(n)
                        unit(f"yb{h}", m)
                        j = 4 * h + m
                        reads = reads_upto(unit_no[f"yb{h}", m])[1]
                        dve.tensor_tensor(sg_b[:, m, :], bank(f"yb{h}", m), sg_b[:, m, :], ALU.mult).then_inc(dve_read, 1)
                        dve.wait_ge(dve_read, reads)
                        chain(dve.tensor_tensor(sg_b[:, m, :], sg_b[:, m, :], sg_a[:, m, :], ALU.add))
                        chain(dve.tensor_copy(merged_hi[:, j, :], sg_b[:, m, :]))
                        dve.tensor_tensor(merged_lo[:, j, :], sg_b[:, m, :], merged_hi[:, j, :].bitcast(F32),
                                          ALU.subtract).then_inc(merged_ready, 1)
                    for n in refills(f"yb{h}"):
                        split_lo(n)

            @block.tensor
            def _(pe):
                def begin(name, m):
                    n = unit_no[name, m]
                    if n >= 3:
                        owner, reads = reads_upto(n - 3)
                        pe.wait_ge(act_read if owner == "act" else dve_read, reads)

                def part(name, m, ks):
                    chunks = group_chunks[name]
                    n = unit_no[name, m]
                    dst = bank(name, m)
                    for k in ks:
                        if m == 0:
                            pe.wait_ge(lo_done, chunks[k // 4] + 1)
                        wh = split_view(w_hi, chunks[k // 4])[:, k % 4, :]
                        wl = split_view(w_lo, chunks[k // 4])[:, k % 4, :]
                        first, last = k == 0, k == KD - 1
                        if name in ("v", "g"):
                            sh, sl = uT_hi[:, k, m * P:(m + 1) * P], uT_lo[:, k, m * P:(m + 1) * P]
                            mh, ml = wh, wl
                        else:
                            sh, sl = wh[:, m * P:(m + 1) * P], wl[:, m * P:(m + 1) * P]
                            mh, ml = uT_hi[:, k, :], uT_lo[:, k, :]
                        pe.matmul(dst, sh, mh, start=first, stop=False)
                        pe.matmul(dst, sh, ml, start=False, stop=False)
                        mm = pe.matmul(dst, sl, mh, start=False, stop=last)
                    if ks[-1] == KD - 1:
                        mm.then_inc(unit_done, 1)

                def group(name):
                    for m in range(4):
                        begin(name, m)
                        part(name, m, range(KD))

                def narrow_group(name, hi, lo):
                    chunk = group_chunks[name][0]
                    pe.wait_ge(lo_done, chunk + 1)
                    for m in range(4):
                        begin(name, m)
                        pairs = [(split_view(w_hi, chunk)[:, k, m * P:(m + 1) * P],
                                  split_view(w_lo, chunk)[:, k, m * P:(m + 1) * P], hi[:, k, :], lo[:, k, :])
                                 for k in range(4)]
                        exact3(pe, bank(name, m), pairs).then_inc(unit_done, 1)

                def diagonal(t):
                    i = 8 * t
                    if i >= 2:
                        pe.wait_ge(sc_read, i - 1)
                    for h in range(HEADS):
                        mm = pe.matmul(ps[:, 3 + i % 2, h * P:(h + 1) * P], kT[:, h, t * P:(t + 1) * P],
                                       qT[:, h, t * P:(t + 1) * P], start=(h == 0), stop=True, skip_group_check=True)
                    mm.then_inc(diag_done, 1)

                def step(t, level):
                    n = 9 * t + level
                    pe.wait_ge(kd_ready, sum(v % 9 != 8 for v in range(n + 1)))
                    pe.wait_ge(qd_ready, sum(v % 9 != 7 for v in range(n + 1)))
                    i = 8 * t + level + 1
                    if level < LEVELS:
                        pe.wait_ge(sc_read, i - 1)
                        for h in range(HEADS):
                            mm = pe.matmul(ps[:, 3 + i % 2, h * P:(h + 1) * P], k_dec[:, n % 2, h, :],
                                           q_dec[:, n % 2, h, :], start=(h == 0), stop=True, skip_group_check=True)
                    elif level == 7:
                        if t >= 1:
                            pe.wait_ge(oT_lo_ready, t)
                        for h in range(HEADS):
                            mm = pe.transpose(ps[:, 5, h * P:(h + 1) * P], k_dec[:, n % 2, h, :], ident)
                    else:
                        pe.wait_ge(sc_read, 8 * (t + 1))
                        if t >= 1:
                            pe.wait_ge(o_read, t)
                            pe.wait_ge(state_ready, t)
                        for h in range(HEADS):
                            dst = ps[:, 6, h * P:(h + 1) * P]
                            mm = pe.matmul(dst, scores[:, h, :], v_tok[:, t, h * P:(h + 1) * P], start=(h == 0),
                                           stop=(t == 0), skip_group_check=True)
                            if t >= 1:
                                mm = pe.matmul(dst, q_dec[:, n % 2, h, :], state[:, h, :], start=False, stop=True,
                                               skip_group_check=True)
                    mm.then_inc(dec_used, 1)

                def new_state(t):
                    pe.wait_ge(ktok_ready, t + 1)
                    if t >= 1:
                        pe.wait_ge(state_ready, t)
                    for h in range(HEADS):
                        mm = pe.matmul(ps[:, 7, h * P:(h + 1) * P], k_tok[:, h, :], v_tok[:, t, h * P:(h + 1) * P],
                                       start=(h == 0), stop=True, skip_group_check=True)
                    mm.then_inc(state_sum, 1)

                def turn_output(t):
                    pe.wait_ge(o_ready, t + 1)
                    pe.wait_ge(ktok_ready, t + 1)
                    for h in range(HEADS):
                        mm = pe.transpose(ps[:, 5, h * P:(h + 1) * P], o_norm[:, h, :], ident)
                    mm.then_inc(o_turned, 1)

                group("f")
                group("q")
                group("v")
                pe.wait_ge(k_ready, HEADS)
                pe.wait_ge(act_read, 3 * HEADS)
                for t, name in enumerate(("g", "cc", "ch", "cb")):
                    for m in range(4):
                        begin(name, m)
                        part(name, m, range(0, 3))
                        if m == 0:
                            diagonal(t)
                        elif m == 3:
                            step(t, 8)
                        else:
                            step(t, 3 * m - 1)
                        part(name, m, range(3, 6))
                        if m == 3:
                            new_state(t)
                        else:
                            step(t, 3 * m)
                        part(name, m, range(6, 8))
                        if m < 3:
                            step(t, 3 * m + 1)
                    turn_output(t)
                for h in range(2):
                    group(f"ga{h}")
                    pe.wait_ge(oT_lo_ready, TT)
                    narrow_group(f"ya{h}", oT_hi, oT_lo)
                    group(f"gb{h}")
                    pe.wait_ge(yc_ready, 4)
                    narrow_group(f"yb{h}", yc_hi, yc_lo)

        row_sum = sem("row_sum")
        row_ready_a = sem("row_ready_a")
        row_ready_v = sem("row_ready_v")
        wf_in = sem("wf_in")
        wr_in = sem("wr_in")
        xt_in = [sem(f"xt_in{s}") for s in range(2)]
        mix_done = sem("mix_done")
        mix_read = sem("mix_read")
        h2_ready = sem("h2_ready")
        h2_sq = sem("h2_sq")
        h2_rms = sem("h2_rms")
        u2_ready = sem("u2_ready")
        u2_turned = sem("u2_turned")
        u2T_ready = sem("u2T_ready")
        routed = sem("routed")
        stored_h = [sem(f"stored_h{s}") for s in range(2)]
        stored_u = [sem(f"stored_u{s}") for s in range(2)]
        dve3 = sem("dve3")

        with nc.Block() as block:
            @block.sync
            def _(sp):
                def store(sp, t):
                    sp.wait_ge(h2_ready, t + 1)
                    sp.dma_start(h2_d[t * P:(t + 1) * P, :], h2[:, t % 2, :]).then_inc(stored_h[t % 2], 16)
                    sp.wait_ge(u2_ready, t + 1)
                    sp.dma_start(u2_d[t * P:(t + 1) * P, :], u2[:, t % 2, :]).then_inc(stored_u[t % 2], 16)

                sp.dma_start(wf_row[:], norm_ffn_w[0:1, :].to_broadcast([P, D])).then_inc(wf_in, 16)
                sp.dma_start(wr[:], w_router[0].rearrange("(k p) e -> p k e", p=P)).then_inc(wr_in, 16)
                sp.dma_start(br[:], b_router).then_inc(wr_in, 16)
                sp.wait_ge(row_sum, 1)
                for t in range(TT):
                    if t >= 2:
                        sp.wait_ge(h2_ready, t - 1)
                    sp.dma_start(x_t[:, t % 2, :], x2[t * P:(t + 1) * P, :]).then_inc(xt_in[t % 2], 16)
                    if t >= 1:
                        store(sp, t - 1)
                store(sp, TT - 1)
                for s in range(2):
                    sp.wait_ge(stored_h[s], 16 * TT // 2)
                    sp.wait_ge(stored_u[s], 16 * TT // 2)

            @block.scalar
            def _(act):
                act.wait_ge(row_sum, 1)
                for r in (0, 1, 3):
                    act.activation(gate_f[:] if r == 3 else rows[:, r, :], ps[:, 2 * r:2 * r + 2, :].rearrange("p b n -> p (b n)"),
                                   ACT.Copy).then_inc(row_ready_a, 1)
                for t in range(TT):
                    act.wait_ge(h2_ready, t + 1)
                    if t >= 1:
                        act.wait_ge(u2_ready, t)
                    act.activation(tmp_j[:], h2[:, t % 2, :], ACT.Square, scale=D ** -0.5,
                                   accum_out=ms[:, t:t + 1]).then_inc(h2_sq, 1)
                    act.wait_ge(h2_sq, t + 1)
                    act.activation(rstd[:, t:t + 1], ms[:, t:t + 1], ACT.Sqrt, bias=eps).then_inc(h2_rms, 1)
                    act.wait_ge(u2_turned, t + 1)
                    if t >= 1:
                        act.wait_ge(routed, t)
                    act.activation(u2T[:], ps[:, 4:6, :].rearrange("p b n -> p (b n)"), ACT.Copy).then_inc(u2T_ready, 1)

            @block.vector
            def _(dve):
                chain = Chain(dve, dve3)
                dve.wait_ge(row_sum, 1)
                dve.wait_ge(wf_in, 16)
                dve.scalar_tensor_tensor(rows[:, 2, :], ps[:, 4:6, :].rearrange("p b n -> p (b n)"), 1.0, wf_row[:],
                                         ALU.add, ALU.mult).then_inc(row_ready_v, 1)
                dve.wait_ge(row_ready_v, 1)
                dve.wait_ge(row_ready_a, 3)
                for t in range(TT):
                    b = 2 * (t % 2)
                    dve.wait_ge(mix_done, t + 1)
                    if t >= 2:
                        dve.wait_ge(stored_h[t % 2], 16 * (t // 2))
                        dve.wait_ge(stored_u[t % 2], 16 * (t // 2))
                        dve.wait_ge(u2_turned, t - 1)
                    dve.tensor_tensor(h2[:, t % 2, :], ps[:, b:b + 2, :].rearrange("p b n -> p (b n)"), rows[:, 0, :],
                                      ALU.mult).then_inc(mix_read, 1)
                    dve.wait_ge(mix_read, t + 1)
                    dve.wait_ge(xt_in[t % 2], 16 * (t // 2 + 1))
                    dve.tensor_tensor(h2[:, t % 2, :], h2[:, t % 2, :], x_t[:, t % 2, :], ALU.add).then_inc(h2_ready, 1)
                    dve.wait_ge(h2_rms, t + 1)
                    chain(dve.reciprocal(rstd[:, t:t + 1], rstd[:, t:t + 1]))
                    chain(dve.scalar_tensor_tensor(u2[:, t % 2, :], h2[:, t % 2, :], rstd[:, t:t + 1], rows[:, 2, :],
                                                   ALU.mult, ALU.mult))
                    dve.tensor_tensor(u2[:, t % 2, :], u2[:, t % 2, :], rows[:, 1, :], ALU.add).then_inc(u2_ready, 1)

            @block.tensor
            def _(pe):
                for r in range(8):
                    mm = pe.matmul(ps[:, r, :], ones, ada12[:, r // 4, (r % 4) * 512:(r % 4 + 1) * 512], start=True,
                                   stop=True)
                mm.then_inc(row_sum, 1)
                pe.wait_ge(row_ready_a, 3)
                pe.wait_ge(row_ready_v, 1)
                pe.wait_ge(wr_in, 32)

                def route(t):
                    pe.wait_ge(u2_ready, t + 1)
                    if t >= 1:
                        pe.wait_ge(u2T_ready, t)
                    for k in range(KD):
                        mm = pe.transpose(ps[:, 4 + k // 4, (k % 4) * P:(k % 4 + 1) * P], u2[:, t % 2, k * P:(k + 1) * P],
                                          ident)
                    mm.then_inc(u2_turned, 1)
                    pe.wait_ge(u2T_ready, t + 1)
                    dst = ps[:, 6, t * E:(t + 1) * E]
                    pe.matmul(dst, ones[0:1, :], br[:], start=(t == 0), stop=False, skip_group_check=True)
                    for k in range(KD):
                        mm = pe.matmul(dst, u2T[:, k * P:(k + 1) * P], wr[:, k, :], start=False, stop=(k == KD - 1),
                                       skip_group_check=True)
                    mm.then_inc(routed, 1)

                for t in range(TT):
                    if t >= 2:
                        pe.wait_ge(mix_read, t - 1)
                    for n in range(2):
                        pairs = []
                        for k in range(KD):
                            chunk = group_chunks[f"mix{n}"][k // 4]
                            pairs.append((merged_hi[:, k, t * P:(t + 1) * P], merged_lo[:, k, t * P:(t + 1) * P],
                                          split_view(w_hi, chunk)[:, k % 4, :], split_view(w_lo, chunk)[:, k % 4, :]))
                        mm = exact3(pe, ps[:, 2 * (t % 2) + n, :], pairs)
                    mm.then_inc(mix_done, 1)
                    if t >= 1:
                        route(t - 1)
                route(TT - 1)

        bias_in = sem("bias_in")
        bias_zero = sem("bias_zero")
        bias_ready = sem("bias_ready")
        pexp_in = sem("pexp_in")
        pexp = sem("pexp")
        chosen_ready = sem("chosen_ready")
        counted = sem("counted")
        nex_ready = sem("nex_ready")
        nex_sum = sem("nex_sum")
        mex_ready = sem("mex_ready")
        mex_sum = sem("mex_sum")
        slot_ready = sem("slot_ready")
        slot_used = sem("slot_used")
        dve4 = sem("dve4")

        raw_in = [sem(f"raw_in{s}") for s in range(RAWS)]
        x_hi_done = sem("x_hi_done")
        x_lo_dve = sem("x_lo_dve")
        x_lo_pool = sem("x_lo_pool")
        x_used = sem("x_used")

        def known(v):
            return type(v) is int

        def lo_wait(eng, i, off):
            quad = 3 * i + off // 4
            if off % 4 == 3:
                eng.wait_ge(x_lo_pool, quad + 1)
            else:
                eng.wait_ge(x_lo_dve, 3 * quad + off % 4 + 1)

        def expert_load(eng, i, off, expert, part, j):
            if not known(i) or 12 * i + off >= RAWS:
                lo_wait(eng, i, off - RAWS)
            slot = off % RAWS
            one = bass.ds(expert, 1)
            if part == "w1":
                src = w1[0, one, j * P:(j + 1) * P, :].rearrange("e p n -> p (e n)")
                dst = raw[:, slot, :]
            else:
                src = w2[0, one, 2 * j * P:2 * (j + 1) * P, :].rearrange("e (k p) n -> p (e k) n", p=P)
                dst = raw[:, slot, :].rearrange("p (k n) -> p k n", k=2)
            eng.dma_start(dst, src).then_inc(raw_in[slot], 16)

        with nc.Block() as block:
            @block.sync
            def _(sp):
                for j in range(8):
                    expert_load(sp, 0, j, 0, "w1", j)
                for j in range(4):
                    expert_load(sp, 1, -4 + j, 1, "w1", j)

            @block.gpsimd
            def _(pool):
                for half_ in range(2):
                    pool.dma_start(b1_raw[32 * half_:32 * half_ + E, :], b1[0]).then_inc(bias_in, 16)
                    pool.dma_start(b2_raw[32 * half_:32 * half_ + E, :], b2[0]).then_inc(bias_in, 16)
                pool.memset(bias1[64:P, :].bitcast(F32), 0.0).then_inc(bias_zero, 1)
                pool.memset(bias2[64:P, :].bitcast(F32), 0.0).then_inc(bias_zero, 1)
                pool.wait_ge(bias_in, 64)
                pool.tensor_copy(bias1[0:64, :], b1_raw[0:64, :]).then_inc(bias_zero, 1)
                pool.tensor_copy(bias2[0:64, :], b2_raw[0:64, :]).then_inc(bias_zero, 1)
                pool.wait_ge(bias_zero, 4)
                pool.tensor_tensor(bias1[32:64, :], b1_raw[32:64, :], bias1[32:64, :].bitcast(F32),
                                   ALU.subtract).then_inc(bias_ready, 1)
                pool.tensor_tensor(bias2[32:64, :], b2_raw[32:64, :], bias2[32:64, :].bitcast(F32),
                                   ALU.subtract).then_inc(bias_ready, 1)
                pool.wait_ge(bias_ready, 2)
                pool.memset(hs[:], 0.0).then_inc(bias_ready, 1)

            @block.scalar
            def _(act):
                act.wait_ge(pexp_in, 1)
                act.activation(prob[:], prob[:], ACT.Exp).then_inc(pexp, 1)

            @block.vector
            def _(dve):
                chain = Chain(dve, dve4)
                chain(dve.tensor_copy(lg[:], ps[:, 6, 0:TT * E].rearrange("p (t e) -> p t e", e=E)))
                for t in range(TT):
                    chain(dve.max(val8[:, t, :], lg[:, t, :]))
                    chain(dve.max_index(idx8[:, t, :], val8[:, t, :], lg[:, t, :]))
                chain(dve.tensor_copy(idxf[:], idx8[:]))
                chain(dve.tensor_tensor(
                    onehot[:], idxf[:, :, 0:TOP, None].to_broadcast([P, TT, TOP, E]),
                    iota[:, None, None, 0:E].to_broadcast([P, TT, TOP, E]), ALU.is_equal))
                dve.tensor_reduce(chosen[:], onehot[:].rearrange("p t k e -> p t e k"), AX.X,
                                  ALU.add).then_inc(chosen_ready, 1)
                dve.tensor_tensor(prob[:], val8[:, :, 0:TOP], val8[:, :, 0:1].to_broadcast([P, TT, TOP]),
                                  ALU.subtract).then_inc(pexp_in, 1)
                dve.wait_ge(pexp, 1)
                chain(dve.tensor_reduce(psm[:], prob[:], AX.X, ALU.add))
                chain(dve.reciprocal(prc[:], psm[:]))
                chain(dve.tensor_tensor(vv[:, 2, :].rearrange("p (t k) -> p t k", k=TOP), prob[:],
                                        prc[:, :, None].to_broadcast([P, TT, TOP]), ALU.mult))
                chain(dve.tensor_copy(vv[:, 0:2, :].rearrange("p a n -> p (a n)"), const[:, C_TOK:C_TOK + 32]))
                dve.wait_ge(counted, 1)
                for t in range(TT):
                    chain(dve.tensor_tensor(ohpos[:, t], onehot[:, t],
                                            ps[:, 0, t * E:(t + 1) * E][:, None, :].to_broadcast([P, TOP, E]), ALU.mult))
                chain(dve.tensor_reduce(pos[:].rearrange("p (t k) -> p t k", k=TOP), ohpos[:], AX.X, ALU.add))
                for b in range(3):
                    chain(dve.tensor_scalar(ge[:, b, :], pos[:], 128.0 * (b + 1), None, ALU.is_ge))
                chain(dve.tensor_tensor(blk[:], ge[:, 0, :], ge[:, 1, :], ALU.add))
                chain(dve.tensor_tensor(blk[:], blk[:], ge[:, 2, :], ALU.add))
                chain(dve.scalar_tensor_tensor(pos[:], blk[:], -128.0, pos[:], ALU.mult, ALU.add))
                chain(dve.scalar_tensor_tensor(qcol[:].rearrange("p (t k) -> p t k", k=TOP), idxf[:, :, 0:TOP], 4.0,
                                               blk[:].rearrange("p (t k) -> p t k", k=TOP), ALU.mult, ALU.add))
                for b in range(3):
                    chain(dve.tensor_scalar(cnt[:, 1 + b:2 + b], ps[0:E, 0, 160:161], 128.0 * (b + 1), None, ALU.is_gt))
                chain(dve.tensor_tensor(cnt[:, 4:5], cnt[:, 1:2], cnt[:, 2:3], ALU.add))
                dve.tensor_tensor(cnt[:, 4:5], cnt[:, 4:5], cnt[:, 3:4], ALU.add).then_inc(nex_ready, 1)
                for j in range(16):
                    if j >= 2:
                        dve.wait_ge(slot_used, j - 1)
                    dve.tensor_scalar(slot_row[:, j % 2, :], iota, pos[:, j:j + 1], None, ALU.is_equal)
                    for a in range(3):
                        ins = dve.tensor_scalar(slot_col[:, j % 2, a, :], iota, qcol[:, j:j + 1], vv[:, a, j:j + 1],
                                                ALU.is_equal, ALU.mult)
                    ins.then_inc(slot_ready, 1)
                dve.wait_ge(nex_sum, 1)
                chain(dve.tensor_copy(cnt[:, 0:1], ps[0:E, 1, 0:1]))
                chain(dve.memset(mex[:], 0.0))
                for b in range(3):
                    chain(dve.tensor_scalar(cnt[:, 5:6], cnt[:, 0:1], float(b), None, ALU.add))
                    chain(dve.tensor_scalar(mtmp[:, 0, :], iota[0:E, 0:MAX_EXTRA], cnt[:, 5:6], cnt[:, 1 + b:2 + b],
                                            ALU.is_equal, ALU.mult))
                    chain(dve.tensor_scalar(mtmp[:, 1, :], mtmp[:, 0, :], float(b + 1), None, ALU.mult))
                    ins = dve.tensor_tensor(mex[:], mex[:], mtmp[:], ALU.add)
                    if b < 2:
                        chain(ins)
                    else:
                        ins.then_inc(mex_ready, 1)
                chain(dve.memset(btf[:], 0.0))
                chain(dve.tensor_copy(btf[:, 0:E], iota[0:1, 0:E]))
                chain(dve.tensor_scalar(btf[:, MAX_BLOCKS:MAX_BLOCKS + E], iota[0:1, 0:E], 4.0, None, ALU.mult))
                dve.wait_ge(mex_sum, 1)
                chain(dve.tensor_copy(btf[:, E:MAX_BLOCKS], ps[0:1, 1, 64:64 + MAX_EXTRA]))
                chain(dve.tensor_copy(btf[:, MAX_BLOCKS + E:2 * MAX_BLOCKS], ps[0:1, 1, 96:96 + MAX_EXTRA]))
                chain(dve.tensor_copy(btf[:, 2 * MAX_BLOCKS:2 * MAX_BLOCKS + 1], ps[0:1, 1, 32:33]))
                chain(dve.tensor_copy(bt[:], btf[:]))
                dve.wait_ge(slot_used, 16)
                chain(dve.tensor_scalar(tabI[:].rearrange("p a n -> p (a n)"), ps[:, 2, 0:2 * P], UNFILLED, None, ALU.add))
                chain(dve.tensor_copy(tabW[:], ps[:, 2, 2 * P:3 * P]))

            @block.tensor
            def _(pe):
                pe.wait_ge(chosen_ready, 1)
                first = True
                for t in range(TT):
                    for s in range(t + 1):
                        pe.matmul(ps[:, 0, t * E:(t + 1) * E], tri if s == t else ones, chosen[:, s, :], start=first,
                                  stop=(s == t), skip_group_check=True)
                        first = False
                for s in range(TT):
                    mm = pe.matmul(ps[0:E, 0, 160:161], chosen[:, s, :], ones[:, 0:1], start=False, stop=(s == TT - 1),
                                   skip_group_check=True)
                mm.then_inc(counted, 1)
                pe.wait_ge(nex_ready, 1)
                pe.matmul(ps[0:E, 1, 0:1], tri[0:E, 0:E], cnt[:, 4:5], start=True, stop=True, skip_group_check=True)
                pe.matmul(ps[0:1, 1, 32:33], ones[0:E, 0:1], cnt[:, 4:5], start=False, stop=True,
                          skip_group_check=True).then_inc(nex_sum, 1)
                for j in range(16):
                    pe.wait_ge(slot_ready, j + 1)
                    pe.matmul(ps[:, 2, 0:3 * P], slot_row[:, j % 2, :],
                              slot_col[:, j % 2].rearrange("p a n -> p (a n)"), start=(j == 0),
                              stop=(j == 15)).then_inc(slot_used, 1)
                pe.wait_ge(mex_ready, 1)
                pe.matmul(ps[0:1, 1, 64:64 + MAX_EXTRA], const[0:E, C_PART:C_PART + 1], mex[:, 0, :], start=False,
                          stop=True, skip_group_check=True)
                pe.matmul(ps[0:1, 1, 96:96 + MAX_EXTRA], const[0:E, C_PART + 1:C_PART + 2], mex[:, 0, :], start=False,
                          stop=False, skip_group_check=True)
                pe.matmul(ps[0:1, 1, 96:96 + MAX_EXTRA], ones[0:E, 0:1], mex[:, 1, :], start=False, stop=True,
                          skip_group_check=True).then_inc(mex_sum, 1)

        gathered = sem("gathered")
        hs_turned = sem("hs_turned")
        hsT_hi_ready = sem("hsT_hi_ready")
        hsT_lo_ready = sem("hsT_lo_ready")
        sel1_ready = sem("sel1_ready")
        sel2_ready = sem("sel2_ready")
        tok_ready = sem("tok_ready")
        row_ready = sem("row_ready")
        wcol_ready = sem("wcol_ready")
        w1_started = sem("w1_started")
        w2_started = sem("w2_started")
        glu_ready = sem("glu_ready")
        sig_ready = sem("sig_ready")
        hid_read = sem("hid_read")
        gs_ready = sem("gs_ready")
        act_ready = sem("act_ready")
        a_turned = sem("a_turned")
        aT_hi_ready = sem("aT_hi_ready")
        aT_lo_ready = sem("aT_lo_ready")
        y_ready = sem("y_ready")
        scattered = sem("scattered")
        row_last = sem("row_last")
        y_last = sem("y_last")

        def w1_end(b):
            return 8 if known(b) and b == 0 else 12 * b + 4

        def w2_end(b, last=False):
            return 12 * b + (12 if last else 20)

        OUTB, TPB = slice(4, 6), slice(6, 8)

        def blocks(eng):
            return E + eng.value_load(bt[0:1, 2 * MAX_BLOCKS:2 * MAX_BLOCKS + 1], min_val=0, max_val=MAX_EXTRA - 1)

        def expert_of(eng, i):
            if known(i) and i < E:
                return i
            return eng.value_load(bt[0:1, bass.ds(i, 1)], min_val=0, max_val=E - 1)

        def column_of(eng, i):
            return eng.value_load(bt[0:1, bass.ds(i + MAX_BLOCKS, 1)], min_val=0, max_val=P - 1)

        with nc.Block() as block:
            @block.sync
            def _(sp):
                n = blocks(sp)
                for j in range(4, 8):
                    expert_load(sp, 1, -4 + j, 1, "w1", j)
                with sp.Fori(2, n) as i:
                    e2 = expert_of(sp, i - 2)
                    for j in range(4):
                        expert_load(sp, i, -8 + j, e2, "w2", j)
                    e1 = expert_of(sp, i)
                    for j in range(8):
                        expert_load(sp, i, -4 + j, e1, "w1", j)
                e2 = expert_of(sp, n - 2)
                for j in range(4):
                    expert_load(sp, n, -8 + j, e2, "w2", j)
                e2 = expert_of(sp, n - 1)
                for j in range(4):
                    expert_load(sp, n, -4 + j, e2, "w2", j)

            @block.gpsimd
            def _(pool):
                n = blocks(pool)

                def split_lo(i, off):
                    pool.wait_ge(x_hi_done, 12 * i + off + 1)
                    pool.tensor_tensor(w_lo[:, off % SPLITS, :], raw[:, off % RAWS, :],
                                       w_hi[:, off % SPLITS, :].bitcast(F32), ALU.subtract).then_inc(x_lo_pool, 1)

                def pick(b):
                    col = column_of(pool, b)
                    if not known(b) or b >= 1:
                        pool.wait_ge(gathered, 16 * b)
                    pool.tensor_copy(cur_tok[:], tabI[:, 0, bass.ds(col, 1)]).then_inc(tok_ready, 1)

                def await_pick(b):
                    pool.wait_ge(tok_ready, b + 1)
                    if not known(b) or b >= 1:
                        pool.wait_ge(hs_turned, b)

                def gather():
                    pool.indirect_dma_start(out=hs[:], out_offset=None, in_=u2_d,
                                            in_offset=bass.IndirectOffsetOnAxis(ap=cur_tok[:], axis=0),
                                            bounds_check=TOKENS - 1, oob_is_err=False).then_inc(gathered, 16)

                def select(sel, b, ready, started):
                    e = expert_of(pool, b)
                    if not known(b) or b >= 1:
                        pool.wait_ge(started, b)
                    pool.tensor_copy(sel[:], const[:, bass.ds(e + C_EYE2, 1)].to_broadcast([P, P])).then_inc(ready, 1)

                def weigh(b, done=row_ready):
                    col = column_of(pool, b)
                    if not known(b) or b >= 1:
                        pool.wait_ge(scattered, 16 * b)
                        pool.wait_ge(y_ready, b)
                    pool.tensor_copy(cur_w[:], tabW[:, bass.ds(col, 1)]).then_inc(wcol_ready, 1)
                    pool.tensor_copy(cur_row[:], tabI[:, 1, bass.ds(col, 1)]).then_inc(done, 1)

                def await_y(b):
                    pool.wait_ge(row_ready, b + 1)
                    pool.wait_ge(y_ready, b + 1)

                def scatter():
                    pool.indirect_dma_start(out=y_d, out_offset=bass.IndirectOffsetOnAxis(ap=cur_row[:], axis=0),
                                            in_=y_out[:], in_offset=None, bounds_check=TOKENS * TOP - 1,
                                            oob_is_err=False).then_inc(scattered, 16)

                pick(0)
                await_pick(0)
                gather()
                select(sel1, 0, sel1_ready, w1_started)
                split_lo(0, 3)
                pick(1)
                await_pick(1)
                gather()
                split_lo(0, 7)
                select(sel1, 1, sel1_ready, w1_started)
                split_lo(1, -1)
                pick(2)
                await_pick(2)
                gather()
                split_lo(1, 3)
                with pool.Fori(2, n) as i:
                    select(sel2, i - 2, sel2_ready, w2_started)
                    weigh(i - 2)
                    split_lo(i, -5)
                    pick(i + 1)
                    select(sel1, i, sel1_ready, w1_started)
                    await_pick(i + 1)
                    split_lo(i, -1)
                    gather()
                    await_y(i - 2)
                    split_lo(i, 3)
                    scatter()
                select(sel2, n - 2, sel2_ready, w2_started)
                weigh(n - 2)
                split_lo(n, -5)
                await_y(n - 2)
                split_lo(n, -1)
                scatter()
                select(sel2, n - 1, sel2_ready, w2_started)
                weigh(n - 1, row_last)
                pool.wait_ge(row_last, 1)
                pool.wait_ge(y_last, 1)
                scatter()
                pool.wait_ge(scattered, 16 * n)

            @block.scalar
            def _(act):
                n = blocks(act)

                def split_hi(i, off):
                    act.wait_ge(raw_in[off % RAWS], 16 * (i + off // RAWS + 1))
                    if not known(i) or 12 * i + off >= SPLITS:
                        act.wait_ge(x_used, 12 * i + off - SPLITS + 1)
                    act.activation(w_hi[:, off % SPLITS, :], raw[:, off % RAWS, :], ACT.Copy).then_inc(x_hi_done, 1)

                def rows_hi(b):
                    act.wait_ge(hs_turned, b + 1)
                    if not known(b) or b >= 1:
                        act.wait_ge(x_used, w1_end(b - 1))
                    act.activation(hsT_hi[:].rearrange("p k t -> p (k t)"), ps[:, TPB, :].rearrange("p b n -> p (b n)"),
                                   ACT.Copy).then_inc(hsT_hi_ready, 1)

                def sigmoid(b):
                    act.wait_ge(glu_ready, b + 1)
                    if not known(b) or b >= 1:
                        act.wait_ge(act_ready, b)
                    act.activation(sig[:], glu[:], ACT.Sigmoid, scale=ALPHA).then_inc(sig_ready, 1)

                def act_hi(b):
                    act.wait_ge(a_turned, b + 1)
                    if not known(b) or b >= 1:
                        act.wait_ge(x_used, w2_end(b - 1))
                    act.activation(aT_hi[:].rearrange("p k t -> p (k t)"), ps[:, TPB, :].rearrange("p b n -> p (b n)"),
                                   ACT.Copy).then_inc(aT_hi_ready, 1)

                def weigh_out(b, last=False):
                    act.wait_ge(x_used, w2_end(b, last))
                    act.wait_ge(wcol_ready, b + 1)
                    if not known(b) or b >= 1:
                        act.wait_ge(scattered, 16 * b)
                    act.activation(y_out[:], ps[:, OUTB, :].rearrange("p b n -> p (b n)"), ACT.Copy,
                                   scale=cur_w[:]).then_inc(y_last if last else y_ready, 1)

                for j in range(4):
                    split_hi(0, j)
                rows_hi(0)
                for j in range(4, 8):
                    split_hi(0, j)
                for j in range(4):
                    split_hi(1, -4 + j)
                rows_hi(1)
                sigmoid(0)
                for j in range(4, 8):
                    split_hi(1, -4 + j)
                act_hi(0)
                with act.Fori(2, n) as i:
                    for j in range(4):
                        split_hi(i, -8 + j)
                    sigmoid(i - 1)
                    rows_hi(i)
                    for j in range(4):
                        split_hi(i, -4 + j)
                    weigh_out(i - 2)
                    for j in range(4, 8):
                        split_hi(i, -4 + j)
                    act_hi(i - 1)
                for j in range(4):
                    split_hi(n, -8 + j)
                sigmoid(n - 1)
                for j in range(4):
                    split_hi(n, -4 + j)
                weigh_out(n - 2)
                act_hi(n - 1)
                weigh_out(n - 1, last=True)

            @block.vector
            def _(dve):
                n = blocks(dve)

                def split_lo(i, off):
                    if off % SPLITS == 3:
                        return
                    dve.wait_ge(x_hi_done, 12 * i + off + 1)
                    dve.tensor_tensor(w_lo[:, off % SPLITS, :], raw[:, off % RAWS, :],
                                      w_hi[:, off % SPLITS, :].bitcast(F32), ALU.subtract).then_inc(x_lo_dve, 1)

                def rows_lo(b):
                    dve.wait_ge(hsT_hi_ready, b + 1)
                    dve.tensor_tensor(hsT_lo[:].rearrange("p k t -> p (k t)"),
                                      ps[:, TPB, :].rearrange("p b n -> p (b n)"),
                                      hsT_hi[:].rearrange("p k t -> p (k t)").bitcast(F32),
                                      ALU.subtract).then_inc(hsT_lo_ready, 1)

                def clamp(b):
                    dve.wait_ge(x_used, w1_end(b))
                    if not known(b) or b >= 1:
                        dve.wait_ge(gs_ready, b)
                    dve.tensor_scalar(glu[:], ps[:, 0:2, :].rearrange("p b n -> p (b n)"), LIMIT, None,
                                      ALU.min).then_inc(glu_ready, 1)
                    if not known(b) or b >= 1:
                        dve.wait_ge(a_turned, b)
                    dve.tensor_scalar(lin[:], ps[:, 2:4, :].rearrange("p b n -> p (b n)"), LIMIT, -LIMIT, ALU.min,
                                      ALU.max).then_inc(hid_read, 1)

                def swish(b):
                    dve.wait_ge(sig_ready, b + 1)
                    dve.tensor_tensor(sig[:], sig[:], glu[:], ALU.mult).then_inc(gs_ready, 1)
                    dve.wait_ge(gs_ready, b + 1)
                    dve.wait_ge(hid_read, b + 1)
                    dve.scalar_tensor_tensor(lin[:], lin[:], 1.0, sig[:], ALU.add, ALU.mult).then_inc(act_ready, 1)

                def act_lo(b):
                    dve.wait_ge(aT_hi_ready, b + 1)
                    dve.tensor_tensor(aT_lo[:].rearrange("p k t -> p (k t)"),
                                      ps[:, TPB, :].rearrange("p b n -> p (b n)"),
                                      aT_hi[:].rearrange("p k t -> p (k t)").bitcast(F32),
                                      ALU.subtract).then_inc(aT_lo_ready, 1)

                for j in range(4):
                    split_lo(0, j)
                rows_lo(0)
                for j in range(4, 8):
                    split_lo(0, j)
                for j in range(4):
                    split_lo(1, -4 + j)
                rows_lo(1)
                clamp(0)
                swish(0)
                for j in range(4, 8):
                    split_lo(1, -4 + j)
                act_lo(0)
                with dve.Fori(2, n) as i:
                    for j in range(4):
                        split_lo(i, -8 + j)
                    clamp(i - 1)
                    rows_lo(i)
                    split_lo(i, -4)
                    swish(i - 1)
                    for j in range(1, 8):
                        split_lo(i, -4 + j)
                    act_lo(i - 1)
                for j in range(4):
                    split_lo(n, -8 + j)
                clamp(n - 1)
                swish(n - 1)
                for j in range(4):
                    split_lo(n, -4 + j)
                act_lo(n - 1)

            @block.tensor
            def _(pe):
                n = blocks(pe)

                def turn_rows(b):
                    pe.wait_ge(gathered, 16 * (b + 1))
                    if not known(b):
                        pe.wait_ge(aT_lo_ready, b - 1)
                    elif b >= 2:
                        pe.wait_ge(aT_lo_ready, b - 1)
                    elif b == 1:
                        pe.wait_ge(hsT_lo_ready, 1)
                    for k in range(KD):
                        mm = pe.transpose(ps[:, 6 + k // 4, (k % 4) * P:(k % 4 + 1) * P], hs[:, k * P:(k + 1) * P], ident)
                    mm.then_inc(hs_turned, 1)

                def turn_act(b):
                    pe.wait_ge(act_ready, b + 1)
                    pe.wait_ge(hsT_lo_ready, b + 2)
                    for k in range(KD):
                        mm = pe.transpose(ps[:, 6 + k // 4, (k % 4) * P:(k % 4 + 1) * P], lin[:, k * P:(k + 1) * P], ident)
                    mm.then_inc(a_turned, 1)

                def turn_last(pe, n):
                    pe.wait_ge(act_ready, n)
                    for k in range(KD):
                        mm = pe.transpose(ps[:, 6 + k // 4, (k % 4) * P:(k % 4 + 1) * P], lin[:, k * P:(k + 1) * P], ident)
                    mm.then_inc(a_turned, 1)

                def w1_bias(b):
                    pe.wait_ge(sel1_ready, b + 1)
                    if not known(b) or b >= 1:
                        pe.wait_ge(hid_read, b)
                        pe.wait_ge(glu_ready, b)
                    for q in range(4):
                        mm = pe.matmul(ps[:, q, :], sel1[:], bias1[:, q * 512:(q + 1) * 512], start=True, stop=False)
                    mm.then_inc(w1_started, 1)
                    pe.wait_ge(hsT_lo_ready, b + 1)

                def w1_chunk(b, i, off, j):
                    lo_wait(pe, i, off)
                    s = off % SPLITS
                    for q in range(4):
                        mh, ml = (w[:, s, q * 512:(q + 1) * 512] for w in (w_hi, w_lo))
                        pe.matmul(ps[:, q, :], hsT_hi[:, j, :], mh, start=False, stop=False)
                        pe.matmul(ps[:, q, :], hsT_hi[:, j, :], ml, start=False, stop=False)
                        mm = pe.matmul(ps[:, q, :], hsT_lo[:, j, :], mh, start=False, stop=(j == 7))
                    mm.then_inc(x_used, 1)

                def w2_block(b, i, off):
                    pe.wait_ge(sel2_ready, b + 1)
                    if not known(b) or b >= 1:
                        pe.wait_ge(y_ready, b)
                    for q in range(2):
                        mm = pe.matmul(ps[:, 4 + q, :], sel2[:], bias2[:, q * 512:(q + 1) * 512], start=True, stop=False)
                    mm.then_inc(w2_started, 1)
                    pe.wait_ge(aT_lo_ready, b + 1)
                    for j in range(4):
                        lo_wait(pe, i, off + j)
                        s = (off + j) % SPLITS
                        for kk in range(2):
                            k = 2 * j + kk
                            for q in range(2):
                                at_ = kk * D + q * 512
                                mh, ml = (w[:, s, at_:at_ + 512] for w in (w_hi, w_lo))
                                dst = ps[:, 4 + q, :]
                                pe.matmul(dst, aT_hi[:, k, :], mh, start=False, stop=False)
                                pe.matmul(dst, aT_hi[:, k, :], ml, start=False, stop=False)
                                mm = pe.matmul(dst, aT_lo[:, k, :], mh, start=False, stop=(k == KD - 1))
                        mm.then_inc(x_used, 1)

                turn_rows(0)
                w1_bias(0)
                for j in range(8):
                    w1_chunk(0, 0, j, j)
                turn_rows(1)
                w1_bias(1)
                for j in range(4):
                    w1_chunk(1, 1, -4 + j, j)
                turn_act(0)
                for j in range(4, 8):
                    w1_chunk(1, 1, -4 + j, j)
                turn_rows(2)
                with pe.Fori(2, n) as i:
                    w2_block(i - 2, i, -8)
                    w1_bias(i)
                    for j in range(4):
                        w1_chunk(i, i, -4 + j, j)
                    turn_act(i - 1)
                    for j in range(4, 8):
                        w1_chunk(i, i, -4 + j, j)
                    turn_rows(i + 1)
                w2_block(n - 2, n, -8)
                turn_last(pe, n)
                w2_block(n - 1, n, -4)

        yh_in = [sem(f"yh_in{s}") for s in range(2)]
        wfin_in = sem("wfin_in")
        y23_ready = sem("y23_ready")
        hsum_ready = sem("hsum_ready")
        fsq_ready = sem("fsq_ready")
        frms_ready = sem("frms_ready")
        out_ready = sem("out_ready")
        out_stored = [sem(f"out_stored{s}") for s in range(2)]
        dve6 = sem("dve6")

        with nc.Block() as block:
            @block.sync
            def _(sp):
                def store_out(sp, t):
                    sp.wait_ge(out_ready, t + 1)
                    sp.dma_start(out2[t * P:(t + 1) * P, :], h_out[:, t % 2, :]).then_inc(out_stored[t % 2], 16)

                sp.dma_start(wfin[:], norm_final_w.rearrange("(a n) -> a n", a=1).to_broadcast([P, D])).then_inc(wfin_in, 16)
                yv = y_d.rearrange("(t k) n -> t k n", k=TOP)
                for t in range(TT):
                    if t >= 2:
                        sp.wait_ge(hsum_ready, t - 1)
                    sp.dma_start(y_in[:, t % 2], yv[t * P:(t + 1) * P]).then_inc(yh_in[t % 2], 16)
                    sp.dma_start(h_in[:, t % 2, :], h2_d[t * P:(t + 1) * P, :]).then_inc(yh_in[t % 2], 16)
                    if t >= 1:
                        store_out(sp, t - 1)
                store_out(sp, TT - 1)
                for s in range(2):
                    sp.wait_ge(out_stored[s], 16 * TT // 2)

            @block.gpsimd
            def _(pool):
                for t in range(TT):
                    pool.wait_ge(yh_in[t % 2], 32 * (t // 2 + 1))
                    if t >= 2:
                        pool.wait_ge(hsum_ready, t - 1)
                    pool.tensor_tensor(y_23[:, t % 2, :], y_in[:, t % 2, 2, :], y_in[:, t % 2, 3, :],
                                       ALU.add).then_inc(y23_ready, 1)

            @block.scalar
            def _(act):
                for t in range(TT):
                    act.wait_ge(hsum_ready, t + 1)
                    if t >= 1:
                        act.wait_ge(fsq_ready, t)
                    act.activation(sq[:], h_out[:, t % 2, :], ACT.Square, scale=D ** -0.5,
                                   accum_out=ms[:, t:t + 1]).then_inc(fsq_ready, 1)
                    act.wait_ge(fsq_ready, t + 1)
                    act.activation(rstd[:, t:t + 1], ms[:, t:t + 1], ACT.Sqrt, bias=eps).then_inc(frms_ready, 1)

            @block.vector
            def _(dve):
                chain = Chain(dve, dve6)
                dve.wait_ge(wfin_in, 16)
                for t in range(TT):
                    s = t % 2
                    dve.wait_ge(yh_in[s], 32 * (t // 2 + 1))
                    chain(dve.tensor_tensor(y_01[:, s, :], y_in[:, s, 0, :], y_in[:, s, 1, :], ALU.add))
                    dve.wait_ge(y23_ready, t + 1)
                    chain(dve.tensor_tensor(y_01[:, s, :], y_01[:, s, :], y_23[:, s, :], ALU.add))
                    chain(dve.tensor_tensor(y_01[:, s, :], y_01[:, s, :], gate_f[:], ALU.mult))
                    if t >= 2:
                        dve.wait_ge(out_stored[t % 2], 16 * (t // 2))
                    dve.tensor_tensor(h_out[:, s, :], y_01[:, s, :], h_in[:, s, :], ALU.add).then_inc(hsum_ready, 1)
                    dve.wait_ge(frms_ready, t + 1)
                    chain(dve.reciprocal(rstd[:, t:t + 1], rstd[:, t:t + 1]))
                    dve.scalar_tensor_tensor(h_out[:, s, :], h_out[:, s, :], rstd[:, t:t + 1], wfin[:], ALU.mult,
                                             ALU.mult).then_inc(out_ready, 1)


_INS = ["x", "c", "w_ada", "b_ada", "norm_mix_w", "w_in", "hgrn_lower_bounds", "hgrn_norm_w", "conv_w", "w_hgrn_out",
        "w_conv_out", "w_mix_out", "norm_ffn_w", "w_router", "b_router", "w1", "b1", "w2", "b2", "norm_final_w"]


def kernel(**inputs):
    import concourse.bacc as _bacc
    from concourse.bass_utils import run_bass_kernel_spmd as _run

    nc = _bacc.Bacc("TRN2", target_bir_lowering=False, num_devices=1, dynamic_dma_scratch_size=4096)
    arrays = {"shape_constants": shape_constants(), "level_masks": level_masks()}
    for name in _INS:
        arrays[f"in_{name}"] = np.ascontiguousarray(inputs[name])
    args = [nc.dram_tensor(n, a.shape, mybir.dt.from_np(a.dtype), kind="ExternalInput").ap() for n, a in arrays.items()]
    out = nc.dram_tensor("layer_out", (1, TOKENS, D), F32, kind="ExternalOutput").ap()
    layer_kernel(nc, *args, out)
    r = _run(nc, [arrays], core_ids=[0])
    return r.results[0]["layer_out"]
```

```python
from contextlib import ExitStack

import numpy as np

import concourse.bass as bass
from concourse import mybir

F32 = mybir.dt.float32
F32R = mybir.dt.float32r
U32 = mybir.dt.uint32
I32 = mybir.dt.int32
U8 = mybir.dt.uint8
ALU = mybir.AluOpType
ACT = mybir.ActivationFunctionType
AX = mybir.AxisListType

P = 128
D = 1024
KD = D // P
TOKENS = 512
TT = TOKENS // P
HEADS = 4
HW = HEADS * P
LEVELS = 7
CONV_K = 3
E = 32
TOP = 4
FF = 1024
LIMIT = 7.0
ALPHA = 1.702
EPS = 1e-6
TINY = 1e-18
CH = 2048
SPLITS = 4
RAWS = 12
MAX_EXTRA = 16
MAX_BLOCKS = E + MAX_EXTRA
UNFILLED = 4096.0
KB = 1024

C_ID, C_ONE, C_TRI, C_IOTA, C_EYE2, C_ROW, C_PART, C_RESET = 0, 128, 256, 384, 512, 544, 576, 608
C_END = C_RESET + TOKENS


def shape_constants():
    c = np.zeros((P, C_END), np.float32)
    p = np.arange(P)
    c[:, C_ID:C_ID + P] = np.eye(P)
    c[:, C_ONE:C_ONE + P] = 1
    c[:, C_TRI:C_TRI + P] = p[:, None] < p[None, :]
    c[:, C_IOTA:C_IOTA + P] = p[None, :]
    c[:64, C_EYE2:C_EYE2 + E] = (p[:64, None] % E) == np.arange(E)[None, :]
    tok = np.arange(TT)[None, :, None] * P + p[:, None, None] + 0 * np.arange(TOP)[None, None, :]
    c[:, C_ROW:C_ROW + 16] = (tok * TOP + np.arange(TOP)).reshape(P, 16) - UNFILLED
    c[:, C_PART] = p
    c[:, C_PART + 1] = TOP * p
    c[:, C_RESET:C_RESET + TOKENS] = (np.arange(TOKENS) % P != 0)[None, :]
    return c


def level_masks():
    s, t = np.arange(P)[:, None], np.arange(P)[None, :]
    m = np.zeros((P, LEVELS, P), np.float32)
    for level in range(LEVELS):
        m[:, level] = ((s ^ t) >> level == 1) & (t > s)
    return m.reshape(P, LEVELS * P)


class Chain:

    def __init__(self, eng, sem, count):
        self.eng, self.sem, self.count = eng, sem, count

    def __call__(self, ins):
        ins.then_inc(self.sem, 1)
        self.count[0] += 1
        self.eng.wait_ge(self.sem, self.count[0])


def layer_kernel(nc, consts, masks, x, c, w_ada, b_ada, norm_mix_w, w_in, lower_bounds, hgrn_norm_w, conv_w,
                 w_hgrn_out, w_conv_out, w_mix_out, norm_ffn_w, w_router, b_router, w1, b1, w2, b2,
                 norm_final_w, out):
    x2 = x[0]
    out2 = out[0]
    u2_d = nc.dram_tensor("ffn_input", [TOKENS, D], F32, kind="Internal").ap()
    h2_d = nc.dram_tensor("residual", [TOKENS, D], F32, kind="Internal").ap()
    y_d = nc.dram_tensor("expert_rows", [TOKENS * TOP, D], F32, kind="Internal").ap()

    with ExitStack() as ctx:
        base = (nc.sbuf_base + 63) // 64 * 64

        def at(name, kb, shape, dt=F32):
            return nc.alloc_sbuf_tensor_at(name, shape, dt, offset=base + int(kb * KB))

        def sem(name):
            return ctx.enter_context(nc.semaphore(name))

        w_hi = at("w_hi", 0, [P, SPLITS, CH], F32R)
        w_lo = at("w_lo", 32, [P, SPLITS, CH], F32R)
        RAW = 64
        raw = at("raw", RAW, [P, RAWS, CH])
        stage_01 = at("stage_01", RAW, [P, 2, CH])
        ada0_in = at("ada0_in", 0, [P, KD, CH])
        uT_hi = at("uT_hi", RAW + 16, [P, KD, TOKENS], F32R)
        uT_lo = at("uT_lo", RAW + 32, [P, KD, TOKENS], F32R)
        M = RAW + 48
        merged_hi = at("merged_hi", M, [P, KD, TOKENS], F32R)
        merged_lo = at("merged_lo", M + 16, [P, KD, TOKENS], F32R)
        ada0 = at("ada0", M, [P, CH])
        wdiff = at("wdiff", M, [P, 2, HEADS, P])
        q_dec = at("q_dec", M + 4, [P, 2, HEADS, P])
        k_dec = at("k_dec", M + 8, [P, 2, HEADS, P])
        scores = at("scores", M + 12, [P, HEADS, P])
        state = at("state", M + 14, [P, HEADS, P])
        k_tok = at("k_tok", M + 16, [P, HEADS, P])
        o_norm = at("o_norm", M + 18, [P, HEADS, P])
        gates = at("gates", M + 20, [P, TT, HW])
        mask_f = at("mask_f", M + 20, [P, LEVELS * P])
        g_sig = at("g_sig", M + 28, [P, HW])
        y_tmp = at("y_tmp", M + 30, [P, TOKENS])
        yc_hi = at("yc_hi", RAW + 80, [P, HEADS, TOKENS], F32R)
        yc_lo = at("yc_lo", RAW + 88, [P, HEADS, TOKENS], F32R)
        cu = at("cu", RAW + 88, [P, HEADS, TOKENS])
        N = RAW + 96
        const = at("const", N, [P, C_RESET])
        ident = const[:, C_ID:C_ID + P]
        ones = const[:, C_ONE:C_ONE + P]
        tri = const[:, C_TRI:C_TRI + P]
        iota = const[:, C_IOTA:C_IOTA + P]
        S0 = N + 2.375
        small = at("small", S0, [P, 352])
        vecT = small[:, 0:28]
        modT = small[:, 28:44]
        lb = small[:, 44:48]
        om_lb = small[:, 48:52]
        cs = small[:, 52:60]
        rstd = small[:, 60:64]
        ms = small[:, 64:68]
        hms = small[:, 68:72]
        hrs = small[:, 72:76]
        elast = small[:, 76:80]
        lbt = small[:, 80:96]
        csig = small[:, 96:104]
        eps = small[:, 104:105]
        R0 = N + 3.75
        qT = at("qT", R0, [P, HEADS, TOKENS])
        kT = at("kT", R0 + 8, [P, HEADS, TOKENS])
        bT = at("bT", R0 + 16, [P, HEADS, TOKENS])
        v_tok = at("v_tok", R0 + 24, [P, TT, HW])
        x_in = at("x_in", R0, [P, TT, D])
        x_n = at("x_n", R0 + 16, [P, TT, D])
        oT_hi = at("oT_hi", R0 + 32, [P, HEADS, TOKENS], F32R)
        oT_lo = at("oT_lo", R0 + 40, [P, HEADS, TOKENS], F32R)
        u_full = at("u_full", R0, [P, KD, TOKENS])
        vec_rows = at("vec_rows", R0 + 36, [28, P])
        reset = at("reset", R0 + 40, [P, TOKENS])
        mask_sb = at("mask_sb", R0 + 48, [P, LEVELS, P], U8)
        nw_row = at("nw_row", R0 + 49, [P, P])
        stage_2 = at("stage_2", R0 + 48, [P, CH])
        ada12 = at("ada12", R0, [P, 2, CH])
        sg_a = at("sg_a", R0 + 16, [P, 4, TOKENS])
        sg_b = at("sg_b", R0 + 24, [P, 4, TOKENS])
        rows = at("rows", RAW + 80, [P, 3, D])
        gate_f = at("gate_f", R0 + 28, [P, D])
        x_t = at("x_t", R0 + 32, [P, 2, D])
        h2 = at("h2", R0 + 8, [P, 2, D])
        u2 = at("u2", R0, [P, 2, D])
        u2T = at("u2T", R0 + 40, [P, D])
        tmp_j = at("tmp_j", R0 + 44, [P, D])
        wr = at("wr", R0 + 52, [P, KD, E])
        br = at("br", R0 + 53, [1, E])
        wf_row = at("wf_row", RAW + 32, [P, D])
        b2_raw = at("b2_raw", RAW + 36, [P, D])
        b1_raw = at("b1_raw", RAW + 40, [P, 2 * FF])
        lg = at("lg", R0 + 32, [P, TT, E])
        val8 = at("val8", R0 + 32.5, [P, TT, 8])
        idx8 = at("idx8", R0 + 32.75, [P, TT, 8], U32)
        idxf = at("idxf", R0 + 33, [P, TT, 8])
        prob = at("prob", R0 + 33.25, [P, TT, TOP])
        psm = at("psm", R0 + 33.375, [P, TT])
        prc = at("prc", R0 + 33.4375, [P, TT])
        pos = at("pos", R0 + 33.5, [P, 16])
        blk = at("blk", R0 + 33.625, [P, 16])
        ge = at("ge", R0 + 33.75, [P, 3, 16])
        qcol = at("qcol", R0 + 33.9375, [P, 16])
        onehot = at("onehot", R0 + 34, [P, TT, TOP, E])
        chosen = at("chosen", R0 + 36, [P, TT, E])
        ohpos = at("ohpos", R0 + 36.5, [P, TT, TOP, E])
        slot_row = at("slot_row", R0 + 38.5, [P, 2, P])
        slot_col = at("slot_col", R0 + 39.5, [P, 2, 2, P])
        vv = at("vv", R0 + 42.5, [P, 2, 16])
        cnt = at("cnt", R0 + 42.75, [E, 8])
        mex = at("mex", R0 + 42.875, [E, 2, MAX_EXTRA])
        mtmp = at("mtmp", R0 + 43, [E, 2, MAX_EXTRA])
        btf = at("btf", R0 + 43.25, [1, 2 * MAX_BLOCKS + 16])
        bias1 = at("bias1", R0 + 16, [P, 2 * FF], F32R)
        bias2 = at("bias2", R0 + 24, [P, D], F32R)
        tabI = at("tabI", R0 + 12, [P, 2, P], U32)
        tabW = at("tabW", R0 + 13, [P, P])
        bt = at("bt", R0 + 13.5, [1, 2 * MAX_BLOCKS + 16], I32)
        sel1 = at("sel1", R0 + 14, [P, P], F32R)
        sel2 = at("sel2", R0 + 14.5, [P, P], F32R)
        cur_tok = at("cur_tok", R0 + 15, [P, 1], U32)
        cur_row = at("cur_row", R0 + 15.0625, [P, 1], U32)
        cur_w = at("cur_w", R0 + 15.125, [P, 1])
        spare = at("spare", R0 + 15.1875, [P, 1])
        hs = at("hs", R0 + 48, [P, D])
        hsT_hi = at("hsT_hi", R0, [P, KD, P], F32R)
        hsT_lo = at("hsT_lo", R0 + 4, [P, KD, P], F32R)
        glu = at("glu", R0 + 8, [P, FF])
        sig = at("sig", R0 + 32, [P, FF])
        lin = at("lin", R0 + 36, [P, FF])
        aT_hi = at("aT_hi", R0 + 40, [P, KD, P], F32R)
        aT_lo = at("aT_lo", R0 + 44, [P, KD, P], F32R)
        y_out = at("y_out", R0 + 52, [P, D])
        h_in = at("h_in", RAW, [P, TT, D])
        wfin = at("wfin", RAW + 16, [P, D])
        y_in = at("y_in", RAW + 32, [P, TT, TOP, D])
        y_01 = at("y_01", 0, [P, 2, D])
        y_23 = at("y_23", 8, [P, 2, D])
        h_out = at("h_out", 16, [P, TT, D])
        sq = at("sq", 32, [P, D])

        ps = ctx.enter_context(nc.psum_tensor("ps", [P, 8, 512], F32))

        consts_in = sem("consts_in")
        vec_in = sem("vec_in")
        c_in = sem("c_in")
        x_inn = [sem(f"x_in{t}") for t in range(TT)]
        ada_bias_in = sem("ada_bias_in")
        ada0_zero = sem("ada0_zero")
        ada_in = [sem(f"ada_in{k}") for k in range(KD)]
        ada0_used = sem("ada0_used")
        csig_ready = sem("csig_ready")
        vec_turned = sem("vec_turned")
        square_x = sem("square_x")
        sqrt_x = sem("sqrt_x")
        eps_set = sem("eps_set")
        xn_ready = sem("xn_ready")
        x_turned = sem("x_turned")
        mod_sum = sem("mod_sum")
        lb_exp_in = sem("lb_exp_in")
        lb_exp = sem("lb_exp")
        u_ready = sem("u_ready")
        u_hi_ready = sem("u_hi_ready")
        u_lo_ready = sem("u_lo_ready")
        dve_step = sem("dve_step")
        order = [0]
        masks_in = sem("masks_in")
        mask_f_in = sem("mask_f_in")
        mask_set = sem("mask_set")
        stage_in = [sem(f"stage_in{s}") for s in range(3)]

        def w_in_chunk(col, half):
            return w_in[0, half * 512:half * 512 + 512, col:col + 512].rearrange("(k p) n -> p k n", p=P)

        def out_chunk(w, row, col):
            return w[0, row:row + 512, col:col + 512].rearrange("(k p) n -> p k n", p=P)

        COL = {"q": 0, "f": 512, "v": 1024, "g": 1536, "cb": 2048, "cc": 2560, "ch": 3072,
               "ga0": 3584, "ga1": 4096, "gb0": 4608, "gb1": 5120}
        weight_chunks = []
        group_chunks = {}
        for name in ("f", "q", "v", "g", "cc", "ch", "cb", "ga0", "ya0", "gb0", "yb0", "ga1", "ya1", "gb1", "yb1",
                     "mix0", "mix1"):
            first = len(weight_chunks)
            if name in COL:
                weight_chunks += [w_in_chunk(COL[name], 0), w_in_chunk(COL[name], 1)]
            elif name[:2] == "ya":
                weight_chunks.append(out_chunk(w_hgrn_out, 0, 512 * int(name[2])))
            elif name[:2] == "yb":
                weight_chunks.append(out_chunk(w_conv_out, 0, 512 * int(name[2])))
            else:
                weight_chunks += [out_chunk(w_mix_out, 0, 512 * int(name[3])), out_chunk(w_mix_out, 512, 512 * int(name[3]))]
            group_chunks[name] = list(range(first, len(weight_chunks)))
        NW = len(weight_chunks)
        def refills(name):
            return [n + SPLITS for n in group_chunks[name] if n + SPLITS < NW]

        LATE = [("ga0", "ya0"), ("gb0", "yb0"), ("ga1", "ya1"), ("gb1", "yb1")]
        stream = [("w", n) for n in range(group_chunks["ga0"][0] + SPLITS)]
        for r, (gate, product) in enumerate(LATE):
            stream += [("ada", 4 * r + j) for j in range(3)]
            stream += [("w", n) for n in refills(gate)]
            stream += [("ada", 4 * r + 3)]
            stream += [("w", n) for n in refills(product)]
        where = {item: n for n, item in enumerate(stream)}
        THIRD_FROM = where["ada", 0]
        stage_of = [n % 2 if n < THIRD_FROM else (2, THIRD_FROM % 2, (THIRD_FROM + 1) % 2)[(n - THIRD_FROM) % 3]
                    for n in range(len(stream))]

        def staged(item):
            slot = stage_of[where[item]]
            return stage_2[:] if slot == 2 else stage_01[:, slot, :]

        ada_v = w_ada[0].rearrange("(p k) n -> p k n", k=KD)

        hi_done = sem("hi_done")
        lo_done = sem("lo_done")
        ada_scaled = sem("ada_scaled")
        ada_done = sem("ada_done")

        def stream_load(eng, n):
            earlier = [e for e in range(n) if stage_of[e] == stage_of[n]]
            if earlier:
                kind, m = stream[earlier[-1]]
                eng.wait_ge(lo_done if kind == "w" else ada_done, m + 1)
            kind, m = stream[n]
            dst = staged(stream[n])
            if kind == "w":
                eng.dma_start(dst.rearrange("p (k n) -> p k n", k=4), weight_chunks[m]).then_inc(stage_in[stage_of[n]], 16)
            else:
                eng.dma_start(dst, ada_v[:, m % KD, CH * (1 + m // KD):CH * (2 + m // KD)]).then_inc(
                    stage_in[stage_of[n]], 16)

        def wait_stage(eng, item):
            n = where[item]
            eng.wait_ge(stage_in[stage_of[n]], 16 * sum(slot == stage_of[n] for slot in stage_of[:n + 1]))

        with nc.Block() as block:
            @block.sync
            def _(sp):
                sp.dma_start(cs, c[0].rearrange("(p k) -> p k", k=KD)).then_inc(c_in, 16)
                for t in range(TT):
                    sp.dma_start(x_in[:, t, :], x2[t * P:(t + 1) * P, :]).then_inc(x_inn[t], 16)
                for k in range(KD):
                    sp.dma_start(ada0_in[:, k, :], ada_v[:, k, 0:CH]).then_inc(ada_in[k], 16)
                stream_load(sp, 0)
                stream_load(sp, 1)

            @block.gpsimd
            def _(pool):
                pool.memset(ada0[:], 0.0).then_inc(ada0_zero, 1)
                pool.memset(eps, EPS).then_inc(eps_set, 1)
                pool.wait_ge(mask_f_in, 16)
                pool.tensor_copy(mask_sb[:].rearrange("p l t -> p (l t)"), mask_f[:]).then_inc(mask_set, 1)
                for j in range(KD):
                    pool.wait_ge(u_hi_ready, j + 1)
                    pool.wait_ge(u_ready, j + 1)
                    pool.tensor_tensor(uT_lo[:, j, :], u_full[:, j, :], uT_hi[:, j, :].bitcast(F32),
                                       ALU.subtract).then_inc(u_lo_ready, 1)

            @block.scalar
            def _(act):
                act.dma_start(const[:], consts[:, 0:C_RESET]).then_inc(consts_in, 16)
                act.dma_start(vec_rows[0:8, :], norm_mix_w[0].rearrange("(j p) -> j p", p=P)).then_inc(vec_in, 16)
                act.dma_start(vec_rows[8:16, :], lower_bounds.rearrange("r (h p) -> (r h) p", p=P)).then_inc(vec_in, 16)
                act.dma_start(vec_rows[16:28, :], conv_w[0].rearrange("r (h p) -> (r h) p", p=P)).then_inc(vec_in, 16)
                act.wait_ge(ada0_zero, 1)
                act.dma_start(ada0[0:1, :], b_ada[:, 0:CH]).then_inc(ada_bias_in, 16)
                act.dma_start(reset[:], consts[:, C_RESET:C_END]).then_inc(masks_in, 16)
                act.dma_start(nw_row[:], hgrn_norm_w[0:1, :].to_broadcast([P, P])).then_inc(masks_in, 16)
                act.dma_start(mask_f[:], masks).then_inc(mask_f_in, 16)
                act.wait_ge(c_in, 16)
                act.activation(csig, cs, ACT.Sigmoid).then_inc(csig_ready, 1)
                for t in range(TT):
                    act.wait_ge(x_inn[t], 16)
                    act.activation(x_n[:, t, :], x_in[:, t, :], ACT.Square, scale=D ** -0.5,
                                   accum_out=ms[:, t:t + 1]).then_inc(square_x, 1)
                act.wait_ge(square_x, TT)
                act.wait_ge(eps_set, 1)
                act.activation(rstd, ms, ACT.Sqrt, bias=eps).then_inc(sqrt_x, 1)
                act.wait_ge(lb_exp_in, 1)
                act.activation(lbt[:, 0:8], lbt[:, 0:8], ACT.Exp).then_inc(lb_exp, 1)
                act.wait_ge(ada0_used, KD)
                for j in range(KD):
                    if j in (0, 4):
                        n = j // 4
                        wait_stage(act, ("w", n))
                        act.activation(w_hi[:, n, :], staged(("w", n)), ACT.Copy).then_inc(hi_done, 1)
                    act.wait_ge(u_ready, j + 1)
                    act.activation(uT_hi[:, j, :], u_full[:, j, :], ACT.Copy).then_inc(u_hi_ready, 1)

            @block.vector
            def _(dve):
                chain = Chain(dve, dve_step, order)
                dve.wait_ge(csig_ready, 1)
                chain(dve.tensor_tensor(cs, cs, csig, ALU.mult))
                dve.wait_ge(sqrt_x, 1)
                chain(dve.reciprocal(rstd, rstd))
                for t in range(TT):
                    dve.tensor_scalar(x_n[:, t, :], x_in[:, t, :], rstd[:, t:t + 1], None, ALU.mult).then_inc(xn_ready, 1)
                dve.wait_ge(vec_turned, 1)
                chain(dve.tensor_copy(vecT, ps[:, 7, 0:28]))
                chain(dve.tensor_tensor(lbt[:, 8:12], vecT[:, 8:12], vecT[:, 12:16], ALU.max))
                chain(dve.tensor_tensor(lbt[:, 0:4], vecT[:, 8:12], lbt[:, 8:12], ALU.subtract))
                dve.tensor_tensor(lbt[:, 4:8], vecT[:, 12:16], lbt[:, 8:12], ALU.subtract).then_inc(lb_exp_in, 1)
                dve.wait_ge(lb_exp, 1)
                chain(dve.tensor_tensor(lbt[:, 8:12], lbt[:, 0:4], lbt[:, 4:8], ALU.add))
                chain(dve.reciprocal(lbt[:, 12:16], lbt[:, 8:12]))
                chain(dve.tensor_tensor(lb, lbt[:, 0:4], lbt[:, 12:16], ALU.mult))
                chain(dve.tensor_tensor(om_lb, lbt[:, 4:8], lbt[:, 12:16], ALU.mult))
                chain(dve.tensor_scalar(lb, lb, TINY, None, ALU.max))
                dve.wait_ge(ada_bias_in, 16)
                for k in range(KD):
                    dve.wait_ge(ada_in[k], 16)
                    dve.scalar_tensor_tensor(ada0[:], ada0_in[:, k, :], cs[:, k:k + 1], ada0[:], ALU.mult,
                                             ALU.add).then_inc(ada0_used, 1)
                    dve.wait_ge(ada0_used, k + 1)
                for j in range(KD):
                    if j % 2 == 0:
                        dve.wait_ge(mod_sum, j // 2 + 1)
                        b = 6 + j // 2 % 2
                        dve.scalar_tensor_tensor(modT[:, j:j + 2], ps[:, b, 40 + j:42 + j], 1.0, vecT[:, j:j + 2],
                                                 ALU.add, ALU.mult)
                        chain(dve.tensor_copy(modT[:, 8 + j:10 + j], ps[:, b, 32 + j:34 + j]))
                    dve.wait_ge(x_turned, j + 1)
                    dve.tensor_scalar(u_full[:, j, :], ps[:, j % 6, :], modT[:, j:j + 1], modT[:, 8 + j:9 + j],
                                      ALU.mult, ALU.add).then_inc(u_ready, 1)
                for n in range(2):
                    dve.wait_ge(hi_done, n + 1)
                    dve.tensor_tensor(w_lo[:, n, :], staged(("w", n)), w_hi[:, n, :].bitcast(F32),
                                      ALU.subtract).then_inc(lo_done, 1)

            @block.tensor
            def _(pe):
                pe.wait_ge(consts_in, 16)
                pe.wait_ge(vec_in, 48)
                pe.transpose(ps[:, 7, 0:28], vec_rows[:], ident[0:28, 0:28]).then_inc(vec_turned, 1)
                pe.wait_ge(xn_ready, TT)

                def turn_x(j):
                    for t in range(TT):
                        mm = pe.transpose(ps[:, j % 6, t * P:(t + 1) * P], x_n[:, t, j * P:(j + 1) * P], ident)
                    mm.then_inc(x_turned, 1)

                for j in range(6):
                    turn_x(j)
                pe.wait_ge(ada0_used, KD)
                pe.wait_ge(dve_step, 3)
                for g in range(KD // 2):
                    if g >= 2:
                        pe.wait_ge(u_ready, 2 * g - 2)
                    for m in (2 * g, 2 * g + 1, KD + 2 * g, KD + 2 * g + 1):
                        mm = pe.matmul(ps[:, 6 + g % 2, 32 + m:33 + m], ada0[:, m * P:(m + 1) * P], ones[:, 0:1],
                                       start=True, stop=True, skip_group_check=True)
                    mm.then_inc(mod_sum, 1)
                    if g >= 2:
                        turn_x(4 + g)

        unit_done = sem("unit_done")
        act_read = sem("act_read")
        dve_read = sem("dve_read")
        sig_f = sem("sig_f")
        k_ready = sem("k_ready")
        logf_ready = sem("logf_ready")
        b_ready = sem("b_ready")
        gsig_ready = sem("gsig_ready")
        g_ready = sem("g_ready")
        elast_ready = sem("elast_ready")
        w_ready = sem("w_ready")
        e_ready = sem("e_ready")
        qd_ready = sem("qd_ready")
        kd_ready = sem("kd_ready")
        dec_used = sem("dec_used")
        diag_done = sem("diag_done")
        sc_read = sem("sc_read")
        ktok_ready = sem("ktok_ready")
        state_sum = sem("state_sum")
        state_ready = sem("state_ready")
        o_sq = sem("o_sq")
        o_ms = sem("o_ms")
        o_rms = sem("o_rms")
        o_ready = sem("o_ready")
        o_read = sem("o_read")
        o_turned = sem("o_turned")
        oT_hi_ready = sem("oT_hi_ready")
        oT_lo_ready = sem("oT_lo_ready")
        dec_zero = sem("dec_zero")
        yc_ready = sem("yc_ready")
        merged_ready = sem("merged_ready")
        ada12_in = sem("ada12_in")
        ada12_zero = sem("ada12_zero")

        units = []
        for name, owner in (("f", "act"), ("q", "act"), ("v", "act"), ("g", "dve"), ("cc", "act"), ("ch", "dve"),
                            ("cb", "dve"), ("ga0", "act"), ("ya0", "dve"), ("gb0", "act"), ("yb0", "dve"),
                            ("ga1", "act"), ("ya1", "dve"), ("gb1", "act"), ("yb1", "dve")):
            units += [(name, m, owner) for m in range(4)]
        unit_no = {(name, m): n for n, (name, m, _) in enumerate(units)}

        def bank(name, m):
            return ps[:, unit_no[name, m] % 3, :]

        def reads_upto(n):
            owner = units[n][2]
            return owner, sum(o == owner for _, _, o in units[:n + 1])

        def group_end(n):
            return next(unit_no[name, 3] + 1 for name, chunks in group_chunks.items() if n in chunks)

        def split_view(buf, n):
            return buf[:, n % SPLITS, :].rearrange("p (k n) -> p k n", k=4)

        def exact3(pe, dst, pairs, wait_for=None):
            n = len(pairs)
            for i, (sh, sl, mh, ml) in enumerate(pairs):
                if wait_for:
                    wait_for(i)
                pe.matmul(dst, sh, mh, start=(i == 0), stop=False)
                pe.matmul(dst, sh, ml, start=False, stop=False)
                mm = pe.matmul(dst, sl, mh, start=False, stop=(i == n - 1))
            return mm

        def half(ap, level, which):
            m = 1 << level
            v = ap.rearrange("p h (s two m) -> p h s two m", two=2, m=m)
            return v[:, :, :, which, :]

        def edge(ap, level):
            m = 1 << level
            v = ap.rearrange("p h (s two m) -> p h s two m", two=2, m=m)
            return v[:, :, :, 0, m - 1:m].to_broadcast([P, HEADS, P // (2 * m), m])

        mix_done = sem("mix_done")

        def mix_product(pe, t):
            for n in range(2):
                pairs = []
                for k in range(KD):
                    chunk = group_chunks[f"mix{n}"][k // 4]
                    pairs.append((merged_hi[:, k, t * P:(t + 1) * P], merged_lo[:, k, t * P:(t + 1) * P],
                                  split_view(w_hi, chunk)[:, k % 4, :], split_view(w_lo, chunk)[:, k % 4, :]))
                wait_k = None
                if t == 0:
                    def wait_k(k, n=n):
                        pe.wait_ge(merged_ready, k + 1)
                        pe.wait_ge(lo_done, group_chunks[f"mix{n}"][k // 4] + 1)
                mm = exact3(pe, ps[:, 4 + 2 * (t % 2) + n, :], pairs, wait_k)
            mm.then_inc(mix_done, 1)

        with nc.Block() as block:
            @block.sync
            def _(sp):
                for n in range(2, len(stream)):
                    if n == THIRD_FROM:
                        sp.wait_ge(sc_read, 8 * TT)
                        sp.wait_ge(g_ready, TT)
                    stream_load(sp, n)

            @block.gpsimd
            def _(pool):
                pool.memset(q_dec[:], 0.0).then_inc(dec_zero, 1)
                pool.memset(k_dec[:], 0.0).then_inc(dec_zero, 1)
                pool.wait_ge(k_ready, HEADS)
                pool.wait_ge(masks_in, 32)
                for t in range(TT):
                    for level in range(LEVELS + 1):
                        n = 9 * t + level
                        pool.wait_ge(e_ready, n + 1)
                        if n >= 2:
                            pool.wait_ge(dec_used, n - 1)
                        kk = kT[:, :, t * P:(t + 1) * P]
                        if n < 2:
                            pool.wait_ge(dec_zero, 2)
                        if level < LEVELS:
                            pool.tensor_tensor(half(k_dec[:, n % 2], level, 0), half(kk, level, 0),
                                               half(wdiff[:, n % 2], level, 0), ALU.mult).then_inc(kd_ready, 1)
                        else:
                            pool.tensor_tensor(k_dec[:, n % 2], kk, wdiff[:, n % 2], ALU.mult).then_inc(kd_ready, 1)
                    if t < 2:
                        for m in (0,) if t == 0 else (1, 2, 3):
                            pool.wait_ge(dve_read, m + 1)
                            v = gates[:, m, :].rearrange("p (h d) -> p h d", h=HEADS)
                            pool.tensor_tensor(v, v, nw_row[:, None, :].to_broadcast([P, HEADS, P]),
                                               ALU.mult).then_inc(g_ready, 1)
                pool.wait_ge(oT_lo_ready, TT)
                pool.memset(ada12[:], 0.0).then_inc(ada12_zero, 1)
                pool.wait_ge(ada12_zero, 1)
                pool.dma_start(ada12[0:1, :, :].rearrange("p a n -> p (a n)"), b_ada[:, CH:3 * CH]).then_inc(ada12_in, 16)
                pool.wait_ge(ada12_in, 16)
                for m in range(2 * KD):
                    pool.wait_ge(ada_scaled, m + 1)
                    if m >= 1:
                        pool.wait_ge(ada_done, m)
                    pool.tensor_tensor(ada12[:, m // KD, :], staged(("ada", m)), ada12[:, m // KD, :],
                                       ALU.add).then_inc(ada_done, 1)

            @block.scalar
            def _(act):

                def scale_ada(m):
                    wait_stage(act, ("ada", m))
                    act.activation(staged(("ada", m)), staged(("ada", m)), ACT.Copy,
                                   scale=cs[:, m % KD:m % KD + 1]).then_inc(ada_scaled, 1)

                def split_hi(n):
                    wait_stage(act, ("w", n))
                    if n >= SPLITS:
                        act.wait_ge(unit_done, group_end(n - SPLITS))
                    act.activation(w_hi[:, n % SPLITS, :], staged(("w", n)), ACT.Copy).then_inc(hi_done, 1)

                def unit(name, m):
                    act.wait_ge(unit_done, unit_no[name, m] + 1)

                def decay(n):
                    t, level = n // 9, n % 9
                    if level == 8:
                        act.wait_ge(kd_ready, 8 * t + 7)
                        act.wait_ge(qd_ready, 8 * t + 7)
                        act.activation(wdiff[:, n % 2], bT[:, :, t * P:(t + 1) * P], ACT.Exp).then_inc(e_ready, 1)
                    else:
                        act.wait_ge(w_ready, 8 * t + level + 1)
                        act.activation(wdiff[:, n % 2], wdiff[:, n % 2], ACT.Exp).then_inc(e_ready, 1)

                for n in range(2, SPLITS):
                    split_hi(n)
                for m in range(HEADS):
                    unit("f", m)
                    act.activation(bT[:, m, :], bank("f", m), ACT.Sigmoid).then_inc(sig_f, 1)
                    act.activation(kT[:, m, :], bank("f", m), ACT.Sigmoid, scale=-1.0).then_inc(act_read, 1)
                for n in refills("f"):
                    split_hi(n)
                for m in range(HEADS):
                    act.wait_ge(sig_f, m + 1)
                    act.activation(bT[:, m, :], bT[:, m, :], ACT.Ln, bias=lb[:, m:m + 1],
                                   scale=om_lb[:, m:m + 1]).then_inc(logf_ready, 1)
                for m in range(HEADS):
                    unit("q", m)
                    act.activation(qT[:, m, :], bank("q", m), ACT.Copy).then_inc(act_read, 1)
                for n in refills("q"):
                    split_hi(n)
                for m in range(TT):
                    unit("v", m)
                    act.activation(v_tok[:, m, :], bank("v", m), ACT.Copy).then_inc(act_read, 1)
                for n in refills("v"):
                    split_hi(n)
                def output_hi(t):
                    act.wait_ge(o_turned, t + 1)
                    act.activation(oT_hi[:, :, t * P:(t + 1) * P], ps[:, 5, :].rearrange("p (h t) -> p h t", h=HEADS),
                                   ACT.Copy).then_inc(oT_hi_ready, 1)

                act.wait_ge(b_ready, HEADS)
                decay(0)
                decay(1)
                for t, name in enumerate(("g", "cc", "ch", "cb")):
                    def filler(m):
                        if name == "g":
                            unit("g", m)
                            if m >= 1:
                                act.wait_ge(dve_read, m)
                            act.activation(g_sig[:], bank("g", m), ACT.Sigmoid).then_inc(gsig_ready, 1)
                        if name == "cc":
                            unit("cc", m)
                            act.activation(cu[:, m, :], bank("cc", m), ACT.Copy).then_inc(act_read, 1)
                    if t >= 1:
                        act.wait_ge(state_ready, t)
                    act.activation(elast, bT[:, :, t * P + P - 1:t * P + P].rearrange("p h o -> p (h o)"),
                                   ACT.Exp).then_inc(elast_ready, 1)
                    if t >= 1:
                        output_hi(t - 1)
                    decay(9 * t + 2)
                    filler(0)
                    for n in (3, 4, 5):
                        decay(9 * t + n)
                    filler(1)
                    for n in (6, 7, 8):
                        decay(9 * t + n)
                    filler(2)
                    act.wait_ge(dec_used, 9 * t + 8)
                    if t >= 1:
                        act.wait_ge(state_sum, t)
                    act.activation(k_tok[:].rearrange("p h d -> p (h d)"), ps[:, 5, :], ACT.Copy).then_inc(ktok_ready, 1)
                    act.wait_ge(dec_used, 9 * t + 9)
                    if t >= 1:
                        act.wait_ge(o_turned, t)
                    act.activation(o_norm[:].rearrange("p h d -> p (h d)"), ps[:, 6, :], ACT.Square,
                                   scale=P ** -0.5).then_inc(o_sq, 1)
                    if t < TT - 1:
                        decay(9 * t + 9)
                    act.wait_ge(o_ms, t + 1)
                    act.activation(hrs, hms, ACT.Sqrt, bias=eps).then_inc(o_rms, 1)
                    if t < TT - 1:
                        decay(9 * t + 10)
                    filler(3)
                    for n in refills(name):
                        split_hi(n)
                output_hi(TT - 1)
                act.wait_ge(oT_lo_ready, TT)
                for r, (gate, product) in enumerate(LATE):
                    sg = sg_a if r % 2 == 0 else sg_b
                    for m in range(4):
                        unit(gate, m)
                        if r >= 2:
                            act.wait_ge(merged_ready, m + 1)
                        act.activation(sg[:, m, :], bank(gate, m), ACT.Sigmoid).then_inc(act_read, 1)
                        if m < 3:
                            scale_ada(4 * r + m)
                    for n in refills(gate):
                        split_hi(n)
                    scale_ada(4 * r + 3)
                    for n in refills(product):
                        split_hi(n)

            @block.vector
            def _(dve):
                chain = Chain(dve, dve_step, order)

                def split_lo(n):
                    dve.wait_ge(hi_done, n + 1)
                    dve.tensor_tensor(w_lo[:, n % SPLITS, :], staged(("w", n)),
                                      w_hi[:, n % SPLITS, :].bitcast(F32), ALU.subtract).then_inc(lo_done, 1)

                def unit(name, m):
                    dve.wait_ge(unit_done, unit_no[name, m] + 1)

                for n in range(2, SPLITS):
                    split_lo(n)
                dve.wait_ge(masks_in, 32)
                dve.wait_ge(mask_set, 1)
                for m in range(HEADS):
                    dve.wait_ge(act_read, m + 1)
                    dve.tensor_scalar(kT[:, m, :], kT[:, m, :], om_lb[:, m:m + 1], None, ALU.mult).then_inc(k_ready, 1)
                for n in refills("f"):
                    split_lo(n)
                for m in range(HEADS):
                    dve.wait_ge(logf_ready, m + 1)
                    dve.tensor_tensor_scan(bT[:, m, :], reset[:], bT[:, m, :], 0.0, ALU.mult, ALU.add).then_inc(b_ready, 1)
                for n in refills("q"):
                    split_lo(n)
                for n in refills("v"):
                    split_lo(n)
                dve.wait_ge(b_ready, HEADS)
                dve.wait_ge(act_read, 3 * HEADS)
                dve.wait_ge(dec_zero, 2)

                def diff(t, level):
                    n = 9 * t + level
                    if n >= 2:
                        p = 9 * t + level - 2
                        dve.wait_ge(qd_ready, sum(x % 9 != 7 for x in range(p + 1)))
                        dve.wait_ge(kd_ready, sum(x % 9 != 8 for x in range(p + 1)))
                    b = bT[:, :, t * P:(t + 1) * P]
                    w = wdiff[:, n % 2]
                    if level < LEVELS:
                        chain(dve.tensor_tensor(half(w, level, 1), half(b, level, 1), edge(b, level), ALU.subtract))
                        dve.tensor_tensor(half(w, level, 0), edge(b, level), half(b, level, 0),
                                          ALU.subtract).then_inc(w_ready, 1)
                    else:
                        dve.tensor_tensor(w, b[:, :, P - 1:P].to_broadcast([P, HEADS, P]), b,
                                          ALU.subtract).then_inc(w_ready, 1)

                def q_decay(t, level):
                    n = 9 * t + level
                    dve.wait_ge(e_ready, n + 1)
                    if n >= 2:
                        dve.wait_ge(dec_used, n - 1)
                    qq = qT[:, :, t * P:(t + 1) * P]
                    if level < LEVELS:
                        dve.tensor_tensor(half(q_dec[:, n % 2], level, 1), half(qq, level, 1),
                                          half(wdiff[:, n % 2], level, 1), ALU.mult).then_inc(qd_ready, 1)
                    else:
                        dve.tensor_tensor(q_dec[:, n % 2], qq, wdiff[:, n % 2], ALU.mult).then_inc(qd_ready, 1)

                def take_scores(t, level):
                    dve.wait_ge(dec_used, 9 * t + level + 1)
                    dve.wait_ge(sc_read, 8 * t + level + 1)
                    b = 3 + (8 * t + level + 1) % 2
                    dve.copy_predicated(scores[:], mask_sb[:, level, None, :].to_broadcast([P, HEADS, P]),
                                        ps[:, b, :].rearrange("p (h t) -> p h t", h=HEADS)).then_inc(sc_read, 1)

                def output_lo(t):
                    dve.wait_ge(oT_hi_ready, t + 1)
                    dve.tensor_tensor(oT_lo[:, :, t * P:(t + 1) * P], ps[:, 5, :].rearrange("p (h t) -> p h t", h=HEADS),
                                      oT_hi[:, :, t * P:(t + 1) * P].bitcast(F32), ALU.subtract).then_inc(oT_lo_ready, 1)

                for t, name in enumerate(("g", "cc", "ch", "cb")):
                    def filler(m):
                        if name == "g":
                            unit("g", m)
                            dve.wait_ge(gsig_ready, m + 1)
                            dve.tensor_tensor(gates[:, m, :], bank("g", m), g_sig[:], ALU.mult).then_inc(dve_read, 1)
                        if name == "ch":
                            unit("ch", m)
                            dve.tensor_tensor(cu[:, m, :], bank("ch", m), cu[:, m, :], ALU.mult).then_inc(dve_read, 1)
                        if name == "cb":
                            tap = lambda k: vecT[:, 16 + 4 * k + m:17 + 4 * k + m]
                            dve.wait_ge(dve_read, 8 + m)
                            chain(dve.tensor_scalar(y_tmp[:], cu[:, m, :], tap(2), None, ALU.mult))
                            chain(dve.scalar_tensor_tensor(y_tmp[:, 1:], cu[:, m, 0:TOKENS - 1], tap(1), y_tmp[:, 1:],
                                                           ALU.mult, ALU.add))
                            chain(dve.scalar_tensor_tensor(y_tmp[:, 2:], cu[:, m, 0:TOKENS - 2], tap(0), y_tmp[:, 2:],
                                                           ALU.mult, ALU.add))
                            unit("cb", m)
                            dve.tensor_tensor(y_tmp[:], y_tmp[:], bank("cb", m), ALU.mult).then_inc(dve_read, 1)
                            dve.wait_ge(dve_read, 9 + m)
                            chain(dve.tensor_copy(yc_hi[:, m, :], y_tmp[:]))
                            dve.tensor_tensor(yc_lo[:, m, :], y_tmp[:], yc_hi[:, m, :].bitcast(F32),
                                              ALU.subtract).then_inc(yc_ready, 1)
                            dve.wait_ge(yc_ready, m + 1)
                    if t == 0:
                        diff(t, 0)
                        diff(t, 1)
                    dve.wait_ge(diag_done, t + 1)
                    if t >= 1:
                        dve.wait_ge(dec_used, 9 * t)
                    dve.tensor_tensor(scores[:], ps[:, 3 + (8 * t) % 2, :].rearrange("p (h t) -> p h t", h=HEADS),
                                      ident[:, None, :].to_broadcast([P, HEADS, P]), ALU.mult).then_inc(sc_read, 1)
                    q_decay(t, 0)
                    for level in range(2, 8):
                        diff(t, level)
                        q_decay(t, level - 1)
                        take_scores(t, level - 2)
                        if level == 2 and t >= 1:
                            output_lo(t - 1)
                        if level in (3, 5, 7):
                            filler(level // 2 - 1)
                    q_decay(t, 8)
                    take_scores(t, 6)
                    if t < TT - 1:
                        diff(t + 1, 0)
                        diff(t + 1, 1)
                    dve.wait_ge(o_sq, t + 1)
                    dve.tensor_reduce(hms, o_norm[:], AX.X, ALU.add).then_inc(o_ms, 1)
                    dve.wait_ge(g_ready, t + 1)
                    dve.wait_ge(o_ms, t + 1)
                    dve.tensor_tensor(o_norm[:].rearrange("p h d -> p (h d)"), ps[:, 6, :], gates[:, t, :],
                                      ALU.mult).then_inc(o_read, 1)
                    dve.wait_ge(o_rms, t + 1)
                    chain(dve.reciprocal(hrs, hrs))
                    dve.wait_ge(o_read, t + 1)
                    dve.tensor_tensor(o_norm[:], o_norm[:], hrs[:, :, None].to_broadcast([P, HEADS, P]),
                                      ALU.mult).then_inc(o_ready, 1)
                    if t < TT - 1:
                        dve.wait_ge(state_sum, t + 1)
                        dve.wait_ge(elast_ready, t + 1)
                        for h in range(HEADS):
                            src = ps[:, 7, h * P:(h + 1) * P]
                            if t == 0:
                                ins = dve.tensor_copy(state[:, h, :], src)
                            else:
                                ins = dve.scalar_tensor_tensor(state[:, h, :], state[:, h, :], elast[:, h:h + 1], src,
                                                               ALU.mult, ALU.add)
                        ins.then_inc(state_ready, 1)
                    filler(3)
                    for n in refills(name):
                        split_lo(n)
                output_lo(TT - 1)
                for r, (gate, product) in enumerate(LATE):
                    first, *second = refills(gate)
                    split_lo(first)
                    for m in range(4):
                        unit(product, m)
                        reads = reads_upto(unit_no[product, m])[1]
                        if r % 2 == 0:
                            dve.tensor_tensor(sg_a[:, m, :], bank(product, m), sg_a[:, m, :],
                                              ALU.mult).then_inc(dve_read, 1)
                        else:
                            j = 4 * (r // 2) + m
                            dve.tensor_tensor(sg_b[:, m, :], bank(product, m), sg_b[:, m, :],
                                              ALU.mult).then_inc(dve_read, 1)
                            dve.wait_ge(dve_read, reads)
                            chain(dve.tensor_tensor(sg_b[:, m, :], sg_b[:, m, :], sg_a[:, m, :], ALU.add))
                            chain(dve.tensor_copy(merged_hi[:, j, :], sg_b[:, m, :]))
                            dve.tensor_tensor(merged_lo[:, j, :], sg_b[:, m, :], merged_hi[:, j, :].bitcast(F32),
                                              ALU.subtract).then_inc(merged_ready, 1)
                        if m == 0:
                            for n in second:
                                split_lo(n)
                    for n in refills(product):
                        split_lo(n)

            @block.tensor
            def _(pe):
                def begin(name, m):
                    n = unit_no[name, m]
                    if n >= 3:
                        owner, reads = reads_upto(n - 3)
                        pe.wait_ge(act_read if owner == "act" else dve_read, reads)

                def part(name, m, ks):
                    chunks = group_chunks[name]
                    n = unit_no[name, m]
                    dst = bank(name, m)
                    for k in ks:
                        if m == 0:
                            pe.wait_ge(lo_done, chunks[k // 4] + 1)
                        wh = split_view(w_hi, chunks[k // 4])[:, k % 4, :]
                        wl = split_view(w_lo, chunks[k // 4])[:, k % 4, :]
                        first, last = k == 0, k == KD - 1
                        if name in ("v", "g"):
                            sh, sl = uT_hi[:, k, m * P:(m + 1) * P], uT_lo[:, k, m * P:(m + 1) * P]
                            mh, ml = wh, wl
                        else:
                            sh, sl = wh[:, m * P:(m + 1) * P], wl[:, m * P:(m + 1) * P]
                            mh, ml = uT_hi[:, k, :], uT_lo[:, k, :]
                        pe.matmul(dst, sh, mh, start=first, stop=False)
                        pe.matmul(dst, sh, ml, start=False, stop=False)
                        mm = pe.matmul(dst, sl, mh, start=False, stop=last)
                    if ks[-1] == KD - 1:
                        mm.then_inc(unit_done, 1)

                def group(name, last_output=None):
                    for m in range(4):
                        begin(name, m)
                        part(name, m, range(KD))
                        if m == 0 and last_output:
                            last_output(TT - 1)

                def narrow_group(name, hi, lo):
                    chunk = group_chunks[name][0]
                    pe.wait_ge(lo_done, chunk + 1)
                    for m in range(4):
                        begin(name, m)
                        pairs = [(split_view(w_hi, chunk)[:, k, m * P:(m + 1) * P],
                                  split_view(w_lo, chunk)[:, k, m * P:(m + 1) * P], hi[:, k, :], lo[:, k, :])
                                 for k in range(4)]
                        exact3(pe, bank(name, m), pairs).then_inc(unit_done, 1)

                def diagonal(t):
                    i = 8 * t
                    if i >= 2:
                        pe.wait_ge(sc_read, i - 1)
                    for h in range(HEADS):
                        mm = pe.matmul(ps[:, 3 + i % 2, h * P:(h + 1) * P], kT[:, h, t * P:(t + 1) * P],
                                       qT[:, h, t * P:(t + 1) * P], start=(h == 0), stop=True, skip_group_check=True)
                    mm.then_inc(diag_done, 1)

                def step(t, level):
                    n = 9 * t + level
                    pe.wait_ge(kd_ready, sum(v % 9 != 8 for v in range(n + 1)))
                    pe.wait_ge(qd_ready, sum(v % 9 != 7 for v in range(n + 1)))
                    i = 8 * t + level + 1
                    if level < LEVELS:
                        pe.wait_ge(sc_read, i - 1)
                        for h in range(HEADS):
                            mm = pe.matmul(ps[:, 3 + i % 2, h * P:(h + 1) * P], k_dec[:, n % 2, h, :],
                                           q_dec[:, n % 2, h, :], start=(h == 0), stop=True, skip_group_check=True)
                    elif level == 7:
                        if t >= 1:
                            pe.wait_ge(oT_lo_ready, t)
                        for h in range(HEADS):
                            mm = pe.transpose(ps[:, 5, h * P:(h + 1) * P], k_dec[:, n % 2, h, :], ident)
                    else:
                        pe.wait_ge(sc_read, 8 * (t + 1))
                        if t >= 1:
                            pe.wait_ge(o_read, t)
                            pe.wait_ge(state_ready, t)
                        for h in range(HEADS):
                            dst = ps[:, 6, h * P:(h + 1) * P]
                            mm = pe.matmul(dst, scores[:, h, :], v_tok[:, t, h * P:(h + 1) * P], start=(h == 0),
                                           stop=(t == 0), skip_group_check=True)
                            if t >= 1:
                                mm = pe.matmul(dst, q_dec[:, n % 2, h, :], state[:, h, :], start=False, stop=True,
                                               skip_group_check=True)
                    mm.then_inc(dec_used, 1)

                def new_state(t):
                    pe.wait_ge(ktok_ready, t + 1)
                    if t >= 1:
                        pe.wait_ge(state_ready, t)
                    for h in range(HEADS):
                        mm = pe.matmul(ps[:, 7, h * P:(h + 1) * P], k_tok[:, h, :], v_tok[:, t, h * P:(h + 1) * P],
                                       start=(h == 0), stop=True, skip_group_check=True)
                    mm.then_inc(state_sum, 1)

                def turn_output(t):
                    pe.wait_ge(o_ready, t + 1)
                    pe.wait_ge(ktok_ready, t + 1)
                    for h in range(HEADS):
                        mm = pe.transpose(ps[:, 5, h * P:(h + 1) * P], o_norm[:, h, :], ident)
                    mm.then_inc(o_turned, 1)

                group("f")
                group("q")
                group("v")
                pe.wait_ge(k_ready, HEADS)
                pe.wait_ge(act_read, 3 * HEADS)
                for t, name in enumerate(("g", "cc", "ch", "cb")):
                    for m in range(4):
                        begin(name, m)
                        part(name, m, range(0, 3))
                        if m == 0:
                            diagonal(t)
                        elif m == 3:
                            step(t, 8)
                        else:
                            step(t, 3 * m - 1)
                        part(name, m, range(3, 6))
                        if m == 0 and t >= 1:
                            turn_output(t - 1)
                        if m == 3:
                            new_state(t)
                        else:
                            step(t, 3 * m)
                        part(name, m, range(6, 8))
                        if m < 3:
                            step(t, 3 * m + 1)
                for h in range(2):
                    group(f"ga{h}", turn_output if h == 0 else None)
                    pe.wait_ge(oT_lo_ready, TT)
                    narrow_group(f"ya{h}", oT_hi, oT_lo)
                    group(f"gb{h}")
                    pe.wait_ge(yc_ready, 4)
                    narrow_group(f"yb{h}", yc_hi, yc_lo)
                for t in range(2):
                    mix_product(pe, t)

        bias_in = sem("bias_in")
        bias_zero = sem("bias_zero")
        bias_ready = sem("bias_ready")
        raw_in = [sem(f"raw_in{s}") for s in range(RAWS)]
        x_hi_done = sem("x_hi_done")
        x_lo_012 = sem("x_lo_012")
        x_lo_3 = sem("x_lo_3")
        x_used = sem("x_used")

        def known(v):
            return type(v) is int

        def lo_wait(eng, i, off):
            quad = 3 * i + off // 4
            if off % 4 == 3:
                eng.wait_ge(x_lo_3, quad + 1)
            else:
                eng.wait_ge(x_lo_012, 3 * quad + off % 4 + 1)

        def expert_load(eng, i, off, expert, part, j):
            if not known(i) or 12 * i + off >= RAWS:
                lo_wait(eng, i, off - RAWS)
            slot = off % RAWS
            one = bass.ds(expert, 1)
            if part == "w1":
                src = w1[0, one, j * P:(j + 1) * P, :].rearrange("e p n -> p (e n)")
                dst = raw[:, slot, :]
            else:
                src = w2[0, one, 2 * j * P:2 * (j + 1) * P, :].rearrange("e (k p) n -> p (e k) n", p=P)
                dst = raw[:, slot, :].rearrange("p (k n) -> p k n", k=2)
            eng.dma_start(dst, src).then_inc(raw_in[slot], 16)

        row_sum = sem("row_sum")
        row_ready_a = sem("row_ready_a")
        row_ready_v = sem("row_ready_v")
        wf_in = sem("wf_in")
        wr_in = sem("wr_in")
        xt_in = [sem(f"xt_in{s}") for s in range(2)]
        mix_read = sem("mix_read")
        h2_ready = sem("h2_ready")
        h2_sq = sem("h2_sq")
        h2_rms = sem("h2_rms")
        u2_ready = sem("u2_ready")
        u2_turned = sem("u2_turned")
        u2T_ready = sem("u2T_ready")
        routed = sem("routed")
        stored_h = [sem(f"stored_h{s}") for s in range(2)]
        stored_u = [sem(f"stored_u{s}") for s in range(2)]

        with nc.Block() as block:
            @block.sync
            def _(sp):
                def store(sp, t):
                    sp.wait_ge(h2_ready, t + 1)
                    sp.dma_start(h2_d[t * P:(t + 1) * P, :], h2[:, t % 2, :]).then_inc(stored_h[t % 2], 16)
                    sp.wait_ge(u2_ready, t + 1)
                    sp.dma_start(u2_d[t * P:(t + 1) * P, :], u2[:, t % 2, :]).then_inc(stored_u[t % 2], 16)

                sp.dma_start(wf_row[:], norm_ffn_w[0:1, :].to_broadcast([P, D])).then_inc(wf_in, 16)
                sp.dma_start(wr[:], w_router[0].rearrange("(k p) e -> p k e", p=P)).then_inc(wr_in, 16)
                sp.dma_start(br[:], b_router).then_inc(wr_in, 16)
                for t in range(2):
                    sp.dma_start(x_t[:, t, :], x2[t * P:(t + 1) * P, :]).then_inc(xt_in[t], 16)
                for j in range(4):
                    expert_load(sp, 0, j, 0, "w1", j)
                for t in range(2, TT):
                    sp.wait_ge(h2_ready, t - 1)
                    sp.dma_start(x_t[:, t % 2, :], x2[t * P:(t + 1) * P, :]).then_inc(xt_in[t % 2], 16)
                    store(sp, t - 2)
                store(sp, TT - 2)
                sp.wait_ge(row_ready_v, 1)
                sp.wait_ge(bias_ready, 2)
                for j in range(4, 6):
                    expert_load(sp, 0, j, 0, "w1", j)
                sp.wait_ge(mix_done, TT)
                for j in range(6, 8):
                    expert_load(sp, 0, j, 0, "w1", j)
                for j in range(2):
                    expert_load(sp, 1, -4 + j, 1, "w1", j)
                store(sp, TT - 1)


            @block.gpsimd
            def _(pool):
                for half_ in range(2):
                    pool.dma_start(b1_raw[32 * half_:32 * half_ + E, :], b1[0]).then_inc(bias_in, 16)
                    pool.dma_start(b2_raw[32 * half_:32 * half_ + E, :], b2[0]).then_inc(bias_in, 16)
                pool.memset(bias1[64:P, :].bitcast(F32), 0.0).then_inc(bias_zero, 1)
                pool.memset(bias2[64:P, :].bitcast(F32), 0.0).then_inc(bias_zero, 1)
                pool.wait_ge(bias_in, 64)
                pool.tensor_copy(bias1[0:64, :], b1_raw[0:64, :]).then_inc(bias_zero, 1)
                pool.tensor_copy(bias2[0:64, :], b2_raw[0:64, :]).then_inc(bias_zero, 1)
                pool.wait_ge(bias_zero, 4)
                pool.tensor_tensor(bias1[32:64, :], b1_raw[32:64, :], bias1[32:64, :].bitcast(F32),
                                   ALU.subtract).then_inc(bias_ready, 1)
                pool.tensor_tensor(bias2[32:64, :], b2_raw[32:64, :], bias2[32:64, :].bitcast(F32),
                                   ALU.subtract).then_inc(bias_ready, 1)
                pool.wait_ge(bias_ready, 2)
                pool.memset(hs[:], 0.0).then_inc(bias_ready, 1)

            @block.scalar
            def _(act):
                for r in (0, 1, 3):
                    act.wait_ge(row_sum, r + 1)
                    b = 2 * (r % 2)
                    act.activation(gate_f[:] if r == 3 else rows[:, r, :], ps[:, b:b + 2, :].rearrange("p b n -> p (b n)"),
                                   ACT.Copy).then_inc(row_ready_a, 1)
                for t in range(TT):
                    act.wait_ge(h2_ready, t + 1)
                    if t >= 1:
                        act.wait_ge(u2_ready, t)
                    act.activation(tmp_j[:], h2[:, t % 2, :], ACT.Square, scale=D ** -0.5,
                                   accum_out=ms[:, t:t + 1]).then_inc(h2_sq, 1)
                    act.wait_ge(h2_sq, t + 1)
                    act.activation(rstd[:, t:t + 1], ms[:, t:t + 1], ACT.Sqrt, bias=eps).then_inc(h2_rms, 1)
                    act.wait_ge(u2_turned, t + 1)
                    if t >= 1:
                        act.wait_ge(routed, t)
                    act.activation(u2T[:], ps[:, 0:2, :].rearrange("p b n -> p (b n)"), ACT.Copy).then_inc(u2T_ready, 1)

            @block.vector
            def _(dve):
                chain = Chain(dve, dve_step, order)
                dve.wait_ge(row_sum, 3)
                dve.wait_ge(wf_in, 16)
                dve.scalar_tensor_tensor(rows[:, 2, :], ps[:, 0:2, :].rearrange("p b n -> p (b n)"), 1.0, wf_row[:],
                                         ALU.add, ALU.mult).then_inc(row_ready_v, 1)
                dve.wait_ge(row_ready_v, 1)
                dve.wait_ge(row_ready_a, 2)
                for t in range(TT):
                    b = 4 + 2 * (t % 2)
                    dve.wait_ge(mix_done, t + 1)
                    if t >= 2:
                        dve.wait_ge(stored_h[t % 2], 16 * (t // 2))
                        dve.wait_ge(stored_u[t % 2], 16 * (t // 2))
                        dve.wait_ge(u2_turned, t - 1)
                    dve.tensor_tensor(h2[:, t % 2, :], ps[:, b:b + 2, :].rearrange("p b n -> p (b n)"), rows[:, 0, :],
                                      ALU.mult).then_inc(mix_read, 1)
                    dve.wait_ge(mix_read, t + 1)
                    dve.wait_ge(xt_in[t % 2], 16 * (t // 2 + 1))
                    dve.tensor_tensor(h2[:, t % 2, :], h2[:, t % 2, :], x_t[:, t % 2, :], ALU.add).then_inc(h2_ready, 1)
                    dve.wait_ge(h2_rms, t + 1)
                    chain(dve.reciprocal(rstd[:, t:t + 1], rstd[:, t:t + 1]))
                    chain(dve.scalar_tensor_tensor(u2[:, t % 2, :], h2[:, t % 2, :], rstd[:, t:t + 1], rows[:, 2, :],
                                                   ALU.mult, ALU.mult))
                    dve.tensor_tensor(u2[:, t % 2, :], u2[:, t % 2, :], rows[:, 1, :], ALU.add).then_inc(u2_ready, 1)

            @block.tensor
            def _(pe):
                for r in range(4):
                    if r >= 2:
                        pe.wait_ge(row_ready_a, r - 1)
                    for n in range(2):
                        mm = pe.matmul(ps[:, 2 * (r % 2) + n, :], ones,
                                       ada12[:, r // 2, (r % 2) * D + n * 512:(r % 2) * D + (n + 1) * 512], start=True,
                                       stop=True)
                    mm.then_inc(row_sum, 1)

                def route(t):
                    pe.wait_ge(u2_ready, t + 1)
                    if t >= 1:
                        pe.wait_ge(u2T_ready, t)
                    for k in range(KD):
                        mm = pe.transpose(ps[:, k // 4, (k % 4) * P:(k % 4 + 1) * P], u2[:, t % 2, k * P:(k + 1) * P],
                                          ident)
                    mm.then_inc(u2_turned, 1)
                    pe.wait_ge(u2T_ready, t + 1)
                    if t == 0:
                        pe.wait_ge(row_ready_a, 3)
                        pe.wait_ge(wr_in, 32)
                    dst = ps[:, 2, t * E:(t + 1) * E]
                    pe.matmul(dst, ones[0:1, :], br[:], start=(t == 0), stop=False, skip_group_check=True)
                    for k in range(KD):
                        mm = pe.matmul(dst, u2T[:, k * P:(k + 1) * P], wr[:, k, :], start=False, stop=(k == KD - 1),
                                       skip_group_check=True)
                    mm.then_inc(routed, 1)

                for t in range(2, TT):
                    pe.wait_ge(mix_read, t - 1)
                    mix_product(pe, t)
                    route(t - 2)
                route(TT - 2)
                route(TT - 1)

        pexp_in = sem("pexp_in")
        pexp = sem("pexp")
        chosen_ready = sem("chosen_ready")
        counted = sem("counted")
        nex_ready = sem("nex_ready")
        nex_sum = sem("nex_sum")
        mex_ready = sem("mex_ready")
        mex_sum = sem("mex_sum")
        slot_ready = sem("slot_ready")
        slot_used = sem("slot_used")

        with nc.Block() as block:
            @block.sync
            def _(sp):
                for j in range(2, 4):
                    expert_load(sp, 1, -4 + j, 1, "w1", j)
                for j in range(4, 8):
                    expert_load(sp, 1, -4 + j, 1, "w1", j)
                for s in range(2):
                    sp.wait_ge(stored_h[s], 16 * TT // 2)
                    sp.wait_ge(stored_u[s], 16 * TT // 2)

            @block.gpsimd
            def _(pool):
                for g in range(SPLITS):
                    pool.wait_ge(x_hi_done, g + 1)
                    pool.tensor_tensor(w_lo[:, g, :], raw[:, g, :], w_hi[:, g, :].bitcast(F32),
                                       ALU.subtract).then_inc(x_lo_3 if g == 3 else x_lo_012, 1)

            @block.scalar
            def _(act):
                act.wait_ge(pexp_in, 1)
                act.activation(prob[:], prob[:], ACT.Exp).then_inc(pexp, 1)
                for g in range(SPLITS):
                    act.wait_ge(raw_in[g], 16)
                    act.activation(w_hi[:, g, :], raw[:, g, :], ACT.Copy).then_inc(x_hi_done, 1)

            @block.vector
            def _(dve):
                chain = Chain(dve, dve_step, order)
                chain(dve.tensor_copy(lg[:], ps[:, 2, 0:TT * E].rearrange("p (t e) -> p t e", e=E)))
                for t in range(TT):
                    chain(dve.max(val8[:, t, :], lg[:, t, :]))
                    chain(dve.max_index(idx8[:, t, :], val8[:, t, :], lg[:, t, :]))
                chain(dve.tensor_copy(idxf[:], idx8[:]))
                chain(dve.tensor_tensor(
                    onehot[:], idxf[:, :, 0:TOP, None].to_broadcast([P, TT, TOP, E]),
                    iota[:, None, None, 0:E].to_broadcast([P, TT, TOP, E]), ALU.is_equal))
                dve.tensor_reduce(chosen[:], onehot[:].rearrange("p t k e -> p t e k"), AX.X,
                                  ALU.add).then_inc(chosen_ready, 1)
                dve.tensor_tensor(prob[:], val8[:, :, 0:TOP], val8[:, :, 0:1].to_broadcast([P, TT, TOP]),
                                  ALU.subtract).then_inc(pexp_in, 1)
                dve.wait_ge(pexp, 1)
                chain(dve.tensor_reduce(psm[:], prob[:], AX.X, ALU.add))
                chain(dve.reciprocal(prc[:], psm[:]))
                chain(dve.tensor_tensor(vv[:, 1, :].rearrange("p (t k) -> p t k", k=TOP), prob[:],
                                        prc[:, :, None].to_broadcast([P, TT, TOP]), ALU.mult))
                chain(dve.tensor_copy(vv[:, 0, :], const[:, C_ROW:C_ROW + 16]))
                dve.wait_ge(counted, 1)
                for t in range(TT):
                    chain(dve.tensor_tensor(ohpos[:, t], onehot[:, t],
                                            ps[:, 0, t * E:(t + 1) * E][:, None, :].to_broadcast([P, TOP, E]), ALU.mult))
                chain(dve.tensor_reduce(pos[:].rearrange("p (t k) -> p t k", k=TOP), ohpos[:], AX.X, ALU.add))
                for b in range(3):
                    chain(dve.tensor_scalar(ge[:, b, :], pos[:], 128.0 * (b + 1), None, ALU.is_ge))
                chain(dve.tensor_tensor(blk[:], ge[:, 0, :], ge[:, 1, :], ALU.add))
                chain(dve.tensor_tensor(blk[:], blk[:], ge[:, 2, :], ALU.add))
                chain(dve.scalar_tensor_tensor(pos[:], blk[:], -128.0, pos[:], ALU.mult, ALU.add))
                chain(dve.scalar_tensor_tensor(qcol[:].rearrange("p (t k) -> p t k", k=TOP), idxf[:, :, 0:TOP], 4.0,
                                               blk[:].rearrange("p (t k) -> p t k", k=TOP), ALU.mult, ALU.add))
                for b in range(3):
                    chain(dve.tensor_scalar(cnt[:, 1 + b:2 + b], ps[0:E, 0, 160:161], 128.0 * (b + 1), None, ALU.is_gt))
                chain(dve.tensor_tensor(cnt[:, 4:5], cnt[:, 1:2], cnt[:, 2:3], ALU.add))
                dve.tensor_tensor(cnt[:, 4:5], cnt[:, 4:5], cnt[:, 3:4], ALU.add).then_inc(nex_ready, 1)
                def extra_blocks():
                    dve.wait_ge(nex_sum, 1)
                    chain(dve.tensor_copy(cnt[:, 0:1], ps[0:E, 1, 0:1]))
                    chain(dve.memset(mex[:], 0.0))
                    for b in range(3):
                        chain(dve.tensor_scalar(cnt[:, 5:6], cnt[:, 0:1], float(b), None, ALU.add))
                        chain(dve.tensor_scalar(mtmp[:, 0, :], iota[0:E, 0:MAX_EXTRA], cnt[:, 5:6], cnt[:, 1 + b:2 + b],
                                                ALU.is_equal, ALU.mult))
                        chain(dve.tensor_scalar(mtmp[:, 1, :], mtmp[:, 0, :], float(b + 1), None, ALU.mult))
                        ins = dve.tensor_tensor(mex[:], mex[:], mtmp[:], ALU.add)
                        if b < 2:
                            chain(ins)
                        else:
                            ins.then_inc(mex_ready, 1)
                    chain(dve.memset(btf[:], 0.0))
                    chain(dve.tensor_copy(btf[:, 0:E], iota[0:1, 0:E]))
                    chain(dve.tensor_scalar(btf[:, MAX_BLOCKS:MAX_BLOCKS + E], iota[0:1, 0:E], 4.0, None, ALU.mult))

                for j in range(16):
                    if j == 10:
                        extra_blocks()
                    if j >= 2:
                        dve.wait_ge(slot_used, j - 1)
                    dve.tensor_scalar(slot_row[:, j % 2, :], iota, pos[:, j:j + 1], None, ALU.is_equal)
                    for a in range(2):
                        ins = dve.tensor_scalar(slot_col[:, j % 2, a, :], iota, qcol[:, j:j + 1], vv[:, a, j:j + 1],
                                                ALU.is_equal, ALU.mult)
                    ins.then_inc(slot_ready, 1)
                dve.wait_ge(mex_sum, 1)
                chain(dve.tensor_copy(btf[:, E:MAX_BLOCKS], ps[0:1, 1, 64:64 + MAX_EXTRA]))
                chain(dve.tensor_copy(btf[:, MAX_BLOCKS + E:2 * MAX_BLOCKS], ps[0:1, 1, 96:96 + MAX_EXTRA]))
                chain(dve.tensor_copy(btf[:, 2 * MAX_BLOCKS:2 * MAX_BLOCKS + 1], ps[0:1, 1, 32:33]))
                for s in range(2):
                    dve.wait_ge(stored_h[s], 16 * TT // 2)
                chain(dve.tensor_copy(bt[:], btf[:]))
                dve.wait_ge(slot_used, 16)
                chain(dve.tensor_scalar(tabI[:, 1, :], ps[:, 3, 0:P], UNFILLED, None, ALU.add))
                chain(dve.tensor_scalar(tabI[:, 0, :], tabI[:, 1, :], 2, None, ALU.logical_shift_right))
                chain(dve.tensor_copy(tabW[:], ps[:, 3, P:2 * P]))

            @block.tensor
            def _(pe):
                pe.wait_ge(chosen_ready, 1)
                first = True
                for t in range(TT):
                    for s in range(t + 1):
                        pe.matmul(ps[:, 0, t * E:(t + 1) * E], tri if s == t else ones, chosen[:, s, :], start=first,
                                  stop=(s == t), skip_group_check=True)
                        first = False
                for s in range(TT):
                    mm = pe.matmul(ps[0:E, 0, 160:161], chosen[:, s, :], ones[:, 0:1], start=False, stop=(s == TT - 1),
                                   skip_group_check=True)
                mm.then_inc(counted, 1)
                pe.wait_ge(nex_ready, 1)
                pe.matmul(ps[0:E, 1, 0:1], tri[0:E, 0:E], cnt[:, 4:5], start=True, stop=True, skip_group_check=True)
                pe.matmul(ps[0:1, 1, 32:33], ones[0:E, 0:1], cnt[:, 4:5], start=False, stop=True,
                          skip_group_check=True).then_inc(nex_sum, 1)
                def extra_blocks():
                    pe.wait_ge(mex_ready, 1)
                    pe.matmul(ps[0:1, 1, 64:64 + MAX_EXTRA], const[0:E, C_PART:C_PART + 1], mex[:, 0, :], start=False,
                              stop=True, skip_group_check=True)
                    pe.matmul(ps[0:1, 1, 96:96 + MAX_EXTRA], const[0:E, C_PART + 1:C_PART + 2], mex[:, 0, :], start=False,
                              stop=False, skip_group_check=True)
                    pe.matmul(ps[0:1, 1, 96:96 + MAX_EXTRA], ones[0:E, 0:1], mex[:, 1, :], start=False, stop=True,
                              skip_group_check=True).then_inc(mex_sum, 1)

                for j in range(16):
                    if j == 12:
                        extra_blocks()
                    pe.wait_ge(slot_ready, j + 1)
                    pe.matmul(ps[:, 3, 0:2 * P], slot_row[:, j % 2, :],
                              slot_col[:, j % 2].rearrange("p a n -> p (a n)"), start=(j == 0),
                              stop=(j == 15)).then_inc(slot_used, 1)

        gathered = sem("gathered")
        hs_turned = sem("hs_turned")
        hsT_hi_ready = sem("hsT_hi_ready")
        hsT_lo_ready = sem("hsT_lo_ready")
        sel1_ready = sem("sel1_ready")
        sel2_ready = sem("sel2_ready")
        tok_ready = sem("tok_ready")
        row_ready = sem("row_ready")
        wcol_ready = sem("wcol_ready")
        w1_started = sem("w1_started")
        w2_started = sem("w2_started")
        glu_ready = sem("glu_ready")
        sig_ready = sem("sig_ready")
        hid_read = sem("hid_read")
        gs_ready = sem("gs_ready")
        act_ready = sem("act_ready")
        a_turned = sem("a_turned")
        aT_hi_ready = sem("aT_hi_ready")
        aT_lo_ready = sem("aT_lo_ready")
        y_ready = sem("y_ready")
        scattered = sem("scattered")
        row_last = sem("row_last")
        y_last = sem("y_last")

        def w1_end(b):
            return 8 if known(b) and b == 0 else 12 * b + 4

        def w2_end(b, last=False):
            return 12 * b + (12 if last else 20)

        OUTB, TPB = slice(4, 6), slice(6, 8)

        def blocks(eng):
            return E + eng.value_load(bt[0:1, 2 * MAX_BLOCKS:2 * MAX_BLOCKS + 1], min_val=0, max_val=MAX_EXTRA - 1)

        def expert_of(eng, i):
            if known(i) and i < E:
                return i
            return eng.value_load(bt[0:1, bass.ds(i, 1)], min_val=0, max_val=E - 1)

        def column_of(eng, i):
            return eng.value_load(bt[0:1, bass.ds(i + MAX_BLOCKS, 1)], min_val=0, max_val=P - 1)

        h_in_in = sem("h_in_in")

        with nc.Block() as block:
            @block.sync
            def _(sp):
                n = blocks(sp)
                with sp.Fori(2, n) as i:
                    e2 = expert_of(sp, i - 2)
                    for j in range(4):
                        expert_load(sp, i, -8 + j, e2, "w2", j)
                    e1 = expert_of(sp, i)
                    for j in range(8):
                        expert_load(sp, i, -4 + j, e1, "w1", j)
                e2 = expert_of(sp, n - 2)
                for j in range(4):
                    expert_load(sp, n, -8 + j, e2, "w2", j)
                e2 = expert_of(sp, n - 1)
                for j in range(4):
                    expert_load(sp, n, -4 + j, e2, "w2", j)
                lo_wait(sp, n, -10)
                sp.dma_start(h_in[:], h2_d.rearrange("(t p) n -> p t n", p=P)).then_inc(h_in_in, 16)
                sp.dma_start(wfin[:], norm_final_w.rearrange("(a n) -> a n", a=1).to_broadcast([P, D])).then_inc(h_in_in, 16)

            @block.gpsimd
            def _(pool):
                n = blocks(pool)

                def split_lo(i, off):
                    pool.wait_ge(x_hi_done, 12 * i + off + 1)
                    pool.tensor_tensor(w_lo[:, off % SPLITS, :], raw[:, off % RAWS, :],
                                       w_hi[:, off % SPLITS, :].bitcast(F32), ALU.subtract).then_inc(x_lo_3, 1)

                def take_waits():
                    pool.tensor_tensor(spare[:], ones[:, 0:1], ones[:, 0:1], ALU.add)

                def pick(b):
                    col = column_of(pool, b)
                    if not known(b) or b >= 1:
                        pool.wait_ge(gathered, 16 * b)
                    pool.tensor_copy(cur_tok[:], tabI[:, 0, bass.ds(col, 1)]).then_inc(tok_ready, 1)

                def await_pick(b):
                    pool.wait_ge(tok_ready, b + 1)
                    if not known(b) or b >= 1:
                        pool.wait_ge(hs_turned, b)

                def gather():
                    pool.indirect_dma_start(out=hs[:], out_offset=None, in_=u2_d,
                                            in_offset=bass.IndirectOffsetOnAxis(ap=cur_tok[:], axis=0),
                                            bounds_check=TOKENS - 1, oob_is_err=False).then_inc(gathered, 16)

                def select(sel, b, ready, started):
                    e = expert_of(pool, b)
                    if not known(b) or b >= 1:
                        pool.wait_ge(started, b)
                    pool.tensor_copy(sel[:], const[:, bass.ds(e + C_EYE2, 1)].to_broadcast([P, P])).then_inc(ready, 1)

                def weigh(b, done=row_ready):
                    col = column_of(pool, b)
                    if not known(b) or b >= 1:
                        pool.wait_ge(scattered, 16 * b)
                        pool.wait_ge(y_ready, b)
                    pool.tensor_copy(cur_w[:], tabW[:, bass.ds(col, 1)]).then_inc(wcol_ready, 1)
                    pool.tensor_copy(cur_row[:], tabI[:, 1, bass.ds(col, 1)]).then_inc(done, 1)

                def await_y(b):
                    pool.wait_ge(row_ready, b + 1)
                    pool.wait_ge(y_ready, b + 1)

                def scatter():
                    pool.indirect_dma_start(out=y_d, out_offset=bass.IndirectOffsetOnAxis(ap=cur_row[:], axis=0),
                                            in_=y_out[:], in_offset=None, bounds_check=TOKENS * TOP - 1,
                                            oob_is_err=False).then_inc(scattered, 16)

                pick(0)
                await_pick(0)
                gather()
                select(sel1, 0, sel1_ready, w1_started)
                pick(1)
                await_pick(1)
                gather()
                select(sel1, 1, sel1_ready, w1_started)
                split_lo(0, 7)
                split_lo(1, -1)
                pick(2)
                await_pick(2)
                gather()
                split_lo(1, 3)
                with pool.Fori(2, n) as i:
                    select(sel2, i - 2, sel2_ready, w2_started)
                    pick(i + 1)
                    await_pick(i + 1)
                    take_waits()
                    gather()
                    split_lo(i, -5)
                    select(sel1, i, sel1_ready, w1_started)
                    split_lo(i, -1)
                    weigh(i - 2)
                    await_y(i - 2)
                    take_waits()
                    scatter()
                    split_lo(i, 3)
                select(sel2, n - 2, sel2_ready, w2_started)
                split_lo(n, -5)
                weigh(n - 2)
                await_y(n - 2)
                take_waits()
                scatter()
                select(sel2, n - 1, sel2_ready, w2_started)
                split_lo(n, -1)
                weigh(n - 1, row_last)
                pool.wait_ge(row_last, 1)
                pool.wait_ge(y_last, 1)
                scatter()
                pool.wait_ge(scattered, 16 * n)

            @block.scalar
            def _(act):
                n = blocks(act)

                def split_hi(i, off):
                    act.wait_ge(raw_in[off % RAWS], 16 * (i + off // RAWS + 1))
                    if not known(i) or 12 * i + off >= SPLITS:
                        act.wait_ge(x_used, 12 * i + off - SPLITS + 1)
                    act.activation(w_hi[:, off % SPLITS, :], raw[:, off % RAWS, :], ACT.Copy).then_inc(x_hi_done, 1)

                def rows_hi(b):
                    act.wait_ge(hs_turned, b + 1)
                    if not known(b) or b >= 1:
                        act.wait_ge(x_used, w1_end(b - 1))
                    act.activation(hsT_hi[:].rearrange("p k t -> p (k t)"), ps[:, TPB, :].rearrange("p b n -> p (b n)"),
                                   ACT.Copy).then_inc(hsT_hi_ready, 1)

                def sigmoid(b):
                    act.wait_ge(glu_ready, b + 1)
                    if not known(b) or b >= 1:
                        act.wait_ge(act_ready, b)
                    act.activation(sig[:], glu[:], ACT.Sigmoid, scale=ALPHA).then_inc(sig_ready, 1)

                def act_hi(b):
                    act.wait_ge(a_turned, b + 1)
                    if not known(b) or b >= 1:
                        act.wait_ge(x_used, w2_end(b - 1))
                    act.activation(aT_hi[:].rearrange("p k t -> p (k t)"), ps[:, TPB, :].rearrange("p b n -> p (b n)"),
                                   ACT.Copy).then_inc(aT_hi_ready, 1)

                def weigh_out(b, last=False):
                    act.wait_ge(x_used, w2_end(b, last))
                    act.wait_ge(wcol_ready, b + 1)
                    if not known(b) or b >= 1:
                        act.wait_ge(scattered, 16 * b)
                    act.activation(y_out[:], ps[:, OUTB, :].rearrange("p b n -> p (b n)"), ACT.Copy,
                                   scale=cur_w[:]).then_inc(y_last if last else y_ready, 1)

                rows_hi(0)
                for j in range(4, 8):
                    split_hi(0, j)
                for j in range(4):
                    split_hi(1, -4 + j)
                rows_hi(1)
                sigmoid(0)
                for j in range(4, 8):
                    split_hi(1, -4 + j)
                act_hi(0)
                with act.Fori(2, n) as i:
                    for j in range(4):
                        split_hi(i, -8 + j)
                    sigmoid(i - 1)
                    rows_hi(i)
                    for j in range(4):
                        split_hi(i, -4 + j)
                    weigh_out(i - 2)
                    for j in range(4, 8):
                        split_hi(i, -4 + j)
                    act_hi(i - 1)
                for j in range(4):
                    split_hi(n, -8 + j)
                sigmoid(n - 1)
                for j in range(4):
                    split_hi(n, -4 + j)
                weigh_out(n - 2)
                act_hi(n - 1)
                weigh_out(n - 1, last=True)

            @block.vector
            def _(dve):
                n = blocks(dve)

                def split_lo(i, off):
                    if off % SPLITS == 3:
                        return
                    dve.wait_ge(x_hi_done, 12 * i + off + 1)
                    dve.tensor_tensor(w_lo[:, off % SPLITS, :], raw[:, off % RAWS, :],
                                      w_hi[:, off % SPLITS, :].bitcast(F32), ALU.subtract).then_inc(x_lo_012, 1)

                def rows_lo(b):
                    dve.wait_ge(hsT_hi_ready, b + 1)
                    dve.tensor_tensor(hsT_lo[:].rearrange("p k t -> p (k t)"),
                                      ps[:, TPB, :].rearrange("p b n -> p (b n)"),
                                      hsT_hi[:].rearrange("p k t -> p (k t)").bitcast(F32),
                                      ALU.subtract).then_inc(hsT_lo_ready, 1)

                def clamp(b):
                    dve.wait_ge(x_used, w1_end(b))
                    if not known(b) or b >= 1:
                        dve.wait_ge(gs_ready, b)
                    dve.tensor_scalar(glu[:], ps[:, 0:2, :].rearrange("p b n -> p (b n)"), LIMIT, None,
                                      ALU.min).then_inc(glu_ready, 1)
                    if not known(b) or b >= 1:
                        dve.wait_ge(a_turned, b)
                    dve.tensor_scalar(lin[:], ps[:, 2:4, :].rearrange("p b n -> p (b n)"), LIMIT, -LIMIT, ALU.min,
                                      ALU.max).then_inc(hid_read, 1)

                def swish(b):
                    dve.wait_ge(sig_ready, b + 1)
                    dve.tensor_tensor(sig[:], sig[:], glu[:], ALU.mult).then_inc(gs_ready, 1)
                    dve.wait_ge(gs_ready, b + 1)
                    dve.wait_ge(hid_read, b + 1)
                    dve.scalar_tensor_tensor(lin[:], lin[:], 1.0, sig[:], ALU.add, ALU.mult).then_inc(act_ready, 1)

                def act_lo(b):
                    dve.wait_ge(aT_hi_ready, b + 1)
                    dve.tensor_tensor(aT_lo[:].rearrange("p k t -> p (k t)"),
                                      ps[:, TPB, :].rearrange("p b n -> p (b n)"),
                                      aT_hi[:].rearrange("p k t -> p (k t)").bitcast(F32),
                                      ALU.subtract).then_inc(aT_lo_ready, 1)

                rows_lo(0)
                for j in range(4, 8):
                    split_lo(0, j)
                for j in range(4):
                    split_lo(1, -4 + j)
                rows_lo(1)
                clamp(0)
                swish(0)
                for j in range(4, 8):
                    split_lo(1, -4 + j)
                act_lo(0)
                with dve.Fori(2, n) as i:
                    for j in range(4):
                        split_lo(i, -8 + j)
                    clamp(i - 1)
                    rows_lo(i)
                    split_lo(i, -4)
                    swish(i - 1)
                    for j in range(1, 8):
                        split_lo(i, -4 + j)
                    act_lo(i - 1)
                for j in range(4):
                    split_lo(n, -8 + j)
                clamp(n - 1)
                swish(n - 1)
                for j in range(4):
                    split_lo(n, -4 + j)
                act_lo(n - 1)

            @block.tensor
            def _(pe):
                n = blocks(pe)

                def turn_rows(b):
                    pe.wait_ge(gathered, 16 * (b + 1))
                    if not known(b):
                        pe.wait_ge(aT_lo_ready, b - 1)
                    elif b >= 2:
                        pe.wait_ge(aT_lo_ready, b - 1)
                    elif b == 1:
                        pe.wait_ge(hsT_lo_ready, 1)
                    for k in range(KD):
                        mm = pe.transpose(ps[:, 6 + k // 4, (k % 4) * P:(k % 4 + 1) * P], hs[:, k * P:(k + 1) * P], ident)
                    mm.then_inc(hs_turned, 1)

                def turn_act(b):
                    pe.wait_ge(act_ready, b + 1)
                    pe.wait_ge(hsT_lo_ready, b + 2)
                    for k in range(KD):
                        mm = pe.transpose(ps[:, 6 + k // 4, (k % 4) * P:(k % 4 + 1) * P], lin[:, k * P:(k + 1) * P], ident)
                    mm.then_inc(a_turned, 1)

                def turn_last(pe, n):
                    pe.wait_ge(act_ready, n)
                    for k in range(KD):
                        mm = pe.transpose(ps[:, 6 + k // 4, (k % 4) * P:(k % 4 + 1) * P], lin[:, k * P:(k + 1) * P], ident)
                    mm.then_inc(a_turned, 1)

                def w1_bias(b):
                    pe.wait_ge(sel1_ready, b + 1)
                    if not known(b) or b >= 1:
                        pe.wait_ge(hid_read, b)
                        pe.wait_ge(glu_ready, b)
                    for q in range(4):
                        mm = pe.matmul(ps[:, q, :], sel1[:], bias1[:, q * 512:(q + 1) * 512], start=True, stop=False)
                    mm.then_inc(w1_started, 1)
                    pe.wait_ge(hsT_lo_ready, b + 1)

                def w1_chunk(b, i, off, j):
                    lo_wait(pe, i, off)
                    s = off % SPLITS
                    for q in range(4):
                        mh, ml = (w[:, s, q * 512:(q + 1) * 512] for w in (w_hi, w_lo))
                        pe.matmul(ps[:, q, :], hsT_hi[:, j, :], mh, start=False, stop=False)
                        pe.matmul(ps[:, q, :], hsT_hi[:, j, :], ml, start=False, stop=False)
                        mm = pe.matmul(ps[:, q, :], hsT_lo[:, j, :], mh, start=False, stop=(j == 7))
                    mm.then_inc(x_used, 1)

                def w2_block(b, i, off):
                    pe.wait_ge(sel2_ready, b + 1)
                    if not known(b) or b >= 1:
                        pe.wait_ge(y_ready, b)
                    for q in range(2):
                        mm = pe.matmul(ps[:, 4 + q, :], sel2[:], bias2[:, q * 512:(q + 1) * 512], start=True, stop=False)
                    mm.then_inc(w2_started, 1)
                    pe.wait_ge(aT_lo_ready, b + 1)
                    for j in range(4):
                        lo_wait(pe, i, off + j)
                        s = (off + j) % SPLITS
                        for kk in range(2):
                            k = 2 * j + kk
                            for q in range(2):
                                at_ = kk * D + q * 512
                                mh, ml = (w[:, s, at_:at_ + 512] for w in (w_hi, w_lo))
                                dst = ps[:, 4 + q, :]
                                pe.matmul(dst, aT_hi[:, k, :], mh, start=False, stop=False)
                                pe.matmul(dst, aT_hi[:, k, :], ml, start=False, stop=False)
                                mm = pe.matmul(dst, aT_lo[:, k, :], mh, start=False, stop=(k == KD - 1))
                        mm.then_inc(x_used, 1)

                turn_rows(0)
                w1_bias(0)
                for j in range(8):
                    w1_chunk(0, 0, j, j)
                turn_rows(1)
                w1_bias(1)
                for j in range(4):
                    w1_chunk(1, 1, -4 + j, j)
                turn_act(0)
                for j in range(4, 8):
                    w1_chunk(1, 1, -4 + j, j)
                turn_rows(2)
                with pe.Fori(2, n) as i:
                    w2_block(i - 2, i, -8)
                    w1_bias(i)
                    for j in range(4):
                        w1_chunk(i, i, -4 + j, j)
                    turn_act(i - 1)
                    for j in range(4, 8):
                        w1_chunk(i, i, -4 + j, j)
                    turn_rows(i + 1)
                w2_block(n - 2, n, -8)
                turn_last(pe, n)
                w2_block(n - 1, n, -4)

        y_in_in = x_inn
        y23_ready = sem("y23_ready")
        hsum_ready = sem("hsum_ready")
        fsq_ready = sem("fsq_ready")
        frms_ready = sem("frms_ready")
        out_ready = sem("out_ready")
        out_stored = sem("out_stored")

        with nc.Block() as block:
            @block.sync
            def _(sp):
                yv = y_d.rearrange("(t k) n -> t k n", k=TOP)
                for t in range(TT):
                    sp.dma_start(y_in[:, t], yv[t * P:(t + 1) * P]).then_inc(y_in_in[t], 16)
                for t in range(TT):
                    sp.wait_ge(out_ready, t + 1)
                    sp.dma_start(out2[t * P:(t + 1) * P, :], h_out[:, t, :]).then_inc(out_stored, 16)
                sp.wait_ge(out_stored, 16 * TT)
                sp.wait_ge(h_in_in, 32)

            @block.gpsimd
            def _(pool):
                for t in range(TT):
                    pool.wait_ge(y_in_in[t], 32)
                    if t >= 2:
                        pool.wait_ge(hsum_ready, t - 1)
                    pool.tensor_tensor(y_23[:, t % 2, :], y_in[:, t, 2, :], y_in[:, t, 3, :],
                                       ALU.add).then_inc(y23_ready, 1)

            @block.scalar
            def _(act):
                for t in range(TT):
                    act.wait_ge(hsum_ready, t + 1)
                    if t >= 1:
                        act.wait_ge(fsq_ready, t)
                    act.activation(sq[:], h_out[:, t, :], ACT.Square, scale=D ** -0.5,
                                   accum_out=ms[:, t:t + 1]).then_inc(fsq_ready, 1)
                    act.wait_ge(fsq_ready, t + 1)
                    act.activation(rstd[:, t:t + 1], ms[:, t:t + 1], ACT.Sqrt, bias=eps).then_inc(frms_ready, 1)

            @block.vector
            def _(dve):
                chain = Chain(dve, dve_step, order)
                dve.wait_ge(h_in_in, 32)
                for t in range(TT + 1):
                    if t < TT:
                        s = t % 2
                        dve.wait_ge(y_in_in[t], 32)
                        chain(dve.tensor_tensor(y_01[:, s, :], y_in[:, t, 0, :], y_in[:, t, 1, :], ALU.add))
                        dve.wait_ge(y23_ready, t + 1)
                        chain(dve.tensor_tensor(y_01[:, s, :], y_01[:, s, :], y_23[:, s, :], ALU.add))
                        chain(dve.tensor_tensor(y_01[:, s, :], y_01[:, s, :], gate_f[:], ALU.mult))
                        dve.tensor_tensor(h_out[:, t, :], y_01[:, s, :], h_in[:, t, :], ALU.add).then_inc(hsum_ready, 1)
                    if t >= 1:
                        b = t - 1
                        dve.wait_ge(frms_ready, b + 1)
                        chain(dve.reciprocal(rstd[:, b:b + 1], rstd[:, b:b + 1]))
                        dve.scalar_tensor_tensor(h_out[:, b, :], h_out[:, b, :], rstd[:, b:b + 1], wfin[:], ALU.mult,
                                                 ALU.mult).then_inc(out_ready, 1)


_INS = ["x", "c", "w_ada", "b_ada", "norm_mix_w", "w_in", "hgrn_lower_bounds", "hgrn_norm_w", "conv_w", "w_hgrn_out",
        "w_conv_out", "w_mix_out", "norm_ffn_w", "w_router", "b_router", "w1", "b1", "w2", "b2", "norm_final_w"]


def kernel(**inputs):
    import concourse.bacc as _bacc
    from concourse.bass_utils import run_bass_kernel_spmd as _run

    nc = _bacc.Bacc("TRN2", target_bir_lowering=False, num_devices=1, dynamic_dma_scratch_size=4096)
    arrays = {"shape_constants": shape_constants(), "level_masks": level_masks()}
    for name in _INS:
        arrays[f"in_{name}"] = np.ascontiguousarray(inputs[name])
    args = [nc.dram_tensor(n, a.shape, mybir.dt.from_np(a.dtype), kind="ExternalInput").ap() for n, a in arrays.items()]
    out = nc.dram_tensor("layer_out", (1, TOKENS, D), F32, kind="ExternalOutput").ap()
    layer_kernel(nc, *args, out)
    r = _run(nc, [arrays], core_ids=[0])
    return r.results[0]["layer_out"]
```

```python
from contextlib import ExitStack

import numpy as np

import concourse.bass as bass
from concourse import mybir

F32 = mybir.dt.float32
F32R = mybir.dt.float32r
U32 = mybir.dt.uint32
I32 = mybir.dt.int32
U8 = mybir.dt.uint8
ALU = mybir.AluOpType
ACT = mybir.ActivationFunctionType
AX = mybir.AxisListType

P = 128
D = 1024
KD = D // P
TOKENS = 512
TT = TOKENS // P
HEADS = 4
HW = HEADS * P
LEVELS = 7
CONV_K = 3
E = 32
TOP = 4
FF = 1024
LIMIT = 7.0
ALPHA = 1.702
EPS = 1e-6
TINY = 1e-18
CH = 2048
SPLITS = 4
RAWS = 12
MAX_EXTRA = 16
MAX_BLOCKS = E + MAX_EXTRA
UNFILLED = 4096.0
KB = 1024

C_ID, C_ONE, C_TRI, C_IOTA, C_EYE2, C_ROW, C_PART, C_RESET = 0, 128, 256, 384, 512, 544, 576, 608
C_END = C_RESET + TOKENS


def shape_constants():
    c = np.zeros((P, C_END), np.float32)
    p = np.arange(P)
    c[:, C_ID:C_ID + P] = np.eye(P)
    c[:, C_ONE:C_ONE + P] = 1
    c[:, C_TRI:C_TRI + P] = p[:, None] < p[None, :]
    c[:, C_IOTA:C_IOTA + P] = p[None, :]
    c[:64, C_EYE2:C_EYE2 + E] = (p[:64, None] % E) == np.arange(E)[None, :]
    tok = np.arange(TT)[None, :, None] * P + p[:, None, None] + 0 * np.arange(TOP)[None, None, :]
    c[:, C_ROW:C_ROW + 16] = (tok * TOP + np.arange(TOP)).reshape(P, 16) - UNFILLED
    c[:, C_PART] = p
    c[:, C_PART + 1] = TOP * p
    c[:, C_RESET:C_RESET + TOKENS] = (np.arange(TOKENS) % P != 0)[None, :]
    return c


def level_masks():
    s, t = np.arange(P)[:, None], np.arange(P)[None, :]
    m = np.zeros((P, LEVELS, P), np.float32)
    for level in range(LEVELS):
        m[:, level] = ((s ^ t) >> level == 1) & (t > s)
    return m.reshape(P, LEVELS * P)


class Chain:

    def __init__(self, eng, sem, count):
        self.eng, self.sem, self.count = eng, sem, count

    def __call__(self, ins):
        ins.then_inc(self.sem, 1)
        self.count[0] += 1
        self.eng.wait_ge(self.sem, self.count[0])


def layer_kernel(nc, consts, masks, x, c, w_ada, b_ada, norm_mix_w, w_in, lower_bounds, hgrn_norm_w, conv_w,
                 w_hgrn_out, w_conv_out, w_mix_out, norm_ffn_w, w_router, b_router, w1, b1, w2, b2,
                 norm_final_w, out):
    x2 = x[0]
    out2 = out[0]
    u2_d = nc.dram_tensor("ffn_input", [TOKENS, D], F32, kind="Internal").ap()
    h2_d = nc.dram_tensor("residual", [TOKENS, D], F32, kind="Internal").ap()
    y_d = nc.dram_tensor("expert_rows", [TOKENS * TOP, D], F32, kind="Internal").ap()

    with ExitStack() as ctx:
        base = (nc.sbuf_base + 63) // 64 * 64

        def at(name, kb, shape, dt=F32):
            return nc.alloc_sbuf_tensor_at(name, shape, dt, offset=base + int(kb * KB))

        def sem(name):
            return ctx.enter_context(nc.semaphore(name))

        w_hi = at("w_hi", 0, [P, SPLITS, CH], F32R)
        w_lo = at("w_lo", 32, [P, SPLITS, CH], F32R)
        RAW = 64
        raw = at("raw", RAW, [P, RAWS, CH])
        stage_01 = at("stage_01", RAW, [P, 2, CH])
        ada0_in = at("ada0_in", 0, [P, KD, CH])
        uT_hi = at("uT_hi", RAW + 16, [P, KD, TOKENS], F32R)
        uT_lo = at("uT_lo", RAW + 32, [P, KD, TOKENS], F32R)
        M = RAW + 48
        merged_hi = at("merged_hi", M, [P, KD, TOKENS], F32R)
        merged_lo = at("merged_lo", M + 16, [P, KD, TOKENS], F32R)
        ada0 = at("ada0", M, [P, CH])
        wdiff = at("wdiff", M, [P, 2, HEADS, P])
        q_dec = at("q_dec", M + 4, [P, 2, HEADS, P])
        k_dec = at("k_dec", M + 8, [P, 2, HEADS, P])
        scores = at("scores", M + 12, [P, HEADS, P])
        state = at("state", M + 14, [P, HEADS, P])
        k_tok = at("k_tok", M + 16, [P, HEADS, P])
        o_norm = at("o_norm", M + 18, [P, HEADS, P])
        gates = at("gates", M + 20, [P, TT, HW])
        mask_f = at("mask_f", M + 20, [P, LEVELS * P])
        g_sig = at("g_sig", M + 28, [P, HW])
        y_tmp = at("y_tmp", M + 30, [P, TOKENS])
        yc_hi = at("yc_hi", RAW + 80, [P, HEADS, TOKENS], F32R)
        yc_lo = at("yc_lo", RAW + 88, [P, HEADS, TOKENS], F32R)
        cu = at("cu", RAW + 88, [P, HEADS, TOKENS])
        N = RAW + 96
        const = at("const", N, [P, C_RESET])
        ident = const[:, C_ID:C_ID + P]
        ones = const[:, C_ONE:C_ONE + P]
        tri = const[:, C_TRI:C_TRI + P]
        iota = const[:, C_IOTA:C_IOTA + P]
        S0 = N + 2.375
        small = at("small", S0, [P, 324])
        vecT = small[:, 0:28]
        modT = small[:, 28:44]
        lb = small[:, 44:48]
        om_lb = small[:, 48:52]
        cs = small[:, 52:60]
        rstd = small[:, 60:64]
        ms = small[:, 64:68]
        hms = small[:, 68:72]
        hrs = small[:, 72:76]
        elast = small[:, 76:80]
        lbt = small[:, 80:96]
        csig = small[:, 96:104]
        eps = small[:, 104:105]
        R0 = N + 3.75
        qT = at("qT", R0, [P, HEADS, TOKENS])
        kT = at("kT", R0 + 8, [P, HEADS, TOKENS])
        bT = at("bT", R0 + 16, [P, HEADS, TOKENS])
        v_tok = at("v_tok", R0 + 24, [P, TT, HW])
        x_in = at("x_in", R0, [P, TT, D])
        x_n = at("x_n", R0 + 16, [P, TT, D])
        oT_hi = at("oT_hi", R0 + 32, [P, HEADS, TOKENS], F32R)
        oT_lo = at("oT_lo", R0 + 40, [P, HEADS, TOKENS], F32R)
        u_full = at("u_full", R0, [P, KD, TOKENS])
        vec_rows = at("vec_rows", R0 + 36, [28, P])
        reset = at("reset", R0 + 40, [P, TOKENS])
        mask_sb = at("mask_sb", R0 + 48, [P, LEVELS, P], U8)
        nw_row = at("nw_row", R0 + 49, [P, P])
        stage_2 = at("stage_2", R0 + 48, [P, CH])
        ada12 = at("ada12", R0, [P, 2, CH])
        sg_a = at("sg_a", R0 + 16, [P, 4, TOKENS])
        sg_b = at("sg_b", R0 + 24, [P, 4, TOKENS])
        rows = at("rows", RAW + 80, [P, 3, D])
        gate_f = at("gate_f", R0 + 28, [P, D])
        x_t = at("x_t", R0 + 32, [P, 2, D])
        h2 = at("h2", R0 + 8, [P, 2, D])
        u2 = at("u2", R0, [P, 2, D])
        u2T = at("u2T", R0 + 40, [P, D])
        tmp_j = at("tmp_j", R0 + 44, [P, D])
        wr = at("wr", R0 + 52, [P, KD, E])
        br = at("br", R0 + 53, [1, E])
        wf_row = at("wf_row", RAW + 32, [P, D])
        b2_raw = at("b2_raw", RAW + 36, [P, D])
        b1_raw = at("b1_raw", RAW + 40, [P, 2 * FF])
        val8 = small[:, 108:140].rearrange("p (t k) -> p t k", k=8)
        idxf = small[:, 140:172].rearrange("p (t k) -> p t k", k=8)
        prob = small[:, 172:188].rearrange("p (t k) -> p t k", k=TOP)
        psm = small[:, 188:192]
        prc = small[:, 192:196]
        pos = small[:, 196:212]
        blk = small[:, 212:228]
        ge = small[:, 228:276].rearrange("p (b n) -> p b n", b=3)
        qcol = small[:, 276:292]
        vv = small[:, 292:324].rearrange("p (a n) -> p a n", a=2)
        idx8 = at("idx8", S0 + 1.28125, [P, 8], U32)
        lg = at("lg", R0 + 53.125, [P, E])
        slot_col = at("slot_col", R0 + 53.25, [P, 2, 2, P])
        btf = at("btf", R0 + 55.25, [1, 2 * MAX_BLOCKS + 16])
        mex = at("mex", R0 + 55.6875, [E, 2, MAX_EXTRA])
        mtmp = at("mtmp", R0 + 55.8125, [E, 2, MAX_EXTRA])
        cnt = at("cnt", R0 + 55.9375, [E, 8])
        onehot = at("onehot", RAW + 92, [P, TT, TOP, E])
        chosen = at("chosen", RAW + 94, [P, TT, E])
        slot_row = at("slot_row", RAW + 95, [P, 2, P])
        bias1 = at("bias1", R0 + 16, [P, 2 * FF], F32R)
        bias2 = at("bias2", R0 + 24, [P, D], F32R)
        tabI = at("tabI", R0 + 12, [P, 2, P], U32)
        tabW = at("tabW", R0 + 13, [P, P])
        bt = at("bt", R0 + 13.5, [1, 2 * MAX_BLOCKS + 16], I32)
        sel1 = at("sel1", R0 + 14, [P, P], F32R)
        sel2 = at("sel2", R0 + 14.5, [P, P], F32R)
        cur_tok = at("cur_tok", R0 + 15, [P, 1], U32)
        cur_row = at("cur_row", R0 + 15.0625, [P, 1], U32)
        cur_w = at("cur_w", R0 + 15.125, [P, 1])
        spare = at("spare", R0 + 15.1875, [P, 1])
        last_w = at("last_w", R0 + 15.25, [P, 1])
        hs = at("hs", R0 + 48, [P, D])
        hsT_hi = at("hsT_hi", R0, [P, KD, P], F32R)
        hsT_lo = at("hsT_lo", R0 + 4, [P, KD, P], F32R)
        glu = at("glu", R0 + 8, [P, FF])
        sig = at("sig", R0 + 32, [P, FF])
        lin = at("lin", R0 + 36, [P, FF])
        aT_hi = at("aT_hi", R0 + 40, [P, KD, P], F32R)
        aT_lo = at("aT_lo", R0 + 44, [P, KD, P], F32R)
        y_out = at("y_out", R0 + 52, [P, D])
        h_in = at("h_in", RAW, [P, TT, D])
        wfin = at("wfin", RAW + 16, [P, D])
        y_in = at("y_in", RAW + 32, [P, TT, TOP, D])
        y_01 = at("y_01", 0, [P, 2, D])
        y_23 = at("y_23", 8, [P, 2, D])
        h_out = at("h_out", 16, [P, TT, D])
        sq = at("sq", 32, [P, D])

        ps = ctx.enter_context(nc.psum_tensor("ps", [P, 8, 512], F32))

        consts_in = sem("consts_in")
        vec_in = sem("vec_in")
        c_in = sem("c_in")
        x_inn = [sem(f"x_in{t}") for t in range(TT)]
        ada_bias_in = sem("ada_bias_in")
        prepared = sem("prepared")
        ada_in = [sem(f"ada_in{k}") for k in range(KD)]
        ada0_used = sem("ada0_used")
        csig_ready = sem("csig_ready")
        vec_turned = sem("vec_turned")
        square_x = sem("square_x")
        sqrt_x = sem("sqrt_x")
        xn_ready = sem("xn_ready")
        x_turned = sem("x_turned")
        mod_sum = sem("mod_sum")
        lb_exp_in = sem("lb_exp_in")
        lb_exp = sem("lb_exp")
        u_ready = sem("u_ready")
        u_hi_ready = sem("u_hi_ready")
        dve_step = sem("dve_step")
        order = [0]
        masks_in = sem("masks_in")
        mask_f_in = sem("mask_f_in")
        stage_in = [sem(f"stage_in{s}") for s in range(3)]

        def w_in_chunk(col, half):
            return w_in[0, half * 512:half * 512 + 512, col:col + 512].rearrange("(k p) n -> p k n", p=P)

        def out_chunk(w, row, col):
            return w[0, row:row + 512, col:col + 512].rearrange("(k p) n -> p k n", p=P)

        COL = {"q": 0, "f": 512, "v": 1024, "g": 1536, "cb": 2048, "cc": 2560, "ch": 3072,
               "ga0": 3584, "ga1": 4096, "gb0": 4608, "gb1": 5120}
        weight_chunks = []
        group_chunks = {}
        for name in ("f", "q", "v", "g", "cc", "ch", "cb", "ga0", "ya0", "gb0", "yb0", "ga1", "ya1", "gb1", "yb1",
                     "mix0", "mix1"):
            first = len(weight_chunks)
            if name in COL:
                weight_chunks += [w_in_chunk(COL[name], 0), w_in_chunk(COL[name], 1)]
            elif name[:2] == "ya":
                weight_chunks.append(out_chunk(w_hgrn_out, 0, 512 * int(name[2])))
            elif name[:2] == "yb":
                weight_chunks.append(out_chunk(w_conv_out, 0, 512 * int(name[2])))
            else:
                weight_chunks += [out_chunk(w_mix_out, 0, 512 * int(name[3])), out_chunk(w_mix_out, 512, 512 * int(name[3]))]
            group_chunks[name] = list(range(first, len(weight_chunks)))
        NW = len(weight_chunks)
        def refills(name):
            return [n + SPLITS for n in group_chunks[name] if n + SPLITS < NW]

        LATE = [("ga0", "ya0"), ("gb0", "yb0"), ("ga1", "ya1"), ("gb1", "yb1")]
        stream = [("w", n) for n in range(group_chunks["ga0"][0] + SPLITS)]
        for r, (gate, product) in enumerate(LATE):
            stream += [("ada", 4 * r + j) for j in range(3)]
            stream += [("w", n) for n in refills(gate)]
            stream += [("ada", 4 * r + 3)]
            stream += [("w", n) for n in refills(product)]
        where = {item: n for n, item in enumerate(stream)}
        THIRD_FROM = where["ada", 0]
        stage_of = [n % 2 if n < THIRD_FROM else (2, THIRD_FROM % 2, (THIRD_FROM + 1) % 2)[(n - THIRD_FROM) % 3]
                    for n in range(len(stream))]

        def staged(item):
            slot = stage_of[where[item]]
            return stage_2[:] if slot == 2 else stage_01[:, slot, :]

        ada_v = w_ada[0].rearrange("(p k) n -> p k n", k=KD)

        hi_done = sem("hi_done")
        lo_done = sem("lo_done")
        ada_scaled = sem("ada_scaled")
        ada_done = sem("ada_done")

        def stream_load(eng, n):
            earlier = [e for e in range(n) if stage_of[e] == stage_of[n]]
            if earlier:
                kind, m = stream[earlier[-1]]
                eng.wait_ge(lo_done if kind == "w" else ada_done, m + 1)
            kind, m = stream[n]
            dst = staged(stream[n])
            if kind == "w":
                eng.dma_start(dst.rearrange("p (k n) -> p k n", k=4), weight_chunks[m]).then_inc(stage_in[stage_of[n]], 16)
            else:
                eng.dma_start(dst, ada_v[:, m % KD, CH * (1 + m // KD):CH * (2 + m // KD)]).then_inc(
                    stage_in[stage_of[n]], 16)

        def wait_stage(eng, item):
            n = where[item]
            eng.wait_ge(stage_in[stage_of[n]], 16 * sum(slot == stage_of[n] for slot in stage_of[:n + 1]))

        with nc.Block() as block:
            @block.sync
            def _(sp):
                sp.dma_start(cs, c[0].rearrange("(p k) -> p k", k=KD)).then_inc(c_in, 16)
                for t in range(TT):
                    sp.dma_start(x_in[:, t, :], x2[t * P:(t + 1) * P, :]).then_inc(x_inn[t], 16)
                for k in range(KD):
                    sp.dma_start(ada0_in[:, k, :], ada_v[:, k, 0:CH]).then_inc(ada_in[k], 16)
                stream_load(sp, 0)
                stream_load(sp, 1)

            @block.gpsimd
            def _(pool):
                pool.memset(ada0[:], 0.0).then_inc(prepared, 1)
                pool.memset(eps, EPS).then_inc(prepared, 1)
                pool.wait_ge(mask_f_in, 16)
                pool.tensor_copy(mask_sb[:].rearrange("p l t -> p (l t)"), mask_f[:]).then_inc(prepared, 1)
                for j in range(KD - 1):
                    pool.wait_ge(u_hi_ready, j + 1)
                    pool.wait_ge(u_ready, j + 1)
                    pool.tensor_tensor(uT_lo[:, j, :], u_full[:, j, :], uT_hi[:, j, :].bitcast(F32),
                                       ALU.subtract)

            @block.scalar
            def _(act):
                act.dma_start(const[:], consts[:, 0:C_RESET]).then_inc(consts_in, 16)
                act.dma_start(vec_rows[0:8, :], norm_mix_w[0].rearrange("(j p) -> j p", p=P)).then_inc(vec_in, 16)
                act.dma_start(vec_rows[8:16, :], lower_bounds.rearrange("r (h p) -> (r h) p", p=P)).then_inc(vec_in, 16)
                act.dma_start(vec_rows[16:28, :], conv_w[0].rearrange("r (h p) -> (r h) p", p=P)).then_inc(vec_in, 16)
                act.wait_ge(prepared, 1)
                act.dma_start(ada0[0:1, :], b_ada[:, 0:CH]).then_inc(ada_bias_in, 16)
                act.dma_start(reset[:], consts[:, C_RESET:C_END]).then_inc(masks_in, 16)
                act.dma_start(nw_row[:], hgrn_norm_w[0:1, :].to_broadcast([P, P])).then_inc(masks_in, 16)
                act.dma_start(mask_f[:], masks).then_inc(mask_f_in, 16)
                act.wait_ge(c_in, 16)
                act.activation(csig, cs, ACT.Sigmoid).then_inc(csig_ready, 1)
                for t in range(TT):
                    act.wait_ge(x_inn[t], 16)
                    act.activation(x_n[:, t, :], x_in[:, t, :], ACT.Square, scale=D ** -0.5,
                                   accum_out=ms[:, t:t + 1]).then_inc(square_x, 1)
                act.wait_ge(square_x, TT)
                act.wait_ge(prepared, 2)
                act.activation(rstd, ms, ACT.Sqrt, bias=eps).then_inc(sqrt_x, 1)
                act.wait_ge(lb_exp_in, 1)
                act.activation(lbt[:, 0:8], lbt[:, 0:8], ACT.Exp).then_inc(lb_exp, 1)
                act.wait_ge(ada0_used, KD)
                for j in range(KD):
                    if j == 0:
                        wait_stage(act, ("w", 0))
                        act.activation(w_hi[:, 0, :], staged(("w", 0)), ACT.Copy).then_inc(hi_done, 1)
                    act.wait_ge(u_ready, j + 1)
                    act.activation(uT_hi[:, j, :], u_full[:, j, :], ACT.Copy).then_inc(u_hi_ready, 1)
                wait_stage(act, ("w", 1))
                act.activation(w_hi[:, 1, :], staged(("w", 1)), ACT.Copy).then_inc(hi_done, 1)

            @block.vector
            def _(dve):
                chain = Chain(dve, dve_step, order)
                dve.wait_ge(csig_ready, 1)
                chain(dve.tensor_tensor(cs, cs, csig, ALU.mult))
                dve.wait_ge(sqrt_x, 1)
                chain(dve.reciprocal(rstd, rstd))
                for t in range(TT):
                    dve.tensor_scalar(x_n[:, t, :], x_in[:, t, :], rstd[:, t:t + 1], None, ALU.mult).then_inc(xn_ready, 1)
                dve.wait_ge(vec_turned, 1)
                chain(dve.tensor_copy(vecT, ps[:, 7, 0:28]))
                chain(dve.tensor_tensor(lbt[:, 8:12], vecT[:, 8:12], vecT[:, 12:16], ALU.max))
                chain(dve.tensor_tensor(lbt[:, 0:4], vecT[:, 8:12], lbt[:, 8:12], ALU.subtract))
                dve.tensor_tensor(lbt[:, 4:8], vecT[:, 12:16], lbt[:, 8:12], ALU.subtract).then_inc(lb_exp_in, 1)
                dve.wait_ge(lb_exp, 1)
                chain(dve.tensor_tensor(lbt[:, 8:12], lbt[:, 0:4], lbt[:, 4:8], ALU.add))
                chain(dve.reciprocal(lbt[:, 12:16], lbt[:, 8:12]))
                chain(dve.tensor_tensor(lb, lbt[:, 0:4], lbt[:, 12:16], ALU.mult))
                chain(dve.tensor_tensor(om_lb, lbt[:, 4:8], lbt[:, 12:16], ALU.mult))
                chain(dve.tensor_scalar(lb, lb, TINY, None, ALU.max))
                dve.wait_ge(ada_bias_in, 16)
                for k in range(KD):
                    dve.wait_ge(ada_in[k], 16)
                    dve.scalar_tensor_tensor(ada0[:], ada0_in[:, k, :], cs[:, k:k + 1], ada0[:], ALU.mult,
                                             ALU.add).then_inc(ada0_used, 1)
                    dve.wait_ge(ada0_used, k + 1)
                for j in range(KD):
                    if j % 2 == 0:
                        dve.wait_ge(mod_sum, j // 2 + 1)
                        b = 6 + j // 2 % 2
                        dve.scalar_tensor_tensor(modT[:, j:j + 2], ps[:, b, 40 + j:42 + j], 1.0, vecT[:, j:j + 2],
                                                 ALU.add, ALU.mult)
                        chain(dve.tensor_copy(modT[:, 8 + j:10 + j], ps[:, b, 32 + j:34 + j]))
                    dve.wait_ge(x_turned, j + 1)
                    dve.tensor_scalar(u_full[:, j, :], ps[:, j % 6, :], modT[:, j:j + 1], modT[:, 8 + j:9 + j],
                                      ALU.mult, ALU.add).then_inc(u_ready, 1)
                dve.wait_ge(hi_done, 1)
                dve.tensor_tensor(w_lo[:, 0, :], staged(("w", 0)), w_hi[:, 0, :].bitcast(F32),
                                  ALU.subtract).then_inc(lo_done, 1)
                dve.wait_ge(u_hi_ready, KD)
                dve.wait_ge(u_ready, KD)
                dve.tensor_tensor(uT_lo[:, KD - 1, :], u_full[:, KD - 1, :], uT_hi[:, KD - 1, :].bitcast(F32),
                                  ALU.subtract)

            @block.tensor
            def _(pe):
                pe.wait_ge(consts_in, 16)
                pe.wait_ge(vec_in, 48)
                pe.transpose(ps[:, 7, 0:28], vec_rows[:], ident[0:28, 0:28]).then_inc(vec_turned, 1)
                pe.wait_ge(xn_ready, TT)

                def turn_x(j):
                    for t in range(TT):
                        mm = pe.transpose(ps[:, j % 6, t * P:(t + 1) * P], x_n[:, t, j * P:(j + 1) * P], ident)
                    mm.then_inc(x_turned, 1)

                for j in range(6):
                    turn_x(j)
                pe.wait_ge(ada0_used, KD)
                pe.wait_ge(dve_step, 3)
                for g in range(KD // 2):
                    if g >= 2:
                        pe.wait_ge(u_ready, 2 * g - 2)
                    for m in (2 * g, 2 * g + 1, KD + 2 * g, KD + 2 * g + 1):
                        mm = pe.matmul(ps[:, 6 + g % 2, 32 + m:33 + m], ada0[:, m * P:(m + 1) * P], ones[:, 0:1],
                                       start=True, stop=True, skip_group_check=True)
                    mm.then_inc(mod_sum, 1)
                    if g >= 2:
                        turn_x(4 + g)

        unit_done = sem("unit_done")
        act_read = sem("act_read")
        dve_read = sem("dve_read")
        sig_f = sem("sig_f")
        k_ready = sem("k_ready")
        logf_ready = sem("logf_ready")
        b_ready = sem("b_ready")
        gsig_ready = sem("gsig_ready")
        g_ready = sem("g_ready")
        elast_ready = sem("elast_ready")
        w_ready = sem("w_ready")
        e_ready = sem("e_ready")
        qd_ready = sem("qd_ready")
        kd_ready = sem("kd_ready")
        dec_used = sem("dec_used")
        diag_done = sem("diag_done")
        sc_read = sem("sc_read")
        ktok_ready = sem("ktok_ready")
        state_sum = sem("state_sum")
        state_ready = sem("state_ready")
        o_sq = sem("o_sq")
        o_ms = sem("o_ms")
        o_rms = sem("o_rms")
        o_ready = sem("o_ready")
        o_read = sem("o_read")
        o_turned = sem("o_turned")
        oT_hi_ready = sem("oT_hi_ready")
        oT_lo_ready = sem("oT_lo_ready")
        dec_zero = sem("dec_zero")
        yc_ready = sem("yc_ready")
        merged_ready = sem("merged_ready")
        ada12_in = sem("ada12_in")

        units = []
        for name, owner in (("f", "act"), ("q", "act"), ("v", "act"), ("g", "dve"), ("cc", "act"), ("ch", "dve"),
                            ("cb", "dve"), ("ga0", "act"), ("ya0", "dve"), ("gb0", "act"), ("yb0", "dve"),
                            ("ga1", "act"), ("ya1", "dve"), ("gb1", "act"), ("yb1", "dve")):
            units += [(name, m, owner) for m in range(4)]
        unit_no = {(name, m): n for n, (name, m, _) in enumerate(units)}

        def bank(name, m):
            return ps[:, unit_no[name, m] % 3, :]

        def reads_upto(n):
            owner = units[n][2]
            return owner, sum(o == owner for _, _, o in units[:n + 1])

        def group_end(n):
            return next(unit_no[name, 3] + 1 for name, chunks in group_chunks.items() if n in chunks)

        def split_view(buf, n):
            return buf[:, n % SPLITS, :].rearrange("p (k n) -> p k n", k=4)

        def exact3(pe, dst, pairs, wait_for=None):
            n = len(pairs)
            for i, (sh, sl, mh, ml) in enumerate(pairs):
                if wait_for:
                    wait_for(i)
                pe.matmul(dst, sh, mh, start=(i == 0), stop=False)
                pe.matmul(dst, sh, ml, start=False, stop=False)
                mm = pe.matmul(dst, sl, mh, start=False, stop=(i == n - 1))
            return mm

        def half(ap, level, which):
            m = 1 << level
            v = ap.rearrange("p h (s two m) -> p h s two m", two=2, m=m)
            return v[:, :, :, which, :]

        def edge(ap, level):
            m = 1 << level
            v = ap.rearrange("p h (s two m) -> p h s two m", two=2, m=m)
            return v[:, :, :, 0, m - 1:m].to_broadcast([P, HEADS, P // (2 * m), m])

        mix_done = sem("mix_done")

        def mix_product(pe, t):
            for n in range(2):
                pairs = []
                for k in range(KD):
                    chunk = group_chunks[f"mix{n}"][k // 4]
                    pairs.append((merged_hi[:, k, t * P:(t + 1) * P], merged_lo[:, k, t * P:(t + 1) * P],
                                  split_view(w_hi, chunk)[:, k % 4, :], split_view(w_lo, chunk)[:, k % 4, :]))
                wait_k = None
                if t == 0:
                    def wait_k(k, n=n):
                        pe.wait_ge(merged_ready, k + 1)
                        pe.wait_ge(lo_done, group_chunks[f"mix{n}"][k // 4] + 1)
                mm = exact3(pe, ps[:, 4 + 2 * (t % 2) + n, :], pairs, wait_k)
            mm.then_inc(mix_done, 1)

        with nc.Block() as block:
            @block.sync
            def _(sp):
                for n in range(2, len(stream)):
                    if n == THIRD_FROM:
                        sp.wait_ge(sc_read, 8 * TT)
                        sp.wait_ge(g_ready, TT)
                    stream_load(sp, n)

            @block.gpsimd
            def _(pool):
                pool.memset(q_dec[:], 0.0).then_inc(dec_zero, 1)
                pool.memset(k_dec[:], 0.0).then_inc(dec_zero, 1)
                pool.wait_ge(k_ready, HEADS)
                pool.wait_ge(masks_in, 32)
                for t in range(TT):
                    for level in range(LEVELS + 1):
                        n = 9 * t + level
                        pool.wait_ge(e_ready, n + 1)
                        if n >= 2:
                            pool.wait_ge(dec_used, n - 1)
                        kk = kT[:, :, t * P:(t + 1) * P]
                        if n < 2:
                            pool.wait_ge(dec_zero, 2)
                        if level < LEVELS:
                            pool.tensor_tensor(half(k_dec[:, n % 2], level, 0), half(kk, level, 0),
                                               half(wdiff[:, n % 2], level, 0), ALU.mult).then_inc(kd_ready, 1)
                        else:
                            pool.tensor_tensor(k_dec[:, n % 2], kk, wdiff[:, n % 2], ALU.mult).then_inc(kd_ready, 1)
                    if t < 2:
                        for m in (0,) if t == 0 else (1, 2, 3):
                            pool.wait_ge(dve_read, m + 1)
                            v = gates[:, m, :].rearrange("p (h d) -> p h d", h=HEADS)
                            pool.tensor_tensor(v, v, nw_row[:, None, :].to_broadcast([P, HEADS, P]),
                                               ALU.mult).then_inc(g_ready, 1)
                pool.wait_ge(oT_lo_ready, TT)
                pool.memset(ada12[:], 0.0).then_inc(dec_zero, 1)
                pool.wait_ge(dec_zero, 3)
                pool.dma_start(ada12[0:1, :, :].rearrange("p a n -> p (a n)"), b_ada[:, CH:3 * CH]).then_inc(ada12_in, 16)
                pool.wait_ge(ada12_in, 16)
                for m in range(2 * KD):
                    pool.wait_ge(ada_scaled, m + 1)
                    if m >= 1:
                        pool.wait_ge(ada_done, m)
                    pool.tensor_tensor(ada12[:, m // KD, :], staged(("ada", m)), ada12[:, m // KD, :],
                                       ALU.add).then_inc(ada_done, 1)

            @block.scalar
            def _(act):

                def scale_ada(m):
                    wait_stage(act, ("ada", m))
                    act.activation(staged(("ada", m)), staged(("ada", m)), ACT.Copy,
                                   scale=cs[:, m % KD:m % KD + 1]).then_inc(ada_scaled, 1)

                def split_hi(n):
                    wait_stage(act, ("w", n))
                    if n >= SPLITS:
                        act.wait_ge(unit_done, group_end(n - SPLITS))
                    act.activation(w_hi[:, n % SPLITS, :], staged(("w", n)), ACT.Copy).then_inc(hi_done, 1)

                def unit(name, m):
                    act.wait_ge(unit_done, unit_no[name, m] + 1)

                def decay(n):
                    t, level = n // 9, n % 9
                    if level == 8:
                        act.wait_ge(kd_ready, 8 * t + 7)
                        act.wait_ge(qd_ready, 8 * t + 7)
                        act.activation(wdiff[:, n % 2], bT[:, :, t * P:(t + 1) * P], ACT.Exp).then_inc(e_ready, 1)
                    else:
                        act.wait_ge(w_ready, 8 * t + level + 1)
                        act.activation(wdiff[:, n % 2], wdiff[:, n % 2], ACT.Exp).then_inc(e_ready, 1)

                for n in range(2, SPLITS):
                    split_hi(n)
                for m in range(HEADS):
                    unit("f", m)
                    act.activation(bT[:, m, :], bank("f", m), ACT.Sigmoid).then_inc(sig_f, 1)
                    act.activation(kT[:, m, :], bank("f", m), ACT.Sigmoid, scale=-1.0).then_inc(act_read, 1)
                for n in refills("f"):
                    split_hi(n)
                for m in range(HEADS):
                    act.wait_ge(sig_f, m + 1)
                    act.activation(bT[:, m, :], bT[:, m, :], ACT.Ln, bias=lb[:, m:m + 1],
                                   scale=om_lb[:, m:m + 1]).then_inc(logf_ready, 1)
                for m in range(HEADS):
                    unit("q", m)
                    act.activation(qT[:, m, :], bank("q", m), ACT.Copy).then_inc(act_read, 1)
                for n in refills("q"):
                    split_hi(n)
                for m in range(TT):
                    unit("v", m)
                    act.activation(v_tok[:, m, :], bank("v", m), ACT.Copy).then_inc(act_read, 1)
                for n in refills("v"):
                    split_hi(n)
                def output_hi(t):
                    act.wait_ge(o_turned, t + 1)
                    act.activation(oT_hi[:, :, t * P:(t + 1) * P], ps[:, 5, :].rearrange("p (h t) -> p h t", h=HEADS),
                                   ACT.Copy).then_inc(oT_hi_ready, 1)

                act.wait_ge(b_ready, HEADS)
                decay(0)
                decay(1)
                for t, name in enumerate(("g", "cc", "ch", "cb")):
                    def filler(m):
                        if name == "g":
                            unit("g", m)
                            if m >= 1:
                                act.wait_ge(dve_read, m)
                            act.activation(g_sig[:], bank("g", m), ACT.Sigmoid).then_inc(gsig_ready, 1)
                        if name == "cc":
                            unit("cc", m)
                            act.activation(cu[:, m, :], bank("cc", m), ACT.Copy).then_inc(act_read, 1)
                    if t >= 1:
                        act.wait_ge(state_ready, t)
                    act.activation(elast, bT[:, :, t * P + P - 1:t * P + P].rearrange("p h o -> p (h o)"),
                                   ACT.Exp).then_inc(elast_ready, 1)
                    if t >= 1:
                        output_hi(t - 1)
                    decay(9 * t + 2)
                    filler(0)
                    for n in (3, 4, 5):
                        decay(9 * t + n)
                    filler(1)
                    for n in (6, 7, 8):
                        decay(9 * t + n)
                    filler(2)
                    act.wait_ge(dec_used, 9 * t + 8)
                    if t >= 1:
                        act.wait_ge(state_sum, t)
                    act.activation(k_tok[:].rearrange("p h d -> p (h d)"), ps[:, 5, :], ACT.Copy).then_inc(ktok_ready, 1)
                    act.wait_ge(dec_used, 9 * t + 9)
                    if t >= 1:
                        act.wait_ge(o_turned, t)
                    act.activation(o_norm[:].rearrange("p h d -> p (h d)"), ps[:, 6, :], ACT.Square,
                                   scale=P ** -0.5).then_inc(o_sq, 1)
                    if t < TT - 1:
                        decay(9 * t + 9)
                    act.wait_ge(o_ms, t + 1)
                    act.activation(hrs, hms, ACT.Sqrt, bias=eps).then_inc(o_rms, 1)
                    if t < TT - 1:
                        decay(9 * t + 10)
                    filler(3)
                    for n in refills(name):
                        split_hi(n)
                output_hi(TT - 1)
                act.wait_ge(oT_lo_ready, TT)
                for r, (gate, product) in enumerate(LATE):
                    sg = sg_a if r % 2 == 0 else sg_b
                    for m in range(4):
                        unit(gate, m)
                        if r >= 2:
                            act.wait_ge(merged_ready, m + 1)
                        act.activation(sg[:, m, :], bank(gate, m), ACT.Sigmoid).then_inc(act_read, 1)
                        if m < 3:
                            scale_ada(4 * r + m)
                    for n in refills(gate):
                        split_hi(n)
                    scale_ada(4 * r + 3)
                    for n in refills(product):
                        split_hi(n)

            @block.vector
            def _(dve):
                chain = Chain(dve, dve_step, order)

                def split_lo(n):
                    dve.wait_ge(hi_done, n + 1)
                    dve.tensor_tensor(w_lo[:, n % SPLITS, :], staged(("w", n)),
                                      w_hi[:, n % SPLITS, :].bitcast(F32), ALU.subtract).then_inc(lo_done, 1)

                def unit(name, m):
                    dve.wait_ge(unit_done, unit_no[name, m] + 1)

                for n in range(1, SPLITS):
                    split_lo(n)
                dve.wait_ge(masks_in, 32)
                dve.wait_ge(prepared, 3)
                for m in range(HEADS):
                    dve.wait_ge(act_read, m + 1)
                    dve.tensor_scalar(kT[:, m, :], kT[:, m, :], om_lb[:, m:m + 1], None, ALU.mult).then_inc(k_ready, 1)
                for n in refills("f"):
                    split_lo(n)
                for m in range(HEADS):
                    dve.wait_ge(logf_ready, m + 1)
                    dve.tensor_tensor_scan(bT[:, m, :], reset[:], bT[:, m, :], 0.0, ALU.mult, ALU.add).then_inc(b_ready, 1)
                for n in refills("q"):
                    split_lo(n)
                for n in refills("v"):
                    split_lo(n)
                dve.wait_ge(b_ready, HEADS)
                dve.wait_ge(act_read, 3 * HEADS)
                dve.wait_ge(dec_zero, 2)

                def diff(t, level):
                    n = 9 * t + level
                    if n >= 2:
                        p = 9 * t + level - 2
                        dve.wait_ge(qd_ready, sum(x % 9 != 7 for x in range(p + 1)))
                        dve.wait_ge(kd_ready, sum(x % 9 != 8 for x in range(p + 1)))
                    b = bT[:, :, t * P:(t + 1) * P]
                    w = wdiff[:, n % 2]
                    if level < LEVELS:
                        chain(dve.tensor_tensor(half(w, level, 1), half(b, level, 1), edge(b, level), ALU.subtract))
                        dve.tensor_tensor(half(w, level, 0), edge(b, level), half(b, level, 0),
                                          ALU.subtract).then_inc(w_ready, 1)
                    else:
                        dve.tensor_tensor(w, b[:, :, P - 1:P].to_broadcast([P, HEADS, P]), b,
                                          ALU.subtract).then_inc(w_ready, 1)

                def q_decay(t, level):
                    n = 9 * t + level
                    dve.wait_ge(e_ready, n + 1)
                    if n >= 2:
                        dve.wait_ge(dec_used, n - 1)
                    qq = qT[:, :, t * P:(t + 1) * P]
                    if level < LEVELS:
                        dve.tensor_tensor(half(q_dec[:, n % 2], level, 1), half(qq, level, 1),
                                          half(wdiff[:, n % 2], level, 1), ALU.mult).then_inc(qd_ready, 1)
                    else:
                        dve.tensor_tensor(q_dec[:, n % 2], qq, wdiff[:, n % 2], ALU.mult).then_inc(qd_ready, 1)

                def take_scores(t, level):
                    dve.wait_ge(dec_used, 9 * t + level + 1)
                    dve.wait_ge(sc_read, 8 * t + level + 1)
                    b = 3 + (8 * t + level + 1) % 2
                    dve.copy_predicated(scores[:], mask_sb[:, level, None, :].to_broadcast([P, HEADS, P]),
                                        ps[:, b, :].rearrange("p (h t) -> p h t", h=HEADS)).then_inc(sc_read, 1)

                def output_lo(t):
                    dve.wait_ge(oT_hi_ready, t + 1)
                    dve.tensor_tensor(oT_lo[:, :, t * P:(t + 1) * P], ps[:, 5, :].rearrange("p (h t) -> p h t", h=HEADS),
                                      oT_hi[:, :, t * P:(t + 1) * P].bitcast(F32), ALU.subtract).then_inc(oT_lo_ready, 1)

                for t, name in enumerate(("g", "cc", "ch", "cb")):
                    def filler(m):
                        if name == "g":
                            unit("g", m)
                            dve.wait_ge(gsig_ready, m + 1)
                            dve.tensor_tensor(gates[:, m, :], bank("g", m), g_sig[:], ALU.mult).then_inc(dve_read, 1)
                        if name == "ch":
                            unit("ch", m)
                            dve.tensor_tensor(cu[:, m, :], bank("ch", m), cu[:, m, :], ALU.mult).then_inc(dve_read, 1)
                        if name == "cb":
                            tap = lambda k: vecT[:, 16 + 4 * k + m:17 + 4 * k + m]
                            dve.wait_ge(dve_read, 8 + m)
                            chain(dve.tensor_scalar(y_tmp[:], cu[:, m, :], tap(2), None, ALU.mult))
                            chain(dve.scalar_tensor_tensor(y_tmp[:, 1:], cu[:, m, 0:TOKENS - 1], tap(1), y_tmp[:, 1:],
                                                           ALU.mult, ALU.add))
                            chain(dve.scalar_tensor_tensor(y_tmp[:, 2:], cu[:, m, 0:TOKENS - 2], tap(0), y_tmp[:, 2:],
                                                           ALU.mult, ALU.add))
                            unit("cb", m)
                            dve.tensor_tensor(y_tmp[:], y_tmp[:], bank("cb", m), ALU.mult).then_inc(dve_read, 1)
                            dve.wait_ge(dve_read, 9 + m)
                            chain(dve.tensor_copy(yc_hi[:, m, :], y_tmp[:]))
                            dve.tensor_tensor(yc_lo[:, m, :], y_tmp[:], yc_hi[:, m, :].bitcast(F32),
                                              ALU.subtract).then_inc(yc_ready, 1)
                            dve.wait_ge(yc_ready, m + 1)
                    if t == 0:
                        diff(t, 0)
                        diff(t, 1)
                    dve.wait_ge(diag_done, t + 1)
                    if t >= 1:
                        dve.wait_ge(dec_used, 9 * t)
                    dve.tensor_tensor(scores[:], ps[:, 3 + (8 * t) % 2, :].rearrange("p (h t) -> p h t", h=HEADS),
                                      ident[:, None, :].to_broadcast([P, HEADS, P]), ALU.mult).then_inc(sc_read, 1)
                    q_decay(t, 0)
                    for level in range(2, 8):
                        diff(t, level)
                        q_decay(t, level - 1)
                        take_scores(t, level - 2)
                        if level == 2 and t >= 1:
                            output_lo(t - 1)
                        if level in (3, 5, 7):
                            filler(level // 2 - 1)
                    q_decay(t, 8)
                    take_scores(t, 6)
                    if t < TT - 1:
                        diff(t + 1, 0)
                        diff(t + 1, 1)
                    dve.wait_ge(o_sq, t + 1)
                    dve.tensor_reduce(hms, o_norm[:], AX.X, ALU.add).then_inc(o_ms, 1)
                    dve.wait_ge(g_ready, t + 1)
                    dve.wait_ge(o_ms, t + 1)
                    dve.tensor_tensor(o_norm[:].rearrange("p h d -> p (h d)"), ps[:, 6, :], gates[:, t, :],
                                      ALU.mult).then_inc(o_read, 1)
                    dve.wait_ge(o_rms, t + 1)
                    chain(dve.reciprocal(hrs, hrs))
                    dve.wait_ge(o_read, t + 1)
                    dve.tensor_tensor(o_norm[:], o_norm[:], hrs[:, :, None].to_broadcast([P, HEADS, P]),
                                      ALU.mult).then_inc(o_ready, 1)
                    if t < TT - 1:
                        dve.wait_ge(state_sum, t + 1)
                        dve.wait_ge(elast_ready, t + 1)
                        for h in range(HEADS):
                            src = ps[:, 7, h * P:(h + 1) * P]
                            if t == 0:
                                ins = dve.tensor_copy(state[:, h, :], src)
                            else:
                                ins = dve.scalar_tensor_tensor(state[:, h, :], state[:, h, :], elast[:, h:h + 1], src,
                                                               ALU.mult, ALU.add)
                        ins.then_inc(state_ready, 1)
                    filler(3)
                    for n in refills(name):
                        split_lo(n)
                output_lo(TT - 1)
                for r, (gate, product) in enumerate(LATE):
                    first, *second = refills(gate)
                    split_lo(first)
                    for m in range(4):
                        unit(product, m)
                        reads = reads_upto(unit_no[product, m])[1]
                        if r % 2 == 0:
                            dve.tensor_tensor(sg_a[:, m, :], bank(product, m), sg_a[:, m, :],
                                              ALU.mult).then_inc(dve_read, 1)
                        else:
                            j = 4 * (r // 2) + m
                            dve.tensor_tensor(sg_b[:, m, :], bank(product, m), sg_b[:, m, :],
                                              ALU.mult).then_inc(dve_read, 1)
                            dve.wait_ge(dve_read, reads)
                            chain(dve.tensor_tensor(sg_b[:, m, :], sg_b[:, m, :], sg_a[:, m, :], ALU.add))
                            chain(dve.tensor_copy(merged_hi[:, j, :], sg_b[:, m, :]))
                            dve.tensor_tensor(merged_lo[:, j, :], sg_b[:, m, :], merged_hi[:, j, :].bitcast(F32),
                                              ALU.subtract).then_inc(merged_ready, 1)
                        if m == 0:
                            for n in second:
                                split_lo(n)
                    for n in refills(product):
                        split_lo(n)

            @block.tensor
            def _(pe):
                def begin(name, m):
                    n = unit_no[name, m]
                    if n >= 3:
                        owner, reads = reads_upto(n - 3)
                        pe.wait_ge(act_read if owner == "act" else dve_read, reads)

                def part(name, m, ks):
                    chunks = group_chunks[name]
                    n = unit_no[name, m]
                    dst = bank(name, m)
                    for k in ks:
                        if m == 0:
                            pe.wait_ge(lo_done, chunks[k // 4] + 1)
                        wh = split_view(w_hi, chunks[k // 4])[:, k % 4, :]
                        wl = split_view(w_lo, chunks[k // 4])[:, k % 4, :]
                        first, last = k == 0, k == KD - 1
                        if name in ("v", "g"):
                            sh, sl = uT_hi[:, k, m * P:(m + 1) * P], uT_lo[:, k, m * P:(m + 1) * P]
                            mh, ml = wh, wl
                        else:
                            sh, sl = wh[:, m * P:(m + 1) * P], wl[:, m * P:(m + 1) * P]
                            mh, ml = uT_hi[:, k, :], uT_lo[:, k, :]
                        pe.matmul(dst, sh, mh, start=first, stop=False)
                        pe.matmul(dst, sh, ml, start=False, stop=False)
                        mm = pe.matmul(dst, sl, mh, start=False, stop=last)
                    if ks[-1] == KD - 1:
                        mm.then_inc(unit_done, 1)

                def group(name, last_output=None):
                    for m in range(4):
                        begin(name, m)
                        part(name, m, range(KD))
                        if m == 0 and last_output:
                            last_output(TT - 1)

                def narrow_group(name, hi, lo):
                    chunk = group_chunks[name][0]
                    pe.wait_ge(lo_done, chunk + 1)
                    for m in range(4):
                        begin(name, m)
                        pairs = [(split_view(w_hi, chunk)[:, k, m * P:(m + 1) * P],
                                  split_view(w_lo, chunk)[:, k, m * P:(m + 1) * P], hi[:, k, :], lo[:, k, :])
                                 for k in range(4)]
                        exact3(pe, bank(name, m), pairs).then_inc(unit_done, 1)

                def diagonal(t):
                    i = 8 * t
                    if i >= 2:
                        pe.wait_ge(sc_read, i - 1)
                    for h in range(HEADS):
                        mm = pe.matmul(ps[:, 3 + i % 2, h * P:(h + 1) * P], kT[:, h, t * P:(t + 1) * P],
                                       qT[:, h, t * P:(t + 1) * P], start=(h == 0), stop=True, skip_group_check=True)
                    mm.then_inc(diag_done, 1)

                def step(t, level):
                    n = 9 * t + level
                    pe.wait_ge(kd_ready, sum(v % 9 != 8 for v in range(n + 1)))
                    pe.wait_ge(qd_ready, sum(v % 9 != 7 for v in range(n + 1)))
                    i = 8 * t + level + 1
                    if level < LEVELS:
                        pe.wait_ge(sc_read, i - 1)
                        for h in range(HEADS):
                            mm = pe.matmul(ps[:, 3 + i % 2, h * P:(h + 1) * P], k_dec[:, n % 2, h, :],
                                           q_dec[:, n % 2, h, :], start=(h == 0), stop=True, skip_group_check=True)
                    elif level == 7:
                        if t >= 1:
                            pe.wait_ge(oT_lo_ready, t)
                        for h in range(HEADS):
                            mm = pe.transpose(ps[:, 5, h * P:(h + 1) * P], k_dec[:, n % 2, h, :], ident)
                    else:
                        pe.wait_ge(sc_read, 8 * (t + 1))
                        if t >= 1:
                            pe.wait_ge(o_read, t)
                            pe.wait_ge(state_ready, t)
                        for h in range(HEADS):
                            dst = ps[:, 6, h * P:(h + 1) * P]
                            mm = pe.matmul(dst, scores[:, h, :], v_tok[:, t, h * P:(h + 1) * P], start=(h == 0),
                                           stop=(t == 0), skip_group_check=True)
                            if t >= 1:
                                mm = pe.matmul(dst, q_dec[:, n % 2, h, :], state[:, h, :], start=False, stop=True,
                                               skip_group_check=True)
                    mm.then_inc(dec_used, 1)

                def new_state(t):
                    pe.wait_ge(ktok_ready, t + 1)
                    if t >= 1:
                        pe.wait_ge(state_ready, t)
                    for h in range(HEADS):
                        mm = pe.matmul(ps[:, 7, h * P:(h + 1) * P], k_tok[:, h, :], v_tok[:, t, h * P:(h + 1) * P],
                                       start=(h == 0), stop=True, skip_group_check=True)
                    mm.then_inc(state_sum, 1)

                def turn_output(t):
                    pe.wait_ge(o_ready, t + 1)
                    pe.wait_ge(ktok_ready, t + 1)
                    for h in range(HEADS):
                        mm = pe.transpose(ps[:, 5, h * P:(h + 1) * P], o_norm[:, h, :], ident)
                    mm.then_inc(o_turned, 1)

                group("f")
                group("q")
                group("v")
                pe.wait_ge(k_ready, HEADS)
                pe.wait_ge(act_read, 3 * HEADS)
                for t, name in enumerate(("g", "cc", "ch", "cb")):
                    for m in range(4):
                        begin(name, m)
                        part(name, m, range(0, 3))
                        if m == 0:
                            diagonal(t)
                        elif m == 3:
                            step(t, 8)
                        else:
                            step(t, 3 * m - 1)
                        part(name, m, range(3, 6))
                        if m == 0 and t >= 1:
                            turn_output(t - 1)
                        if m == 3:
                            new_state(t)
                        else:
                            step(t, 3 * m)
                        part(name, m, range(6, 8))
                        if m < 3:
                            step(t, 3 * m + 1)
                for h in range(2):
                    group(f"ga{h}", turn_output if h == 0 else None)
                    pe.wait_ge(oT_lo_ready, TT)
                    narrow_group(f"ya{h}", oT_hi, oT_lo)
                    group(f"gb{h}")
                    pe.wait_ge(yc_ready, 4)
                    narrow_group(f"yb{h}", yc_hi, yc_lo)
                for t in range(2):
                    mix_product(pe, t)

        bias_in = sem("bias_in")
        bias_zero = sem("bias_zero")
        bias_hi = sem("bias_hi")
        bias_ready = sem("bias_ready")
        raw_in = [sem(f"raw_in{s}") for s in range(RAWS)]
        x_hi_done = sem("x_hi_done")
        x_lo_012 = sem("x_lo_012")
        x_lo_3 = sem("x_lo_3")
        x_used = sem("x_used")

        def known(v):
            return type(v) is int

        def lo_wait(eng, i, off):
            quad = 3 * i + off // 4
            if off % 4 == 3:
                eng.wait_ge(x_lo_3, quad + 1)
            else:
                eng.wait_ge(x_lo_012, 3 * quad + off % 4 + 1)

        def expert_load(eng, i, off, expert, part, j):
            if not known(i) or 12 * i + off >= RAWS:
                lo_wait(eng, i, off - RAWS)
            slot = off % RAWS
            one = bass.ds(expert, 1)
            if part == "w1":
                src = w1[0, one, j * P:(j + 1) * P, :].rearrange("e p n -> p (e n)")
                dst = raw[:, slot, :]
            else:
                src = w2[0, one, 2 * j * P:2 * (j + 1) * P, :].rearrange("e (k p) n -> p (e k) n", p=P)
                dst = raw[:, slot, :].rearrange("p (k n) -> p k n", k=2)
            eng.dma_start(dst, src).then_inc(raw_in[slot], 16)

        row_sum = sem("row_sum")
        row_ready_a = sem("row_ready_a")
        row_ready_v = sem("row_ready_v")
        wf_in = sem("wf_in")
        wr_in = sem("wr_in")
        xt_in = [sem(f"xt_in{s}") for s in range(2)]
        mix_read = sem("mix_read")
        h2_ready = sem("h2_ready")
        h2_sq = sem("h2_sq")
        h2_rms = sem("h2_rms")
        u2_ready = sem("u2_ready")
        u2_turned = sem("u2_turned")
        u2T_ready = sem("u2T_ready")
        routed = sem("routed")
        pexp_in = sem("pexp_in")
        pexp = sem("pexp")
        chosen_ready = sem("chosen_ready")
        counted = sem("counted")
        nex_ready = sem("nex_ready")
        nex_sum = sem("nex_sum")
        mex_ready = sem("mex_ready")
        mex_sum = sem("mex_sum")
        logits_read = sem("logits_read")
        columns_ready = sem("columns_ready")
        slot_row_ready = sem("slot_row_ready")
        slot_ready = sem("slot_ready")
        slot_used = sem("slot_used")
        stored_h = [sem(f"stored_h{s}") for s in range(2)]
        stored_u = [sem(f"stored_u{s}") for s in range(2)]

        with nc.Block() as block:
            @block.sync
            def _(sp):
                def store(sp, t):
                    sp.wait_ge(h2_ready, t + 1)
                    sp.dma_start(h2_d[t * P:(t + 1) * P, :], h2[:, t % 2, :]).then_inc(stored_h[t % 2], 16)
                    sp.wait_ge(u2_ready, t + 1)
                    sp.dma_start(u2_d[t * P:(t + 1) * P, :], u2[:, t % 2, :]).then_inc(stored_u[t % 2], 16)

                sp.dma_start(wf_row[:], norm_ffn_w[0:1, :].to_broadcast([P, D])).then_inc(wf_in, 16)
                sp.dma_start(wr[:], w_router[0].rearrange("(k p) e -> p k e", p=P)).then_inc(wr_in, 16)
                sp.dma_start(br[:], b_router).then_inc(wr_in, 16)
                for t in range(2):
                    sp.dma_start(x_t[:, t, :], x2[t * P:(t + 1) * P, :]).then_inc(xt_in[t], 16)
                for half_ in range(2):
                    sp.dma_start(b1_raw[32 * half_:32 * half_ + E, :], b1[0]).then_inc(bias_in, 16)
                    sp.dma_start(b2_raw[32 * half_:32 * half_ + E, :], b2[0]).then_inc(bias_in, 16)
                for j in range(4):
                    expert_load(sp, 0, j, 0, "w1", j)
                for t in range(2, TT):
                    sp.wait_ge(h2_ready, t - 1)
                    sp.dma_start(x_t[:, t % 2, :], x2[t * P:(t + 1) * P, :]).then_inc(xt_in[t % 2], 16)
                    store(sp, t - 2)
                store(sp, TT - 2)
                sp.wait_ge(row_ready_v, 1)
                sp.wait_ge(bias_ready, 2)
                for j in range(4, 6):
                    expert_load(sp, 0, j, 0, "w1", j)
                sp.wait_ge(mix_done, TT)
                for j in range(6, 8):
                    expert_load(sp, 0, j, 0, "w1", j)
                for j in range(2):
                    expert_load(sp, 1, -4 + j, 1, "w1", j)
                store(sp, TT - 1)
                expert_load(sp, 1, -2, 1, "w1", 2)
                for j in range(4, 6):
                    expert_load(sp, 1, -4 + j, 1, "w1", j)
                for s in range(2):
                    sp.wait_ge(stored_h[s], 16 * TT // 2)
                    sp.wait_ge(stored_u[s], 16 * TT // 2)

            @block.gpsimd
            def _(pool):
                pool.memset(bias1[64:P, :].bitcast(F32), 0.0).then_inc(bias_zero, 1)
                pool.memset(bias2[64:P, :].bitcast(F32), 0.0).then_inc(bias_zero, 1)
                pool.wait_ge(bias_zero, 2)
                pool.wait_ge(bias_hi, 2)
                pool.tensor_tensor(bias1[32:64, :], b1_raw[32:64, :], bias1[32:64, :].bitcast(F32),
                                   ALU.subtract).then_inc(bias_ready, 1)
                pool.tensor_tensor(bias2[32:64, :], b2_raw[32:64, :], bias2[32:64, :].bitcast(F32),
                                   ALU.subtract).then_inc(bias_ready, 1)
                pool.wait_ge(bias_ready, 2)
                pool.memset(hs[:], 0.0).then_inc(bias_ready, 1)
                for g in range(2):
                    pool.wait_ge(x_hi_done, g + 1)
                    pool.tensor_tensor(w_lo[:, g, :], raw[:, g, :], w_hi[:, g, :].bitcast(F32),
                                       ALU.subtract).then_inc(x_lo_012, 1)
                pool.wait_ge(columns_ready, 1)
                for j in range(TT * TOP):
                    if j >= 2:
                        pool.wait_ge(slot_used, j - 1)
                    pool.tensor_scalar(slot_row[:, j % 2, :], iota, pos[:, j:j + 1], None,
                                       ALU.is_equal).then_inc(slot_row_ready, 1)

            @block.scalar
            def _(act):
                def bias_hi_part(dst, src):
                    act.wait_ge(bias_in, 64)
                    act.activation(dst[0:64, :], src[0:64, :], ACT.Copy).then_inc(bias_hi, 1)

                for r in (0, 1, 3):
                    act.wait_ge(row_sum, r + 1)
                    b = 2 * (r % 2)
                    act.activation(gate_f[:] if r == 3 else rows[:, r, :], ps[:, b:b + 2, :].rearrange("p b n -> p (b n)"),
                                   ACT.Copy).then_inc(row_ready_a, 1)

                def mean_square(t):
                    act.wait_ge(h2_ready, t + 1)
                    if t >= 1:
                        act.wait_ge(u2_ready, t)
                    act.activation(tmp_j[:], h2[:, t % 2, :], ACT.Square, scale=D ** -0.5,
                                   accum_out=ms[:, t:t + 1]).then_inc(h2_sq, 1)
                    act.wait_ge(h2_sq, t + 1)
                    act.activation(rstd[:, t:t + 1], ms[:, t:t + 1], ACT.Sqrt, bias=eps).then_inc(h2_rms, 1)

                def copy_u2T(t):
                    act.wait_ge(u2_turned, t + 1)
                    if t >= 1:
                        act.wait_ge(routed, t)
                    act.activation(u2T[:], ps[:, 0:2, :].rearrange("p b n -> p (b n)"), ACT.Copy).then_inc(u2T_ready, 1)

                def split_hi(g):
                    act.wait_ge(mix_done, TT)
                    act.wait_ge(raw_in[g], 16)
                    act.activation(w_hi[:, g, :], raw[:, g, :], ACT.Copy).then_inc(x_hi_done, 1)

                mean_square(0)
                mean_square(1)
                bias_hi_part(bias1, b1_raw)
                bias_hi_part(bias2, b2_raw)
                copy_u2T(0)
                mean_square(2)
                copy_u2T(1)
                mean_square(3)
                copy_u2T(2)
                split_hi(0)
                copy_u2T(3)
                split_hi(1)
                act.wait_ge(pexp_in, 1)
                act.activation(prob, prob, ACT.Exp).then_inc(pexp, 1)
                split_hi(2)
                split_hi(3)

            @block.vector
            def _(dve):
                chain = Chain(dve, dve_step, order)
                dve.wait_ge(row_sum, 3)
                dve.wait_ge(wf_in, 16)
                dve.scalar_tensor_tensor(rows[:, 2, :], ps[:, 0:2, :].rearrange("p b n -> p (b n)"), 1.0, wf_row[:],
                                         ALU.add, ALU.mult).then_inc(row_ready_v, 1)
                dve.wait_ge(row_ready_v, 1)
                dve.wait_ge(row_ready_a, 2)

                def join(t):
                    b = 4 + 2 * (t % 2)
                    dve.wait_ge(mix_done, t + 1)
                    if t >= 2:
                        dve.wait_ge(stored_h[t % 2], 16 * (t // 2))
                        dve.wait_ge(stored_u[t % 2], 16 * (t // 2))
                        dve.wait_ge(u2_turned, t - 1)
                    dve.tensor_tensor(h2[:, t % 2, :], ps[:, b:b + 2, :].rearrange("p b n -> p (b n)"), rows[:, 0, :],
                                      ALU.mult).then_inc(mix_read, 1)
                    dve.wait_ge(mix_read, t + 1)
                    dve.wait_ge(xt_in[t % 2], 16 * (t // 2 + 1))
                    dve.tensor_tensor(h2[:, t % 2, :], h2[:, t % 2, :], x_t[:, t % 2, :], ALU.add).then_inc(h2_ready, 1)
                    dve.wait_ge(h2_rms, t + 1)
                    chain(dve.reciprocal(rstd[:, t:t + 1], rstd[:, t:t + 1]))
                    chain(dve.scalar_tensor_tensor(u2[:, t % 2, :], h2[:, t % 2, :], rstd[:, t:t + 1], rows[:, 2, :],
                                                   ALU.mult, ALU.mult))
                    dve.tensor_tensor(u2[:, t % 2, :], u2[:, t % 2, :], rows[:, 1, :], ALU.add).then_inc(u2_ready, 1)

                def top(t):
                    dve.wait_ge(routed, t + 1)
                    dve.tensor_copy(lg[:], ps[:, 2 + t % 2, 0:E]).then_inc(logits_read, 1)
                    dve.wait_ge(logits_read, t + 1)
                    chain(dve.max(val8[:, t, :], lg[:]))
                    chain(dve.max_index(idx8[:], val8[:, t, :], lg[:]))
                    chain(dve.tensor_copy(idxf[:, t, :], idx8[:]))
                    chain(dve.tensor_tensor(
                        onehot[:, t], idxf[:, t, 0:TOP, None].to_broadcast([P, TOP, E]),
                        iota[:, None, 0:E].to_broadcast([P, TOP, E]), ALU.is_equal))
                    dve.tensor_reduce(chosen[:, t, :], onehot[:, t].rearrange("p k e -> p e k"), AX.X,
                                      ALU.add).then_inc(chosen_ready, 1)

                chain(dve.tensor_copy(vv[:, 0, :], const[:, C_ROW:C_ROW + 16]))
                chain(dve.memset(btf[:], 0.0))
                chain(dve.tensor_copy(btf[:, 0:E], iota[0:1, 0:E]))
                chain(dve.tensor_scalar(btf[:, MAX_BLOCKS:MAX_BLOCKS + E], iota[0:1, 0:E], 4.0, None, ALU.mult))
                chain(dve.memset(mex[:], 0.0))
                join(0)
                join(1)
                top(0)
                join(2)
                join(3)
                top(1)
                top(2)
                top(3)
                dve.tensor_tensor(prob, val8[:, :, 0:TOP], val8[:, :, 0:1].to_broadcast([P, TT, TOP]),
                                  ALU.subtract).then_inc(pexp_in, 1)
                dve.wait_ge(pexp, 1)
                chain(dve.tensor_reduce(psm, prob, AX.X, ALU.add))
                chain(dve.reciprocal(prc, psm))
                chain(dve.tensor_tensor(vv[:, 1, :].rearrange("p (t k) -> p t k", k=TOP), prob,
                                        prc[:, :, None].to_broadcast([P, TT, TOP]), ALU.mult))
                dve.wait_ge(counted, 1)
                chain(dve.tensor_tensor(
                    onehot[:], onehot[:],
                    ps[:, 4, 0:TT * E].rearrange("p (t e) -> p t e", e=E)[:, :, None, :].to_broadcast([P, TT, TOP, E]),
                    ALU.mult))
                chain(dve.tensor_reduce(pos.rearrange("p (t k) -> p t k", k=TOP), onehot[:], AX.X, ALU.add))
                for b in range(3):
                    chain(dve.tensor_scalar(ge[:, b, :], pos, 128.0 * (b + 1), None, ALU.is_ge))
                chain(dve.tensor_tensor(blk, ge[:, 0, :], ge[:, 1, :], ALU.add))
                chain(dve.tensor_tensor(blk, blk, ge[:, 2, :], ALU.add))
                dve.scalar_tensor_tensor(pos, blk, -128.0, pos, ALU.mult, ALU.add).then_inc(columns_ready, 1)
                chain(dve.scalar_tensor_tensor(qcol.rearrange("p (t k) -> p t k", k=TOP), idxf[:, :, 0:TOP], 4.0,
                                               blk.rearrange("p (t k) -> p t k", k=TOP), ALU.mult, ALU.add))

                def extra_counts():
                    for b in range(3):
                        chain(dve.tensor_scalar(cnt[:, 1 + b:2 + b], ps[0:E, 4, 160:161], 128.0 * (b + 1), None, ALU.is_gt))
                    chain(dve.tensor_tensor(cnt[:, 4:5], cnt[:, 1:2], cnt[:, 2:3], ALU.add))
                    dve.tensor_tensor(cnt[:, 4:5], cnt[:, 4:5], cnt[:, 3:4], ALU.add).then_inc(nex_ready, 1)

                def extra_block(b):
                    if b == 0:
                        dve.wait_ge(nex_sum, 1)
                        chain(dve.tensor_copy(cnt[:, 0:1], ps[0:E, 5, 0:1]))
                    chain(dve.tensor_scalar(cnt[:, 5:6], cnt[:, 0:1], float(b), None, ALU.add))
                    chain(dve.tensor_scalar(mtmp[:, 0, :], iota[0:E, 0:MAX_EXTRA], cnt[:, 5:6], cnt[:, 1 + b:2 + b],
                                            ALU.is_equal, ALU.mult))
                    chain(dve.tensor_scalar(mtmp[:, 1, :], mtmp[:, 0, :], float(b + 1), None, ALU.mult))
                    ins = dve.tensor_tensor(mex[:], mex[:], mtmp[:], ALU.add)
                    if b < 2:
                        chain(ins)
                    else:
                        ins.then_inc(mex_ready, 1)

                for j in range(16):
                    if j == 3:
                        extra_counts()
                    if j in (9, 11, 13):
                        extra_block((j - 9) // 2)
                    if j >= 2:
                        dve.wait_ge(slot_used, j - 1)
                    for a in range(2):
                        ins = dve.tensor_scalar(slot_col[:, j % 2, a, :], iota, qcol[:, j:j + 1], vv[:, a, j:j + 1],
                                                ALU.is_equal, ALU.mult)
                    ins.then_inc(slot_ready, 1)
                dve.wait_ge(stored_h[0], 16 * TT // 2)
                dve.wait_ge(stored_h[1], 16 * TT // 2)
                dve.wait_ge(mex_sum, 1)
                chain(dve.tensor_copy(btf[:, E:MAX_BLOCKS], ps[0:1, 5, 64:64 + MAX_EXTRA]))
                chain(dve.tensor_copy(btf[:, MAX_BLOCKS + E:2 * MAX_BLOCKS], ps[0:1, 5, 96:96 + MAX_EXTRA]))
                chain(dve.tensor_copy(btf[:, 2 * MAX_BLOCKS:2 * MAX_BLOCKS + 1], ps[0:1, 5, 32:33]))
                chain(dve.tensor_copy(bt[:], btf[:]))
                dve.wait_ge(slot_used, 16)
                chain(dve.tensor_scalar(tabI[:, 1, :], ps[:, 3, 0:P], UNFILLED, None, ALU.add))
                chain(dve.tensor_scalar(tabI[:, 0, :], tabI[:, 1, :], 2, None, ALU.logical_shift_right))
                chain(dve.tensor_copy(tabW[:], ps[:, 3, P:2 * P]))

            @block.tensor
            def _(pe):
                for r in range(4):
                    if r >= 2:
                        pe.wait_ge(row_ready_a, r - 1)
                    for n in range(2):
                        mm = pe.matmul(ps[:, 2 * (r % 2) + n, :], ones,
                                       ada12[:, r // 2, (r % 2) * D + n * 512:(r % 2) * D + (n + 1) * 512], start=True,
                                       stop=True)
                    mm.then_inc(row_sum, 1)

                def route(t):
                    pe.wait_ge(u2_ready, t + 1)
                    if t >= 1:
                        pe.wait_ge(u2T_ready, t)
                    for k in range(KD):
                        mm = pe.transpose(ps[:, k // 4, (k % 4) * P:(k % 4 + 1) * P], u2[:, t % 2, k * P:(k + 1) * P],
                                          ident)
                    mm.then_inc(u2_turned, 1)
                    pe.wait_ge(u2T_ready, t + 1)
                    if t == 0:
                        pe.wait_ge(row_ready_a, 3)
                        pe.wait_ge(wr_in, 32)
                    if t >= 2:
                        pe.wait_ge(logits_read, t - 1)
                    dst = ps[:, 2 + t % 2, 0:E]
                    pe.matmul(dst, ones[0:1, :], br[:], start=True, stop=False, skip_group_check=True)
                    for k in range(KD):
                        mm = pe.matmul(dst, u2T[:, k * P:(k + 1) * P], wr[:, k, :], start=False, stop=(k == KD - 1),
                                       skip_group_check=True)
                    mm.then_inc(routed, 1)

                def mix_tile(t):
                    pe.wait_ge(mix_read, t - 1)
                    mix_product(pe, t)

                mix_tile(2)
                route(0)
                mix_tile(3)
                route(1)
                route(2)
                route(3)
                def count(t, s):
                    return pe.matmul(ps[:, 4, t * E:(t + 1) * E], tri if s == t else ones, chosen[:, s, :],
                                     start=(t == 0), stop=(s == t), skip_group_check=True)

                def total(s):
                    return pe.matmul(ps[0:E, 4, 160:161], chosen[:, s, :], ones[:, 0:1], start=False,
                                     stop=(s == TT - 1), skip_group_check=True)

                pe.wait_ge(mix_read, TT)
                pe.wait_ge(chosen_ready, TT - 1)
                for t in range(TT):
                    for s in range(min(t + 1, TT - 1)):
                        count(t, s)
                for s in range(TT - 1):
                    total(s)
                pe.wait_ge(chosen_ready, TT)
                count(TT - 1, TT - 1)
                mm = total(TT - 1)
                mm.then_inc(counted, 1)
                for j in range(16):
                    if j == 6:
                        pe.wait_ge(nex_ready, 1)
                        pe.matmul(ps[0:E, 5, 0:1], tri[0:E, 0:E], cnt[:, 4:5], start=True, stop=True,
                                  skip_group_check=True)
                        pe.matmul(ps[0:1, 5, 32:33], ones[0:E, 0:1], cnt[:, 4:5], start=False, stop=True,
                                  skip_group_check=True).then_inc(nex_sum, 1)
                    if j == 15:
                        pe.wait_ge(mex_ready, 1)
                        pe.matmul(ps[0:1, 5, 64:64 + MAX_EXTRA], const[0:E, C_PART:C_PART + 1], mex[:, 0, :],
                                  start=False, stop=True, skip_group_check=True)
                        pe.matmul(ps[0:1, 5, 96:96 + MAX_EXTRA], const[0:E, C_PART + 1:C_PART + 2], mex[:, 0, :],
                                  start=False, stop=False, skip_group_check=True)
                        pe.matmul(ps[0:1, 5, 96:96 + MAX_EXTRA], ones[0:E, 0:1], mex[:, 1, :], start=False, stop=True,
                                  skip_group_check=True).then_inc(mex_sum, 1)
                    pe.wait_ge(slot_ready, j + 1)
                    pe.wait_ge(slot_row_ready, j + 1)
                    pe.matmul(ps[:, 3, 0:2 * P], slot_row[:, j % 2, :], slot_col[:, j % 2].rearrange("p a n -> p (a n)"),
                              start=(j == 0), stop=(j == 15)).then_inc(slot_used, 1)

        gathered = sem("gathered")
        hs_turned = sem("hs_turned")
        hsT_hi_ready = sem("hsT_hi_ready")
        hsT_lo_ready = sem("hsT_lo_ready")
        sel1_ready = sem("sel1_ready")
        sel2_ready = sem("sel2_ready")
        tok_ready = sem("tok_ready")
        row_ready = sem("row_ready")
        wcol_ready = sem("wcol_ready")
        w1_started = sem("w1_started")
        w2_started = sem("w2_started")
        glu_ready = sem("glu_ready")
        sig_ready = sem("sig_ready")
        hid_read = sem("hid_read")
        gs_ready = sem("gs_ready")
        act_ready = sem("act_ready")
        a_turned = sem("a_turned")
        aT_hi_ready = sem("aT_hi_ready")
        aT_lo_ready = sem("aT_lo_ready")
        y_ready = sem("y_ready")
        scattered = sem("scattered")
        row_last = sem("row_last")
        y_last = sem("y_last")

        def w1_end(b):
            return 8 if known(b) and b == 0 else 12 * b + 4

        def w2_end(b, last=False):
            return 12 * b + (12 if last else 20)

        OUTB, LASTB, TPB = slice(4, 6), slice(0, 2), slice(6, 8)

        def blocks(eng):
            return E + eng.value_load(bt[0:1, 2 * MAX_BLOCKS:2 * MAX_BLOCKS + 1], min_val=0, max_val=MAX_EXTRA - 1)

        def expert_of(eng, i):
            if known(i) and i < E:
                return i
            return eng.value_load(bt[0:1, bass.ds(i, 1)], min_val=0, max_val=E - 1)

        def column_of(eng, i):
            return eng.value_load(bt[0:1, bass.ds(i + MAX_BLOCKS, 1)], min_val=0, max_val=P - 1)

        h_in_in = sem("h_in_in")

        with nc.Block() as block:
            @block.sync
            def _(sp):
                n = blocks(sp)
                sp.wait_ge(gathered, 16)
                expert_load(sp, 1, -1, 1, "w1", 3)
                for j in (6, 7):
                    expert_load(sp, 1, -4 + j, 1, "w1", j)
                with sp.Fori(2, n) as i:
                    e2 = expert_of(sp, i - 2)
                    for j in range(4):
                        expert_load(sp, i, -8 + j, e2, "w2", j)
                    e1 = expert_of(sp, i)
                    for j in range(8):
                        expert_load(sp, i, -4 + j, e1, "w1", j)
                e2 = expert_of(sp, n - 2)
                for j in range(4):
                    expert_load(sp, n, -8 + j, e2, "w2", j)
                e2 = expert_of(sp, n - 1)
                for j in range(4):
                    expert_load(sp, n, -4 + j, e2, "w2", j)
                lo_wait(sp, n, -10)
                sp.dma_start(h_in[:], h2_d.rearrange("(t p) n -> p t n", p=P)).then_inc(h_in_in, 16)
                sp.dma_start(wfin[:], norm_final_w.rearrange("(a n) -> a n", a=1).to_broadcast([P, D])).then_inc(h_in_in, 16)

            @block.gpsimd
            def _(pool):
                n = blocks(pool)

                def split_lo(i, off):
                    pool.wait_ge(x_hi_done, 12 * i + off + 1)
                    pool.tensor_tensor(w_lo[:, off % SPLITS, :], raw[:, off % RAWS, :],
                                       w_hi[:, off % SPLITS, :].bitcast(F32), ALU.subtract).then_inc(x_lo_3, 1)

                def take_waits():
                    pool.tensor_tensor(spare[:], ones[:, 0:1], ones[:, 0:1], ALU.add)

                def pick(b):
                    col = column_of(pool, b)
                    if not known(b) or b >= 1:
                        pool.wait_ge(gathered, 16 * b)
                    pool.tensor_copy(cur_tok[:], tabI[:, 0, bass.ds(col, 1)]).then_inc(tok_ready, 1)

                def await_pick(b):
                    pool.wait_ge(tok_ready, b + 1)
                    if not known(b) or b >= 1:
                        pool.wait_ge(hs_turned, b)

                def gather():
                    pool.indirect_dma_start(out=hs[:], out_offset=None, in_=u2_d,
                                            in_offset=bass.IndirectOffsetOnAxis(ap=cur_tok[:], axis=0),
                                            bounds_check=TOKENS - 1, oob_is_err=False).then_inc(gathered, 16)

                def select(sel, b, ready, started):
                    e = expert_of(pool, b)
                    if not known(b) or b >= 1:
                        pool.wait_ge(started, b)
                    pool.tensor_copy(sel[:], const[:, bass.ds(e + C_EYE2, 1)].to_broadcast([P, P])).then_inc(ready, 1)

                def weigh(b):
                    col = column_of(pool, b)
                    if not known(b) or b >= 1:
                        pool.wait_ge(scattered, 16 * b)
                        pool.wait_ge(y_ready, b)
                    pool.tensor_copy(cur_w[:], tabW[:, bass.ds(col, 1)]).then_inc(wcol_ready, 1)
                    pool.tensor_copy(cur_row[:], tabI[:, 1, bass.ds(col, 1)]).then_inc(row_ready, 1)

                def await_y(b):
                    pool.wait_ge(row_ready, b + 1)
                    pool.wait_ge(y_ready, b + 1)

                def scatter(rows_, places):
                    pool.indirect_dma_start(out=y_d, out_offset=bass.IndirectOffsetOnAxis(ap=places[:], axis=0),
                                            in_=rows_[:], in_offset=None, bounds_check=TOKENS * TOP - 1,
                                            oob_is_err=False).then_inc(scattered, 16)

                pick(0)
                await_pick(0)
                gather()
                select(sel1, 0, sel1_ready, w1_started)
                pick(1)
                await_pick(1)
                gather()
                select(sel1, 1, sel1_ready, w1_started)
                split_lo(0, 7)
                split_lo(1, -1)
                pick(2)
                await_pick(2)
                gather()
                split_lo(1, 3)
                with pool.Fori(2, n) as i:
                    select(sel2, i - 2, sel2_ready, w2_started)
                    pick(i + 1)
                    await_pick(i + 1)
                    take_waits()
                    gather()
                    split_lo(i, -5)
                    select(sel1, i, sel1_ready, w1_started)
                    split_lo(i, -1)
                    weigh(i - 2)
                    await_y(i - 2)
                    take_waits()
                    scatter(y_out, cur_row)
                    split_lo(i, 3)
                select(sel2, n - 2, sel2_ready, w2_started)
                split_lo(n, -5)
                select(sel2, n - 1, sel2_ready, w2_started)
                weigh(n - 2)
                await_y(n - 2)
                take_waits()
                scatter(y_out, cur_row)
                col = column_of(pool, n - 1)
                pool.wait_ge(hs_turned, n + 1)
                pool.tensor_copy(last_w[:], tabW[:, bass.ds(col, 1)]).then_inc(wcol_ready, 1)
                pool.tensor_copy(cur_tok[:], tabI[:, 1, bass.ds(col, 1)]).then_inc(row_last, 1)
                pool.wait_ge(row_last, 1)
                pool.wait_ge(y_last, 1)
                scatter(hs, cur_tok)
                pool.wait_ge(scattered, 16 * n)

            @block.scalar
            def _(act):
                n = blocks(act)

                def split_hi(i, off):
                    act.wait_ge(raw_in[off % RAWS], 16 * (i + off // RAWS + 1))
                    if not known(i) or 12 * i + off >= SPLITS:
                        act.wait_ge(x_used, 12 * i + off - SPLITS + 1)
                    act.activation(w_hi[:, off % SPLITS, :], raw[:, off % RAWS, :], ACT.Copy).then_inc(x_hi_done, 1)

                def rows_hi(b):
                    act.wait_ge(hs_turned, b + 1)
                    if not known(b) or b >= 1:
                        act.wait_ge(x_used, w1_end(b - 1))
                    act.activation(hsT_hi[:].rearrange("p k t -> p (k t)"), ps[:, TPB, :].rearrange("p b n -> p (b n)"),
                                   ACT.Copy).then_inc(hsT_hi_ready, 1)

                def sigmoid(b):
                    act.wait_ge(glu_ready, b + 1)
                    if not known(b) or b >= 1:
                        act.wait_ge(act_ready, b)
                    act.activation(sig[:], glu[:], ACT.Sigmoid, scale=ALPHA).then_inc(sig_ready, 1)

                def act_hi(b):
                    act.wait_ge(a_turned, b + 1)
                    if not known(b) or b >= 1:
                        act.wait_ge(x_used, w2_end(b - 1))
                    act.activation(aT_hi[:].rearrange("p k t -> p (k t)"), ps[:, TPB, :].rearrange("p b n -> p (b n)"),
                                   ACT.Copy).then_inc(aT_hi_ready, 1)

                def weigh_out(b):
                    act.wait_ge(x_used, w2_end(b))
                    act.wait_ge(wcol_ready, b + 1)
                    if not known(b) or b >= 1:
                        act.wait_ge(scattered, 16 * b)
                    act.activation(y_out[:], ps[:, OUTB, :].rearrange("p b n -> p (b n)"), ACT.Copy,
                                   scale=cur_w[:]).then_inc(y_ready, 1)

                def weigh_out_last():
                    act.wait_ge(x_used, w2_end(n - 1, last=True))
                    act.wait_ge(wcol_ready, n)
                    act.activation(hs[:], ps[:, LASTB, :].rearrange("p b n -> p (b n)"), ACT.Copy,
                                   scale=last_w[:]).then_inc(y_last, 1)

                rows_hi(0)
                for j in range(4, 8):
                    split_hi(0, j)
                for j in range(4):
                    split_hi(1, -4 + j)
                rows_hi(1)
                sigmoid(0)
                for j in range(4, 8):
                    split_hi(1, -4 + j)
                act_hi(0)
                with act.Fori(2, n) as i:
                    for j in range(4):
                        split_hi(i, -8 + j)
                    sigmoid(i - 1)
                    rows_hi(i)
                    for j in range(4):
                        split_hi(i, -4 + j)
                    weigh_out(i - 2)
                    for j in range(4, 8):
                        split_hi(i, -4 + j)
                    act_hi(i - 1)
                for j in range(4):
                    split_hi(n, -8 + j)
                sigmoid(n - 1)
                for j in range(3):
                    split_hi(n, -4 + j)
                act_hi(n - 1)
                split_hi(n, -1)
                weigh_out(n - 2)
                weigh_out_last()

            @block.vector
            def _(dve):
                n = blocks(dve)

                def split_lo(i, off, every=False):
                    if off % SPLITS == 3 and not every:
                        return
                    dve.wait_ge(x_hi_done, 12 * i + off + 1)
                    dve.tensor_tensor(w_lo[:, off % SPLITS, :], raw[:, off % RAWS, :],
                                      w_hi[:, off % SPLITS, :].bitcast(F32),
                                      ALU.subtract).then_inc(x_lo_3 if off % SPLITS == 3 else x_lo_012, 1)

                def rows_lo(b):
                    dve.wait_ge(hsT_hi_ready, b + 1)
                    dve.tensor_tensor(hsT_lo[:].rearrange("p k t -> p (k t)"),
                                      ps[:, TPB, :].rearrange("p b n -> p (b n)"),
                                      hsT_hi[:].rearrange("p k t -> p (k t)").bitcast(F32),
                                      ALU.subtract).then_inc(hsT_lo_ready, 1)

                def clamp(b):
                    dve.wait_ge(x_used, w1_end(b))
                    if not known(b) or b >= 1:
                        dve.wait_ge(gs_ready, b)
                    dve.tensor_scalar(glu[:], ps[:, 0:2, :].rearrange("p b n -> p (b n)"), LIMIT, None,
                                      ALU.min).then_inc(glu_ready, 1)
                    if not known(b) or b >= 1:
                        dve.wait_ge(a_turned, b)
                    dve.tensor_scalar(lin[:], ps[:, 2:4, :].rearrange("p b n -> p (b n)"), LIMIT, -LIMIT, ALU.min,
                                      ALU.max).then_inc(hid_read, 1)

                def swish(b):
                    dve.wait_ge(sig_ready, b + 1)
                    dve.tensor_tensor(sig[:], sig[:], glu[:], ALU.mult).then_inc(gs_ready, 1)
                    dve.wait_ge(gs_ready, b + 1)
                    dve.wait_ge(hid_read, b + 1)
                    dve.scalar_tensor_tensor(lin[:], lin[:], 1.0, sig[:], ALU.add, ALU.mult).then_inc(act_ready, 1)

                def act_lo(b):
                    dve.wait_ge(aT_hi_ready, b + 1)
                    dve.tensor_tensor(aT_lo[:].rearrange("p k t -> p (k t)"),
                                      ps[:, TPB, :].rearrange("p b n -> p (b n)"),
                                      aT_hi[:].rearrange("p k t -> p (k t)").bitcast(F32),
                                      ALU.subtract).then_inc(aT_lo_ready, 1)

                split_lo(0, 2)
                split_lo(0, 3, every=True)
                rows_lo(0)
                for j in range(4, 8):
                    split_lo(0, j)
                for j in range(4):
                    split_lo(1, -4 + j)
                clamp(0)
                rows_lo(1)
                swish(0)
                for j in range(4, 8):
                    split_lo(1, -4 + j)
                act_lo(0)
                with dve.Fori(2, n) as i:
                    for j in range(4):
                        split_lo(i, -8 + j)
                    clamp(i - 1)
                    rows_lo(i)
                    split_lo(i, -4)
                    swish(i - 1)
                    for j in range(1, 8):
                        split_lo(i, -4 + j)
                    act_lo(i - 1)
                for j in range(4):
                    split_lo(n, -8 + j)
                clamp(n - 1)
                swish(n - 1)
                for j in range(3):
                    split_lo(n, -4 + j)
                act_lo(n - 1)
                split_lo(n, -1, every=True)

            @block.tensor
            def _(pe):
                n = blocks(pe)

                def turn_rows(b):
                    pe.wait_ge(gathered, 16 * (b + 1))
                    if not known(b):
                        pe.wait_ge(aT_lo_ready, b - 1)
                    elif b >= 2:
                        pe.wait_ge(aT_lo_ready, b - 1)
                    elif b == 1:
                        pe.wait_ge(hsT_lo_ready, 1)
                    for k in range(KD):
                        mm = pe.transpose(ps[:, 6 + k // 4, (k % 4) * P:(k % 4 + 1) * P], hs[:, k * P:(k + 1) * P], ident)
                    mm.then_inc(hs_turned, 1)

                def turn_act(b):
                    pe.wait_ge(act_ready, b + 1)
                    pe.wait_ge(hsT_lo_ready, b + 2)
                    for k in range(KD):
                        mm = pe.transpose(ps[:, 6 + k // 4, (k % 4) * P:(k % 4 + 1) * P], lin[:, k * P:(k + 1) * P], ident)
                    mm.then_inc(a_turned, 1)

                def turn_last(pe, n):
                    pe.wait_ge(act_ready, n)
                    for k in range(KD):
                        mm = pe.transpose(ps[:, 6 + k // 4, (k % 4) * P:(k % 4 + 1) * P], lin[:, k * P:(k + 1) * P], ident)
                    mm.then_inc(a_turned, 1)

                def w1_bias(b):
                    pe.wait_ge(sel1_ready, b + 1)
                    if not known(b) or b >= 1:
                        pe.wait_ge(hid_read, b)
                        pe.wait_ge(glu_ready, b)
                    for q in range(4):
                        mm = pe.matmul(ps[:, q, :], sel1[:], bias1[:, q * 512:(q + 1) * 512], start=True, stop=False)
                    mm.then_inc(w1_started, 1)
                    pe.wait_ge(hsT_lo_ready, b + 1)

                def w1_chunk(b, i, off, j):
                    lo_wait(pe, i, off)
                    s = off % SPLITS
                    for q in range(4):
                        mh, ml = (w[:, s, q * 512:(q + 1) * 512] for w in (w_hi, w_lo))
                        pe.matmul(ps[:, q, :], hsT_hi[:, j, :], mh, start=False, stop=False)
                        pe.matmul(ps[:, q, :], hsT_hi[:, j, :], ml, start=False, stop=False)
                        mm = pe.matmul(ps[:, q, :], hsT_lo[:, j, :], mh, start=False, stop=(j == 7))
                    mm.then_inc(x_used, 1)

                def w2_block(b, i, off, last=False):
                    pe.wait_ge(sel2_ready, b + 1)
                    bank = (LASTB if last else OUTB).start
                    if last:
                        pe.wait_ge(glu_ready, b + 1)
                        pe.wait_ge(hid_read, b + 1)
                    elif not known(b) or b >= 1:
                        pe.wait_ge(y_ready, b)
                    for q in range(2):
                        mm = pe.matmul(ps[:, bank + q, :], sel2[:], bias2[:, q * 512:(q + 1) * 512], start=True, stop=False)
                    mm.then_inc(w2_started, 1)
                    pe.wait_ge(aT_lo_ready, b + 1)
                    for j in range(4):
                        lo_wait(pe, i, off + j)
                        s = (off + j) % SPLITS
                        for kk in range(2):
                            k = 2 * j + kk
                            for q in range(2):
                                at_ = kk * D + q * 512
                                mh, ml = (w[:, s, at_:at_ + 512] for w in (w_hi, w_lo))
                                dst = ps[:, bank + q, :]
                                pe.matmul(dst, aT_hi[:, k, :], mh, start=False, stop=False)
                                pe.matmul(dst, aT_hi[:, k, :], ml, start=False, stop=False)
                                mm = pe.matmul(dst, aT_lo[:, k, :], mh, start=False, stop=(k == KD - 1))
                        mm.then_inc(x_used, 1)

                turn_rows(0)
                w1_bias(0)
                for j in range(8):
                    w1_chunk(0, 0, j, j)
                turn_rows(1)
                w1_bias(1)
                for j in range(4):
                    w1_chunk(1, 1, -4 + j, j)
                turn_act(0)
                for j in range(4, 8):
                    w1_chunk(1, 1, -4 + j, j)
                turn_rows(2)
                with pe.Fori(2, n) as i:
                    w2_block(i - 2, i, -8)
                    w1_bias(i)
                    for j in range(4):
                        w1_chunk(i, i, -4 + j, j)
                    turn_act(i - 1)
                    for j in range(4, 8):
                        w1_chunk(i, i, -4 + j, j)
                    turn_rows(i + 1)
                w2_block(n - 2, n, -8)
                turn_last(pe, n)
                w2_block(n - 1, n, -4, last=True)

        y_in_in = x_inn
        y23_ready = sem("y23_ready")
        hsum_ready = sem("hsum_ready")
        fsq_ready = sem("fsq_ready")
        frms_ready = sem("frms_ready")
        out_ready = sem("out_ready")
        out_stored = sem("out_stored")

        with nc.Block() as block:
            @block.sync
            def _(sp):
                yv = y_d.rearrange("(t k) n -> t k n", k=TOP)
                for t in range(TT):
                    sp.dma_start(y_in[:, t], yv[t * P:(t + 1) * P]).then_inc(y_in_in[t], 16)
                for t in range(TT):
                    sp.wait_ge(out_ready, t + 1)
                    sp.dma_start(out2[t * P:(t + 1) * P, :], h_out[:, t, :]).then_inc(out_stored, 16)
                sp.wait_ge(out_stored, 16 * TT)
                sp.wait_ge(h_in_in, 32)

            @block.gpsimd
            def _(pool):
                for t in range(TT):
                    pool.wait_ge(y_in_in[t], 32)
                    if t >= 2:
                        pool.wait_ge(hsum_ready, t - 1)
                    pool.tensor_tensor(y_23[:, t % 2, :], y_in[:, t, 2, :], y_in[:, t, 3, :],
                                       ALU.add).then_inc(y23_ready, 1)

            @block.scalar
            def _(act):
                for t in range(TT):
                    act.wait_ge(hsum_ready, t + 1)
                    if t >= 1:
                        act.wait_ge(fsq_ready, t)
                    act.activation(sq[:], h_out[:, t, :], ACT.Square, scale=D ** -0.5,
                                   accum_out=ms[:, t:t + 1]).then_inc(fsq_ready, 1)
                    act.wait_ge(fsq_ready, t + 1)
                    act.activation(rstd[:, t:t + 1], ms[:, t:t + 1], ACT.Sqrt, bias=eps).then_inc(frms_ready, 1)

            @block.vector
            def _(dve):
                chain = Chain(dve, dve_step, order)
                dve.wait_ge(h_in_in, 32)
                for t in range(TT + 1):
                    if t < TT:
                        s = t % 2
                        dve.wait_ge(y_in_in[t], 32)
                        chain(dve.tensor_tensor(y_01[:, s, :], y_in[:, t, 0, :], y_in[:, t, 1, :], ALU.add))
                        dve.wait_ge(y23_ready, t + 1)
                        chain(dve.tensor_tensor(y_01[:, s, :], y_01[:, s, :], y_23[:, s, :], ALU.add))
                        chain(dve.tensor_tensor(y_01[:, s, :], y_01[:, s, :], gate_f[:], ALU.mult))
                        dve.tensor_tensor(h_out[:, t, :], y_01[:, s, :], h_in[:, t, :], ALU.add).then_inc(hsum_ready, 1)
                    if t >= 1:
                        b = t - 1
                        dve.wait_ge(frms_ready, b + 1)
                        chain(dve.reciprocal(rstd[:, b:b + 1], rstd[:, b:b + 1]))
                        dve.scalar_tensor_tensor(h_out[:, b, :], h_out[:, b, :], rstd[:, b:b + 1], wfin[:], ALU.mult,
                                                 ALU.mult).then_inc(out_ready, 1)


_INS = ["x", "c", "w_ada", "b_ada", "norm_mix_w", "w_in", "hgrn_lower_bounds", "hgrn_norm_w", "conv_w", "w_hgrn_out",
        "w_conv_out", "w_mix_out", "norm_ffn_w", "w_router", "b_router", "w1", "b1", "w2", "b2", "norm_final_w"]


def kernel(**inputs):
    import concourse.bacc as _bacc
    from concourse.bass_utils import run_bass_kernel_spmd as _run

    nc = _bacc.Bacc("TRN2", target_bir_lowering=False, num_devices=1, dynamic_dma_scratch_size=4096)
    arrays = {"shape_constants": shape_constants(), "level_masks": level_masks()}
    for name in _INS:
        arrays[f"in_{name}"] = np.ascontiguousarray(inputs[name])
    args = [nc.dram_tensor(n, a.shape, mybir.dt.from_np(a.dtype), kind="ExternalInput").ap() for n, a in arrays.items()]
    out = nc.dram_tensor("layer_out", (1, TOKENS, D), F32, kind="ExternalOutput").ap()
    layer_kernel(nc, *args, out)
    r = _run(nc, [arrays], core_ids=[0])
    return r.results[0]["layer_out"]
```
